# Optimizing a Trainium2 kernel written in Bass

```python
import jax, jax.numpy as jnp
from jax import lax
import numpy as np

D_MODEL = 2048
BATCH = 1
SEQ = 256
DEPTH = 2

N_MIXERS = 2
N_POOL_LAYERS = (DEPTH + 1) // 2
N_ATTN_LAYERS = DEPTH // 2
EPS = 1e-6

POOL_WINDOWS = (2, 4, 8, 16)
N_POOL_GROUPS = 4
POOL_GROUP_DIM = D_MODEL // N_POOL_GROUPS
POOL_IN = 2 * D_MODEL

N_HEADS = 16
HEAD_DIM = D_MODEL // N_HEADS
ATTN_WIDTH = N_HEADS * HEAD_DIM
ROT_DIM = HEAD_DIM // 4
IDX_HEADS = 16
IDX_DIM = 64
IDX_ROT = IDX_DIM // 4
ROPE_THETA = 500000.0
TOP_K_MAX = 256
Q_BLOCK = 128
ATTN_SPLITS = (ATTN_WIDTH, 2 * ATTN_WIDTH, 3 * ATTN_WIDTH, 4 * ATTN_WIDTH,
               4 * ATTN_WIDTH + IDX_HEADS * IDX_DIM,
               4 * ATTN_WIDTH + IDX_HEADS * IDX_DIM + IDX_DIM)
ATTN_IN = 4 * ATTN_WIDTH + IDX_HEADS * IDX_DIM + IDX_DIM + IDX_HEADS


def rms_norm(x, g):
    xf = x.astype(jnp.float32)
    y = xf * lax.rsqrt(jnp.mean(xf * xf, axis=-1, keepdims=True) + EPS)
    return (y * g.astype(jnp.float32)).astype(x.dtype)

def rope_partial(x, positions, rot_dim):
    half = rot_dim // 2
    inv_freq = ROPE_THETA ** (-jnp.arange(half, dtype=jnp.float32) * 2.0 / rot_dim)
    ang = positions.astype(jnp.float32)[..., None] * inv_freq
    cos = jnp.cos(ang)[:, :, None, :]
    sin = jnp.sin(ang)[:, :, None, :]
    xf = x.astype(jnp.float32)
    x1, x2, rest = xf[..., :half], xf[..., half:rot_dim], xf[..., rot_dim:]
    out = jnp.concatenate([x1 * cos - x2 * sin, x2 * cos + x1 * sin, rest], axis=-1)
    return out.astype(x.dtype)

def pool_branch(h, w_in, w_grp, layer_scale, w_out):
    B, L, D = h.shape
    v, gate = jnp.split(h @ w_in, 2, axis=-1)
    vf = v.astype(jnp.float32)
    cs = jnp.concatenate([jnp.zeros((B, 1, D), jnp.float32),
                          jnp.cumsum(vf, axis=1)], axis=1)
    t = jnp.arange(L, dtype=jnp.int32)
    outs = []
    for gi, w in enumerate(POOL_WINDOWS):
        sl = slice(gi * POOL_GROUP_DIM, (gi + 1) * POOL_GROUP_DIM)
        lo = jnp.maximum(t + 1 - w, 0)
        window_sum = cs[:, t + 1, sl] - cs[:, lo, sl]
        count = jnp.minimum(t + 1, w).astype(jnp.float32)[None, :, None]
        pooled = (window_sum / count - vf[:, :, sl]).astype(h.dtype)
        outs.append(jnp.einsum('bsc,cd->bsd', pooled, w_grp[gi]))
    mixed = jnp.concatenate(outs, axis=-1) * layer_scale
    return (mixed * jax.nn.silu(gate)) @ w_out

def dsa_branch(h, positions, w_in, w_out):
    B, L, _ = h.shape
    proj = h @ w_in
    q, k, v, gate, qi, ki, wi = jnp.split(proj, ATTN_SPLITS, axis=-1)
    q = rope_partial(q.reshape(B, L, N_HEADS, HEAD_DIM), positions, ROT_DIM)
    k = rope_partial(k.reshape(B, L, N_HEADS, HEAD_DIM), positions, ROT_DIM)
    v = v.reshape(B, L, N_HEADS, HEAD_DIM)
    qi = rope_partial(qi.reshape(B, L, IDX_HEADS, IDX_DIM), positions, IDX_ROT)
    ki = rope_partial(ki.reshape(B, L, 1, IDX_DIM), positions, IDX_ROT)[:, :, 0]
    ki_f = ki.astype(jnp.float32)
    top_k = min(TOP_K_MAX, L // 4)
    nb = L // Q_BLOCK
    key_idx = jnp.arange(L, dtype=jnp.int32)
    idx_scale = (IDX_HEADS ** -0.5) * (IDX_DIM ** -0.5)
    attn_scale = HEAD_DIM ** -0.5

    def to_blocks(a):
        return jnp.moveaxis(a.reshape(B, nb, Q_BLOCK, *a.shape[2:]), 1, 0)

    def block_fn(args):
        qb, qib, wb, tb = args
        s = jnp.einsum('bqhd,bsd->bqhs', qib.astype(jnp.float32), ki_f)
        score = jnp.einsum('bqhs,bqh->bqs', jax.nn.relu(s),
                           wb.astype(jnp.float32)) * idx_scale
        admissible = key_idx[None, None, :] <= tb[None, :, None]
        score = jnp.where(admissible, score, -jnp.inf)
        _, sel = lax.top_k(score, top_k)
        valid = sel <= tb[None, :, None]
        k_sel = jax.vmap(lambda kk, ii: kk[ii])(k, sel)
        v_sel = jax.vmap(lambda vv, ii: vv[ii])(v, sel)
        logits = jnp.einsum('bqhd,bqkhd->bhqk', qb, k_sel).astype(jnp.float32) * attn_scale
        logits = jnp.where(valid[:, None], logits, -jnp.inf)
        p = jax.nn.softmax(logits, axis=-1).astype(v.dtype)
        return jnp.einsum('bhqk,bqkhd->bqhd', p, v_sel)

    t_blocks = key_idx.reshape(nb, Q_BLOCK)
    outs = lax.map(block_fn, (to_blocks(q), to_blocks(qi), to_blocks(wi), t_blocks))
    o = jnp.moveaxis(outs, 0, 1).reshape(B, L, ATTN_WIDTH)
    return (o * jax.nn.silu(gate)) @ w_out

def first_inputs(seed: int = 0) -> dict:
    key = jax.random.key(seed)
    ks = jax.random.split(key, 13)
    D = D_MODEL
    x = jax.random.normal(ks[0], (BATCH, SEQ, D), jnp.float32)
    c = jax.random.normal(ks[1], (BATCH, D), jnp.float32)
    positions = jnp.broadcast_to(jnp.arange(SEQ, dtype=jnp.int32)[None, :], (BATCH, SEQ))
    norm_g = 1.0 + 0.02 * jax.random.normal(ks[2], (DEPTH, D), jnp.float32)
    mod_w = 0.5 * D ** -0.5 * jax.random.normal(ks[3], (DEPTH, D, 3 * D), jnp.float32)
    mod_b = 0.02 * jax.random.normal(ks[4], (DEPTH, 3 * D), jnp.float32)
    pool_w_in = D ** -0.5 * jax.random.normal(ks[5], (N_POOL_LAYERS, D, POOL_IN), jnp.float32)
    pool_w_grp = POOL_GROUP_DIM ** -0.5 * jax.random.normal(
        ks[6], (N_POOL_LAYERS, N_POOL_GROUPS, POOL_GROUP_DIM, POOL_GROUP_DIM), jnp.float32)
    pool_scale = 1.0 + 0.1 * jax.random.normal(ks[7], (N_POOL_LAYERS, D), jnp.float32)
    pool_w_out = D ** -0.5 * jax.random.normal(ks[8], (N_POOL_LAYERS, D, D), jnp.float32)
    attn_w_in = D ** -0.5 * jax.random.normal(ks[9], (N_ATTN_LAYERS, D, ATTN_IN), jnp.float32)
    attn_w_out = ATTN_WIDTH ** -0.5 * jax.random.normal(
        ks[10], (N_ATTN_LAYERS, ATTN_WIDTH, D), jnp.float32)
    final_g = 1.0 + 0.02 * jax.random.normal(ks[11], (D,), jnp.float32)
    return {"x": x, "c": c, "positions": positions, "norm_g": norm_g,
            "mod_w": mod_w, "mod_b": mod_b, "pool_w_in": pool_w_in,
            "pool_w_grp": pool_w_grp, "pool_scale": pool_scale,
            "pool_w_out": pool_w_out, "attn_w_in": attn_w_in,
            "attn_w_out": attn_w_out, "final_g": final_g}

def first_block(x, c, positions, norm_g, mod_w, mod_b, pool_w_in, pool_w_grp,
              pool_scale, pool_w_out, attn_w_in, attn_w_out, final_g):
    cond = jax.nn.silu(c)
    for i in range(DEPTH):
        mod = cond @ mod_w[i] + mod_b[i]
        shift, scale, gate = jnp.split(mod, 3, axis=-1)
        h = rms_norm(x, norm_g[i]) * (1.0 + scale[:, None, :]) + shift[:, None, :]
        j = i // N_MIXERS
        if i % N_MIXERS == 0:
            out = pool_branch(h, pool_w_in[j], pool_w_grp[j], pool_scale[j], pool_w_out[j])
        else:
            out = dsa_branch(h, positions, attn_w_in[j], attn_w_out[j])
        x = x + gate[:, None, :] * out
    return rms_norm(x, final_g)


DEPTH_2 = 1

PLE_DIM = 256
CHUNK = 128
SGU_GROUPS = 8
SGU_GROUP_DIM = 128
SGU_WIDTH = SGU_GROUPS * SGU_GROUP_DIM
SB_HEADS = 8
SB_HEAD_DIM = 128
SB_WIDTH = SB_HEADS * SB_HEAD_DIM
FFN_HIDDEN = ((8 * D_MODEL + 3 * 256 - 1) // (3 * 256)) * 256
IN_COLS = 2 * SGU_WIDTH + 3 * SB_WIDTH + 2 * D_MODEL


def rmsnorm(x, g):
    xf = x.astype(jnp.float32)
    y = xf * lax.rsqrt(jnp.mean(xf * xf, axis=-1, keepdims=True) + EPS)
    return (y * g.astype(jnp.float32)).astype(x.dtype)

def chunked_spatial_gating(u, v, w_s, b_s):
    B, S, G, C = v.shape
    tri = jnp.tril(jnp.ones((CHUNK, CHUNK), dtype=w_s.dtype))
    ws = w_s * tri[None]
    vc = v.reshape(B, S // CHUNK, CHUNK, G, C)
    mixed = jnp.einsum('gts,bnsgc->bntgc', ws, vc)
    mixed = mixed + jnp.transpose(b_s)[None, None, :, :, None]
    return u * mixed.reshape(B, S, G, C)

def stick_breaking_attention(q, k, v):
    B, S, H, Dh = q.shape
    nb = S // Q_BLOCK
    scale = Dh ** -0.5
    qf = jnp.transpose(q, (0, 2, 1, 3))
    kf = jnp.transpose(k, (0, 2, 1, 3))
    vf = jnp.transpose(v, (0, 2, 1, 3))
    key_pos = jnp.arange(S, dtype=jnp.int32)

    def one_block(blk):
        start = blk * Q_BLOCK
        qi = lax.dynamic_slice_in_dim(qf, start, Q_BLOCK, axis=2)
        z = jnp.einsum('bhqd,bhkd->bhqk', qi, kf).astype(jnp.float32) * scale
        q_pos = start + jnp.arange(Q_BLOCK, dtype=jnp.int32)
        strict = key_pos[None, :] < q_pos[:, None]
        log_beta = jax.nn.log_sigmoid(z)
        log_1m = jnp.where(strict, jax.nn.log_sigmoid(-z), jnp.zeros_like(z))
        tail = lax.cumsum(log_1m, axis=3, reverse=True) - log_1m
        w = jnp.where(strict, jnp.exp(log_beta + tail), jnp.zeros_like(z))
        return jnp.einsum('bhqk,bhkd->bhqd', w.astype(vf.dtype), vf)

    out = lax.map(one_block, jnp.arange(nb, dtype=jnp.int32))
    out = jnp.transpose(out, (1, 0, 3, 2, 4))
    return out.reshape(B, S, H, Dh)

def second_inputs(seed: int = 0) -> dict:
    key = jax.random.key(seed)
    ks = jax.random.split(key, 20)
    f = jnp.float32

    def nrm(k, shape, fan_in):
        return jax.random.normal(k, shape, f) * (fan_in ** -0.5)

    def gain(k, shape):
        return 1.0 + 0.05 * jax.random.normal(k, shape, f)

    return {
        "x": jax.random.normal(ks[0], (BATCH, SEQ, D_MODEL), f),
        "p": jax.random.normal(ks[1], (DEPTH_2, BATCH, SEQ, PLE_DIM), f),
        "attn_norm_g": gain(ks[2], (DEPTH_2, D_MODEL)),
        "w_in": nrm(ks[3], (DEPTH_2, D_MODEL, IN_COLS), D_MODEL),
        "sgu_norm_g": gain(ks[4], (DEPTH_2, SGU_GROUPS, SGU_GROUP_DIM)),
        "w_s": nrm(ks[5], (DEPTH_2, SGU_GROUPS, CHUNK, CHUNK), CHUNK),
        "b_s": 1.0 + 0.1 * jax.random.normal(ks[6], (DEPTH_2, SGU_GROUPS, CHUNK), f),
        "q_norm_g": gain(ks[7], (DEPTH_2, SB_HEAD_DIM)),
        "k_norm_g": gain(ks[8], (DEPTH_2, SB_HEAD_DIM)),
        "w_up_a": nrm(ks[9], (DEPTH_2, SGU_WIDTH, D_MODEL), SGU_WIDTH),
        "w_up_b": nrm(ks[10], (DEPTH_2, SB_WIDTH, D_MODEL), SB_WIDTH),
        "w_o": nrm(ks[11], (DEPTH_2, D_MODEL, D_MODEL), D_MODEL),
        "ffn_norm_g": gain(ks[12], (DEPTH_2, D_MODEL)),
        "w_ffn_in": nrm(ks[13], (DEPTH_2, D_MODEL, 2 * FFN_HIDDEN), D_MODEL),
        "w_ffn_out": nrm(ks[14], (DEPTH_2, FFN_HIDDEN, D_MODEL), FFN_HIDDEN),
        "ple_norm_g": gain(ks[15], (DEPTH_2, D_MODEL)),
        "w_ple_gate": nrm(ks[16], (DEPTH_2, D_MODEL, D_MODEL), D_MODEL),
        "w_ple": nrm(ks[17], (DEPTH_2, PLE_DIM, D_MODEL), PLE_DIM),
    }

def second_block(x, p, attn_norm_g, w_in, sgu_norm_g, w_s, b_s, q_norm_g, k_norm_g,
              w_up_a, w_up_b, w_o, ffn_norm_g, w_ffn_in, w_ffn_out,
              ple_norm_g, w_ple_gate, w_ple):
    B, S, D = x.shape
    c0 = SGU_WIDTH
    c1 = c0 + SGU_WIDTH
    c2 = c1 + SB_WIDTH
    c3 = c2 + SB_WIDTH
    c4 = c3 + SB_WIDTH
    c5 = c4 + D_MODEL
    for i in range(DEPTH_2):
        h = rmsnorm(x, attn_norm_g[i])
        proj = h @ w_in[i]
        u = proj[..., :c0]
        v_sgu = proj[..., c0:c1]
        q = proj[..., c1:c2]
        k = proj[..., c2:c3]
        v_att = proj[..., c3:c4]
        g_a = proj[..., c4:c5]
        g_b = proj[..., c5:]

        u = jax.nn.gelu(u).reshape(B, S, SGU_GROUPS, SGU_GROUP_DIM)
        v_sgu = rmsnorm(jax.nn.gelu(v_sgu).reshape(B, S, SGU_GROUPS, SGU_GROUP_DIM), sgu_norm_g[i])
        y_a = chunked_spatial_gating(u, v_sgu, w_s[i], b_s[i]).reshape(B, S, SGU_WIDTH)

        q = rmsnorm(q.reshape(B, S, SB_HEADS, SB_HEAD_DIM), q_norm_g[i])
        k = rmsnorm(k.reshape(B, S, SB_HEADS, SB_HEAD_DIM), k_norm_g[i])
        v_att = v_att.reshape(B, S, SB_HEADS, SB_HEAD_DIM)
        y_b = stick_breaking_attention(q, k, v_att).reshape(B, S, SB_WIDTH)

        merged = jax.nn.sigmoid(g_a) * (y_a @ w_up_a[i]) + jax.nn.sigmoid(g_b) * (y_b @ w_up_b[i])
        x = x + merged @ w_o[i]

        h = rmsnorm(x, ffn_norm_g[i])
        hid = h @ w_ffn_in[i]
        gate = hid[..., :FFN_HIDDEN]
        up = hid[..., FFN_HIDDEN:]
        x = x + (jax.nn.silu(gate) * up) @ w_ffn_out[i]

        ple = p[i] @ w_ple[i]
        x = x + jax.nn.sigmoid(rmsnorm(x, ple_norm_g[i]) @ w_ple_gate[i]) * ple
    return x


def setup_inputs(seed=0):
    out = dict(first_inputs(seed))
    for name, value in second_inputs(seed + 1).items():
        if name != "x":
            out[name + "_2"] = value
    return out


def reference(
    x, c, positions, norm_g, mod_w, mod_b, pool_w_in, pool_w_grp, pool_scale, pool_w_out,
    attn_w_in, attn_w_out, final_g, p_2, attn_norm_g_2, w_in_2, sgu_norm_g_2, w_s_2, b_s_2,
    q_norm_g_2, k_norm_g_2, w_up_a_2, w_up_b_2, w_o_2, ffn_norm_g_2, w_ffn_in_2, w_ffn_out_2,
    ple_norm_g_2, w_ple_gate_2, w_ple_2,
):
    x = first_block(
        x, c, positions, norm_g, mod_w, mod_b, pool_w_in, pool_w_grp, pool_scale, pool_w_out,
        attn_w_in, attn_w_out, final_g,
    )
    return second_block(
        x, p_2, attn_norm_g_2, w_in_2, sgu_norm_g_2, w_s_2, b_s_2, q_norm_g_2, k_norm_g_2,
        w_up_a_2, w_up_b_2, w_o_2, ffn_norm_g_2, w_ffn_in_2, w_ffn_out_2, ple_norm_g_2,
        w_ple_gate_2, w_ple_2,
    )


_drawn_inputs = setup_inputs


def setup_inputs(seed=0):
    import zlib

    import numpy as np

    out = dict(_drawn_inputs(seed))
    spreads = {}
    factors = {'norm_g': 6.234,
     'mod_b': 3.035,
     'pool_scale': 2.752,
     'sgu_norm_g_2': 5.056,
     'q_norm_g_2': 8.0,
     'k_norm_g_2': 8.0,
     'ple_norm_g_2': 24.994,
     'b_s_2': 2.71}
    for name, (base, spread) in spreads.items():
        noise = np.random.default_rng([zlib.crc32(name.encode()), seed]).standard_normal(out[name].shape)
        drawn = base * np.exp(spread * noise) if base else spread * noise
        out[name] = __import__('jax').numpy.asarray(drawn.astype(out[name].dtype))
    for name, factor in factors.items():
        out[name] = (out[name] * factor).astype(out[name].dtype)
    return out
```

```python
import numpy as np

import concourse.bass as bass
from concourse import mybir

F32 = mybir.dt.float32
F32R = mybir.dt.float32r
I32 = mybir.dt.int32
ALU = mybir.AluOpType
ACT = mybir.ActivationFunctionType
AX_X = mybir.AxisListType.X

P = 128
T = 256
TB = T // P
D = 2048
KT = D // P
N = 512
SLOT = 1024
RAW = 4
SPLIT = 4
EPS = 1e-6
HEADS, HD = 16, 128
IH, ID = 16, 64
ROT, IROT = HD // 4, ID // 4
HALVES = ROT // 2 + IROT // 2
TOPK = 64
SBH = 8
SGU = 8
HID = 5632
HKT = HID // P
LOW = -3.0e38
TAKEN = -3.4e38
TWO_PI = 2 * np.pi
PI_IN = 3.1415925
TWO_PI_PARTS = (6.28125, 1.93500518798828125e-3, 3.019915981e-7)
ROUND = 1.5 * 2.0 ** 23

Q1, K1, V1, G1, QI, KI, WI, PROJ1 = 0, 2048, 4096, 6144, 8192, 9216, 9280, 9296
U2, S2, Q2, K2, V2, GA, GB, PROJ2 = 0, 1024, 2048, 3072, 4096, 5120, 7168, 9216

PHASES = [
    ("mod0", 16, "MMMM"),
    ("pool_v", 4, "WWWWWMMWMMWMMWMM"),
    ("pool_g", 4, "WWWWWMMWMMWMMWMM"),
    ("grp", 4, "WW"),
    ("pool_out", 4, "WWWWWMMWMMWMMWMM"),
    ("attn_qkv", 12, "WWWWWMWWMW"),
    ("attn_gate", 4, "WWWWWMWWMW"),
    ("attn_qi", 2, "WWWWWWWW"),
    ("attn_rest", 1, "WW"),
    ("attn_out", 4, "WWWWWWWW"),
    ("in_uv", 4, "WWWWWWWW"),
    ("in_qkv", 6, "WWWWWWWW"),
    ("in_gates", 8, "WWWWWWWW"),
    ("up", 8, "WWWW"),
    ("w_o", 4, "WWWWWWWW"),
    ("ffn_in", 22, "WWWWWWWW"),
    ("ffn_out", 44, "WW"),
    ("ple_in", 4, "WWWWWWWWW"),
]


class Phase:
    def __init__(self, name, chunks, seq, slot0, w0, chunk0):
        self.name, self.chunks, self.seq = name, chunks, seq
        self.slot0, self.w0, self.chunk0 = slot0, w0, chunk0
        self.per = len(seq)
        self.w_at = [j for j, k in enumerate(seq) if k == "W"]
        self.ws = len(self.w_at)


def plan():
    phases, slot, w, chunk = {}, 0, 0, 0
    for name, chunks, seq in PHASES:
        phases[name] = Phase(name, chunks, seq, slot, w, chunk)
        slot += chunks * len(seq)
        w += chunks * seq.count("W")
        if name == "ple_in":
            chunk += 2 * chunks
        elif name not in ("mod0", "attn_rest", "ffn_out"):
            chunk += chunks
    return phases


def build(nc, x_in, c, positions, norm_g, mod_w, mod_b, pool_w_in, pool_w_grp, pool_scale, pool_w_out,
          attn_w_in, attn_w_out, final_g, p_in, attn_norm_g, w_in, sgu_norm_g, w_s_in, b_s, q_norm_g,
          k_norm_g, w_up_a, w_up_b, w_o, ffn_norm_g, w_ffn_in, w_ffn_out, ple_norm_g, w_ple_gate, w_ple,
          const_in, pool_mix_in, out):
    ph = plan()
    kinds = "".join(seq * chunks for _, chunks, seq in PHASES)

    base = (nc.sbuf_base + 63) // 64 * 64
    K = 1024

    def at(name, kib, shape, dt=F32):
        return nc.alloc_sbuf_tensor_at(name, shape, dt, offset=base + int(kib * K))

    x = at("x", 0, [P, TB, D])
    raw = at("raw", 16, [P, RAW, SLOT])
    w_hi = at("w_hi", 32, [P, SPLIT, SLOT], F32R)
    w_lo = at("w_lo", 48, [P, SPLIT, SLOT], F32R)
    act_hi = at("act_hi", 64, [P, KT, T], F32R)
    act_lo = at("act_lo", 80, [P, KT, T], F32R)
    mod_row = at("mod_row", 96, [P, D])
    const = at("const", 104, [P, 3 * P + 3 * 384 + HALVES])
    vec_rows = at("vec_rows", 112, [P, P])
    vec = at("vec", 112.5, [P, P])
    small = at("small", 113, [P, 192])
    WORK = 114
    TMP = WORK + 73
    v_nat = at("v_nat", WORK, [P, TB, D])
    gate_nat = at("gate_nat", WORK + 16, [P, TB, D])
    u_nat = at("u_nat", WORK + 32, [P, TB, D])
    normed = at("normed", WORK + 32, [P, TB, D])
    pool_mix = at("pool_mix", WORK + 48, [P, TB, 4, T])
    mod_acc = at("mod_acc", WORK + 56, [P, 2 * D])
    turned = at("turned", TMP, [P, 2, 2 * T])
    resid = at("resid", TMP + 4, [P, TB, N])
    proj1 = at("proj1", WORK, [P, TB, PROJ1])
    rope_t = at("rope_t", TMP, [P, 4, 512])
    rope_a = at("rope_a", TMP + 8, [P, 4, TB, HALVES])
    rope_s = at("rope_s", TMP + 9, [P, TB, HALVES])
    rope_c = at("rope_c", TMP + 9.25, [P, TB, HALVES])
    ki_twice = at("ki_twice", TMP + 9.5, [P, TB, P])
    kiT = at("kiT", TMP + 10.5, [P, T])
    qiT = at("qiT", 64, [P, IH // 2, T])
    work = at("work", TMP + 11.5, [P, 384])
    amask = at("amask", TMP + 13, [P, 384])
    relu = at("relu", TMP + 15, [P, 2, 384])
    logit = at("logit", TMP, [P, 2, 384])
    prob = at("prob", TMP + 3, [P, 2, 384])
    probT = at("probT", TMP + 6, [P, 2, 384])
    qT = at("qT", 64, [P, KT, T])
    kT = at("kT", 80, [P, KT, T])
    head_in = at("head_in", TMP + 15, [P, 2, T])
    row = at("row", WORK + 16, [P, D])
    normed2 = at("normed2", WORK, [P, TB, D])
    proj2 = at("proj2", WORK, [P, TB, PROJ2])
    squares = at("squares", TMP, [P, 3072])
    sgu_row = at("sgu_row", TMP + 12, [P, 1024])
    w_s = at("w_s", 96, [P, SGU, P])
    w_sT = at("w_sT", 100, [P, SGU, P])
    sb_abs = at("sb_abs", TMP, [P, 2, 384])
    sb_log = at("sb_log", TMP + 3, [P, 2, 384])
    sb_miss = at("sb_miss", TMP + 6, [P, 2, 384])
    sb_hit = at("sb_hit", TMP + 9, [P, 2, 384])
    sb_w = at("sb_w", TMP + 12, [P, 2, 384])
    q2T = at("q2T", 64, [P, SBH, T])
    k2T = at("k2T", 72, [P, SBH, T])
    hid_hi = at("hid_hi", WORK, [P, HKT, T], F32R)
    hid_lo = at("hid_lo", WORK + 44, [P, HKT, T], F32R)
    hid = at("hid", WORK + 88, [P, TB, N])
    hid_at = at("hid_at", 96, [P, 2, 2, T], F32R)
    pT_hi = at("pT_hi", WORK + 32, [P, 2, T], F32R)
    pT_lo = at("pT_lo", WORK + 34, [P, 2, T], F32R)
    p_nat = at("p_nat", WORK + 36, [P, TB, T])
    ple = at("ple", WORK + 40, [P, TB, N])
    assert (WORK + 92) * K <= nc.sbuf_bytes_remaining

    ident, ones = const[:, 0:P], const[:, P:2 * P]
    later = const[:, 2 * P:3 * P]
    o = 3 * P
    hidden = const[:, o:o + 384]
    strict = const[:, o + 384:o + 768]
    nstrict = const[:, o + 768:o + 1152]
    freq = const[:, o + 1152:o + 1152 + HALVES]
    norm0, norm1, pscale, anorm, fnorm, pnorm, ccol = (vec[:, 16 * i:16 * i + 16] for i in range(7))
    qg, kg, bs = vec[:, 112:113], vec[:, 113:114], vec[:, 114:122]
    cond = small[:, 0:16]
    shift, scale1 = small[:, 16:32], small[:, 32:48]
    sumsq, rstd = small[:, 48:50], small[:, 50:52]
    pos = small[:, 52:54]
    best = small[:, 56:64]
    qgs = small[:, 80:81]
    top, ntop, den, rden = (small[:, 64 + 4 * i:68 + 4 * i] for i in range(4))
    ssq2, rs2 = small[:, 96:144], small[:, 144:192]
    newton = at("newton", TMP + 18, [P, 2, 24])
    pos_i = at("pos_i", 113.875, [P, TB], I32)

    ps = nc.alloc_psum_tensor("ps", [P, 8, N], F32)
    acc = [[ps[:, 0], ps[:, 1]], [ps[:, 2], ps[:, 3]]]
    turn = [ps[:, 4], ps[:, 5]]
    rest = [ps[:, 6], ps[:, 7]]

    def sem(name):
        return nc.alloc_semaphore(name)

    loaded = [sem(f"loaded{i}") for i in range(RAW)]
    hi_ready = sem("hi_ready")
    slot_done = sem("slot_done")
    w_used = sem("w_used")
    pair_read = [sem("pair_read0"), sem("pair_read1")]
    turn_full = sem("turn_full")
    turn_affine = sem("turn_affine")
    turn_hi = sem("turn_hi")
    turn_done = sem("turn_done")
    s_full, s_read, l_max, l_ready, p_ready = map(sem, ("s_full", "s_read", "l_max", "l_ready", "p_ready"))
    pt_full, pt_ready, o_full, r_ready, o_done = map(sem, ("pt_full", "pt_ready", "o_full", "r_ready", "o_done"))
    z_full, z_read, b_abs, b_log, b_sum, b_miss = map(sem, ("z_full", "z_read", "b_abs", "b_log", "b_sum", "b_miss"))
    b_tail, b_arg, b_w, b_mask, y_full, y_done = map(sem, ("b_tail", "b_arg", "b_w", "b_mask", "y_full", "y_done"))
    i_full, i_relu, i_done = map(sem, ("i_full", "i_relu", "i_done"))
    q_copied, k_copied, hid_copied = map(sem, ("q_copied", "k_copied", "hid_copied"))
    gate_ready = sem("gate_ready")
    hid_ready = sem("hid_ready")
    act_chain, dve_chain = sem("act_chain"), sem("dve_chain")
    stored = sem("stored")
    events = {}

    def ev(name):
        if name not in events:
            events[name] = sem(name)
        return events[name]

    def wait(eng, s, value):
        if not (isinstance(value, int) and value <= 0):
            eng.wait_ge(s, value)

    def repeat(eng, n, body):
        if n == 1:
            body(0)
        elif n > 1:
            with eng.Fori(0, n) as i:
                body(i)

    def skewed(eng, n, step):
        for t in range(4):
            step(t, t % 2, True, t >= 1, t >= 2)
        with eng.Fori(0, (n - 4) // 2) as i:
            for q in range(2):
                step(i * 2 + (4 + q), q, True, True, True)
        for t in (n, n + 1):
            step(t, t % 2, False, t == n, True)

    turns, n_turns = {}, 0
    for name, banks in (("h0", 8), ("pooled", 8), ("mixed", 8), ("h1", 8), ("qi", 4), ("ki", 1), ("qk1", 16),
                        ("o1", 8), ("h2", 8), ("qk2", 8), ("y2", 8), ("merged", 8), ("h3", 8), ("hid", 22),
                        ("h4", 8), ("p", 1)):
        turns[name] = n_turns
        n_turns += banks

    def slot_of(p, c, j, i=0, per=0):
        return p.slot0 + c * p.per + j, (i, per * p.per)

    def raw2(r, nk=2, cols=N):
        return raw[:, r, 0:nk * cols].rearrange("p (k n) -> p k n", k=nk)

    x_t = x_in.rearrange("b (t p) d -> p (b t) d", p=P)
    out_t = out.rearrange("b (t p) d -> p (b t) d", p=P)
    pairs_before = ph["ffn_in"].chunk0 // 2
    by_channel = lambda v: v.rearrange("l (k c) -> (l k) c", c=P)
    vec_sources = [by_channel(v) for v in (norm_g, pool_scale, attn_norm_g, ffn_norm_g, ple_norm_g, c, q_norm_g,
                                           k_norm_g)] + [b_s[0]]

    with nc.Block() as block:
        @block.sync
        def _(sp):
            def load(s0, n, i, src, shape=None):
                r = s0 % RAW
                wait(sp, slot_done, s0 - RAW + 1 + i * n)
                dst = raw[:, r, :] if shape is None else raw2(r, *shape)
                sp.dma_start(dst, src).then_inc(loaded[r], 16)

            def rows(w, k0, nk, col, cols):
                return w[bass.ds(k0 * P, nk * P), bass.ds(col, cols)].rearrange("(k p) n -> p k n", p=P)

            def product(name, w, bodies, per, col0=0, mod=None, kts=KT):
                p = ph[name]

                def body(i):
                    for q in range(per):
                        k = m = 0
                        for j, kind in enumerate(p.seq):
                            s0 = p.slot0 + q * p.per + j
                            if kind == "W":
                                src = rows(w, k, 2, (i * per + q) * N + col0, N)
                                load(s0, per * p.per, i, src, (2, N))
                                k += 2
                            else:
                                load(s0, per * p.per, i, mod(i * per + q, m))
                                m += 1
                repeat(sp, bodies, body)

            def mod_rows(layer, kt, col):
                return mod_w[layer, bass.ds(kt * P, P), bass.ds(col, SLOT)]

            def mod0(i):
                for j in range(4):
                    load(j, 4, i, mod_rows(0, i, j * SLOT))

            for j in range(4):
                load(j, 4, 0, mod_rows(0, 0, j * SLOT))
            with sp.Fori(1, KT) as i:
                mod0(i)
            product("pool_v", pool_w_in[0], 2, 2, mod=lambda c, m: mod_rows(0, c * 4 + m // 2, 2 * D + m % 2 * SLOT))
            product("pool_g", pool_w_in[0], 2, 2, D, lambda c, m: mod_rows(1, c * 2 + m // 4, m % 4 * SLOT))
            for g in range(4):
                for j in range(2):
                    load(ph["grp"].slot0 + 2 * g + j, 0, 0, rows(pool_w_grp[0, g], 2 * j, 2, 0, N), (2, N))
            product("pool_out", pool_w_out[0], 2, 2, mod=lambda c, m: mod_rows(1, c * 2 + m // 4 + 8, m % 4 * SLOT))
            gate1 = lambda c, m: mod_rows(1, c, 2 * D + m * SLOT)
            product("attn_qkv", attn_w_in[0], 6, 2, mod=gate1)
            product("attn_gate", attn_w_in[0], 2, 2, 12 * N, lambda c, m: gate1(c + 12, m))
            product("attn_qi", attn_w_in[0], 1, 2, 16 * N)
            for j in range(2):
                load(ph["attn_rest"].slot0 + j, 0, 0, rows(attn_w_in[0], 8 * j, 8, 18 * N, PROJ1 - 18 * N),
                     (8, PROJ1 - 18 * N))
            product("attn_out", attn_w_out[0], 2, 2)
            product("in_uv", w_in[0], 2, 2)
            product("in_qkv", w_in[0], 3, 2, 4 * N)
            product("in_gates", w_in[0], 4, 2, 10 * N)
            p = ph["up"]

            def up(i):
                for q, w in enumerate((w_up_a, w_up_b)):
                    for j in range(4):
                        load(p.slot0 + 4 * q + j, 8, i, rows(w[0], 2 * j, 2, i * N, N), (2, N))
            repeat(sp, 4, up)
            product("w_o", w_o[0], 2, 2)
            p = ph["ffn_in"]

            def ffn_in(i):
                for q in range(2):
                    for j in range(8):
                        load(p.slot0 + 8 * q + j, 16, i, rows(w_ffn_in[0], 2 * j, 2, i * N + q * HID, N), (2, N))
            repeat(sp, 11, ffn_in)
            p = ph["ffn_out"]

            def ffn_out(i):
                for q in range(2):
                    for j in range(2):
                        load(p.slot0 + 2 * q + j, 4, i,
                             w_ffn_out[0, bass.ds((i * 2 + q) * P, P), j * SLOT:(j + 1) * SLOT])
            repeat(sp, HKT // 2, ffn_out)
            p = ph["ple_in"]
            for c in range(4):
                for j in range(9):
                    w, k = (w_ple_gate[0], 2 * j) if j < 8 else (w_ple[0], 0)
                    load(p.slot0 + 9 * c + j, 0, 0, rows(w, k, 2, c * N, N), (2, N))
            for c in range(4):
                sp.wait_ge(ev("x_final"), c + 1)
                sp.dma_start(out_t[:, :, c * N:(c + 1) * N], x[:, :, c * N:(c + 1) * N]).then_inc(stored, 16)
            sp.wait_ge(stored, 64)

        @block.gpsimd
        def _(pool):
            def row_start(buf, width, src, name):
                pool.memset(buf, 0.0).then_inc(ev(name + "_zero"), 1)
                pool.wait_ge(ev(name + "_zero"), 1)
                pool.dma_start(buf[0:1, :], src).then_inc(ev(name), 16)

            def head_copies(n, src, turned, banks, used, copied):
                pool.wait_ge(turn_done, turns[turned] + banks)
                for h in range(2):
                    pool.tensor_copy(head_in[:, h, :], src[:, h, :]).then_inc(copied, 1)
                with pool.Fori(0, n // 2 - 1) as i:
                    for q in range(2):
                        pool.wait_ge(used, i * 2 + q + 1)
                        pool.tensor_copy(head_in[:, q, :], src[:, bass.ds(i * 2 + (q + 2), 1), :].rearrange(
                            "p a t -> p (a t)")).then_inc(copied, 1)

            b0, b1 = mod_b[0:1, :], mod_b[1:2, :]
            row_start(mod_acc[:, :], 2 * D, b0[:, 0:2 * D], "acc0_start")
            row_start(mod_row[:, :], D, b0[:, 2 * D:3 * D], "row0_start")
            pool.wait_ge(ev("cols0_read"), 1)
            row_start(mod_acc[:, :], 2 * D, b1[:, 0:2 * D], "acc1_start")
            pool.wait_ge(ev("x1_done"), 1)
            row_start(mod_row[:, :], D, b1[:, 2 * D:3 * D], "row1_start")
            head_copies(HEADS, qT, "qk1", 16, s_full, q_copied)
            pool.wait_ge(ev("x2_done"), 1)
            pool.dma_start(row[:, :], final_g.rearrange("(a d) -> a d", a=1).partition_broadcast(P)).then_inc(
                ev("final_row"), 16)
            pool.dma_start(w_s[:, :, :], w_s_in[0].rearrange("g t s -> t g s")).then_inc(ev("w_s_in"), 16)
            pool.wait_ge(ev("w_s_in"), 16)
            pool.affine_select(out=w_s[:, :, :], in_=w_s[:, :, :], compare_op=ALU.is_ge, fill=0.0, base=0,
                               pattern=[[0, SGU], [-1, P]], channel_multiplier=1).then_inc(ev("w_s_low"), 1)
            pool.wait_ge(ev("tmp_free"), 1)
            pool.dma_start(sgu_row[:, :], sgu_norm_g.rearrange("a g c -> a (g c)").partition_broadcast(P)).then_inc(
                ev("sgu_row"), 16)
            head_copies(SBH, k2T, "qk2", 8, z_full, k_copied)

            def hid_copy(i, first=False):
                for q in range(2):
                    kt = i * 2 + q
                    if not first:
                        pool.wait_ge(w_used, ph["ffn_out"].w0 + 2 * q - 2 + i * 4)
                    pool.tensor_copy(hid_at[:, q, 0, :], hid_hi[:, bass.ds(kt, 1), :].rearrange(
                        "p a t -> p (a t)").bitcast(F32))
                    pool.tensor_copy(hid_at[:, q, 1, :], hid_lo[:, bass.ds(kt, 1), :].rearrange(
                        "p a t -> p (a t)").bitcast(F32)).then_inc(hid_copied, 1)
            pool.wait_ge(turn_done, turns["h4"])
            hid_copy(0, True)
            with pool.Fori(1, HKT // 2) as i:
                hid_copy(i)
            pool.wait_ge(ev("x5_done"), 1)
            pool.dma_start(p_nat[:, :, :], p_in[0].rearrange("b (t q) c -> q (b t) c", q=P)).then_inc(ev("p_in"), 16)

        @block.scalar
        def _(act):
            pos_w = [0]
            links = [0]

            def link(ins):
                links[0] += 1
                ins.then_inc(act_chain, 1)
                act.wait_ge(act_chain, links[0])

            w_slots = [s for s, k in enumerate(kinds) if k == "W"]

            def round_w(w0, i=0, nw=0, ns=0):
                s0 = w_slots[w0]
                act.wait_ge(loaded[s0 % RAW], 16 * (s0 // RAW + 1) + i * (16 * (ns // RAW)))
                wait(act, w_used, w0 - SPLIT + 1 + i * nw)
                nc.scalar.copy(w_hi[:, w0 % SPLIT, :], raw[:, s0 % RAW, :]).then_inc(hi_ready, 1)

            def advance(to):
                while pos_w[0] < min(to, len(w_slots)):
                    round_w(pos_w[0])
                    pos_w[0] += 1

            def chunks(name, bodies, per, read=None, mid=None):
                p = ph[name]
                assert pos_w[0] == p.w0 + 4, name

                def body(i):
                    for q in range(per):
                        for j in range(p.ws):
                            round_w(p.w0 + 4 + q * p.ws + j, i, per * p.ws, per * p.per)
                        if read:
                            read(i, q)
                repeat(act, bodies, body)
                pos_w[0] += bodies * per * p.ws

            def read_pair(p, func, dst, per=2):
                def read(i, q):
                    c = p.chunk0 + q
                    act.wait_ge(w_used, p.w0 + (q + 1) * p.ws + i * (per * p.ws))
                    for tb in range(TB):
                        ins = nc.scalar.activation(dst(tb, i * per + q), acc[c % 2][tb], func)
                    ins.then_inc(pair_read[c % 2], 1)
                return read

            def turn_hi_of(name, banks, hi, source="plain", scale=None):
                for b in range(banks):
                    g = turns[name] + b
                    if source == "affine":
                        act.wait_ge(turn_affine, (b + 1) + (8 if name == "h1" else 0))
                    else:
                        act.wait_ge(turn_full, g + 1)
                    src = turned[:, b % 2, :] if source == "affine" else turn[g % 2]
                    if source == "half":
                        nc.scalar.activation(hi(b), src[:, 0:T], ACT.Copy,
                                             scale=1.0 if scale is None else scale(b)).then_inc(turn_hi, 1)
                    elif scale is None:
                        nc.scalar.copy(hi[:, 2 * b:2 * b + 2, :].rearrange("p k t -> p (k t)"), src).then_inc(turn_hi, 1)
                    else:
                        for k in range(2):
                            ins = nc.scalar.activation(hi[:, 2 * b + k, :], src[:, k * T:(k + 1) * T], ACT.Copy,
                                                       scale=scale[:, 2 * b + k:2 * b + k + 1])
                        ins.then_inc(turn_hi, 1)

            def square_sums(scratch, name):
                for tb in range(TB):
                    ins = nc.scalar.activation(scratch[:, tb, :], x[:, tb, :], ACT.Square,
                                               accum_out=sumsq[:, tb:tb + 1])
                ins.then_inc(ev(name), 1)

            def gate_row(name):
                for c in range(4):
                    act.wait_ge(ev(name + "_full"), c + 1)
                    nc.scalar.copy(mod_row[:, c * N:(c + 1) * N], rest[c % 2]).then_inc(ev(name + "_row"), 1)

            act.dma_start(x[:, :, :], x_t).then_inc(ev("x_in"), 16)
            act.dma_start(const[:, :], const_in).then_inc(ev("const_in"), 16)
            at_row = 0
            for src in vec_sources:
                n = src.shape[0]
                act.dma_start(vec_rows[at_row:at_row + n, :], src).then_inc(ev("vec_in"), 16)
                at_row += n
            act.dma_start(pos_i[:, :], positions.rearrange("b (t p) -> p (b t)", p=P),
                          allow_slow_non_contiguous=True).then_inc(ev("vec_in"), 16)
            act.dma_start(pool_mix[:, :, :, :], pool_mix_in).then_inc(ev("mix_in"), 16)

            act.wait_ge(ev("vec"), 1)
            nc.scalar.activation(cond, ccol, ACT.Silu).then_inc(ev("cond"), 1)
            act.wait_ge(ev("angles"), 1)
            nc.scalar.activation(rope_s[:, :, :], rope_a[:, 0, :, :], ACT.Sin)
            nc.scalar.activation(rope_c[:, :, :], rope_a[:, 1, :, :], ACT.Sin).then_inc(ev("rope"), 1)
            act.wait_ge(ev("x_in"), 16)
            square_sums(normed, "sq0")
            advance(4)
            turn_hi_of("h0", 8, act_hi, "affine")
            chunks("pool_v", 2, 2, read_pair(ph["pool_v"], ACT.Copy, lambda tb, c: v_nat[:, tb, bass.ds(c * N, N)]))
            chunks("pool_g", 2, 2, read_pair(ph["pool_g"], ACT.Silu, lambda tb, c: gate_nat[:, tb, bass.ds(c * N, N)]))
            gate_row("gate0")
            turn_hi_of("pooled", 8, act_hi)
            advance(ph["pool_out"].w0 + 4)
            turn_hi_of("mixed", 8, act_hi, scale=pscale)
            chunks("pool_out", 2, 2)
            act.wait_ge(ev("x1_done"), 1)
            square_sums(normed, "sq1")
            turn_hi_of("h1", 8, act_hi, "affine")
            chunks("attn_qkv", 6, 2, read_pair(ph["attn_qkv"], ACT.Copy, lambda tb, c: proj1[:, tb, bass.ds(c * N, N)]))
            chunks("attn_gate", 2, 2, read_pair(ph["attn_gate"], ACT.Silu,
                                                lambda tb, c: proj1[:, tb, bass.ds(c * N + G1, N)]))
            chunks("attn_qi", 1, 2, read_pair(ph["attn_qi"], ACT.Copy, lambda tb, c: proj1[:, tb, c * N + QI:c * N + QI + N]))
            advance(ph["attn_out"].w0 + 4)
            act.wait_ge(w_used, ph["attn_rest"].w0 + 2)
            nc.scalar.copy(proj1[:, :, KI:PROJ1], ps[:, 6:8, 0:PROJ1 - KI]).then_inc(
                ev("rest_read"), 1)
            gate_row("gate1")
            turn_hi_of("qi", 4, lambda b: qiT[:, 2 * b, :], "half")
            turn_hi_of("ki", 1, lambda b: kiT[:, :], "half")
            for h in range(IH):
                act.wait_ge(i_full, h + 1)
                wait(act, i_done, h - 1)
                nc.scalar.activation(relu[:, h % 2, :], rest[h % 2][:, 0:384], ACT.Relu).then_inc(i_relu, 1)
            turn_hi_of("qk1", 16, lambda b: (qT if b % 2 == 0 else kT)[:, b // 2 * 2, :], "half")

            def attend(t, par, s1, s2, s3):
                if s2:
                    wait(act, pt_full, t)
                    wait(act, o_full, t - 2)
                    nc.scalar.copy(probT[:, 1 - par, :], turn[1 - par][:, 0:384]).then_inc(pt_ready, 1)
                if s1:
                    wait(act, l_ready, t + 1)
                    wait(act, pt_full, t - 1)
                    wait(act, o_done, t - 1)
                    for tb, (c0, c1) in enumerate(((0, P), (P, 384))):
                        ins = nc.scalar.activation(prob[:, par, c0:c1], logit[:, par, c0:c1], ACT.Exp,
                                                   bias=ntop[:, 2 * par + tb:2 * par + tb + 1],
                                                   accum_out=den[:, 2 * par + tb:2 * par + tb + 1])
                    ins.then_inc(p_ready, 1)
            skewed(act, HEADS, attend)
            turn_hi_of("o1", 8, act_hi)
            chunks("attn_out", 2, 2)
            act.wait_ge(ev("x2_done"), 1)
            square_sums(normed2, "sq2")
            act.wait_ge(ev("x3_done"), 1)
            square_sums(normed2, "sq3")
            turn_hi_of("h2", 8, act_hi, scale=anorm)
            chunks("in_uv", 2, 2, read_pair(ph["in_uv"], ACT.Gelu_apprx_tanh, lambda tb, c: proj2[:, tb, bass.ds(c * N, N)]))
            chunks("in_qkv", 3, 2, read_pair(ph["in_qkv"], ACT.Copy, lambda tb, c: proj2[:, tb, bass.ds(c * N + Q2, N)]))
            chunks("in_gates", 4, 2, read_pair(ph["in_gates"], ACT.Sigmoid, lambda tb, c: proj2[:, tb, bass.ds(c * N + GA, N)]))
            for tb in range(TB):
                wait(act, ev("squares_sum"), tb)
                nc.scalar.activation(squares[:, :], proj2[:, tb, S2:V2], ACT.Square).then_inc(ev("squares"), 1)
            for b in range(2):
                act.wait_ge(ev("ws_turned"), b + 1)
                nc.scalar.copy(w_sT[:, 4 * b:4 * b + 4, :].rearrange("p g t -> p (g t)"), rest[b]).then_inc(ev("w_sT"), 1)
            turn_hi_of("qk2", 8, lambda b: (q2T if b < 4 else k2T)[:, b % 4 * 2, :], "half",
                       scale=lambda b: qgs if b < 4 else kg)

            def stick(t, par, s1, s2, s3):
                if s1:
                    act.wait_ge(z_full, t + 1)
                    wait(act, b_log, t - 1)
                    nc.scalar.activation(sb_abs[:, par, :], rest[par][:, 0:384], ACT.Abs).then_inc(b_abs, 1)
                    act.wait_ge(b_abs, t * 2 + 1)
                    nc.scalar.activation(sb_abs[:, par, :], sb_abs[:, par, :], ACT.Exp, scale=-1.0).then_inc(b_abs, 1)
                    act.wait_ge(b_abs, t * 2 + 2)
                    wait(act, z_read, t - 1)
                    nc.scalar.activation(sb_log[:, par, :], sb_abs[:, par, :], ACT.Ln, bias=1.0).then_inc(b_log, 1)
                if s2:
                    act.wait_ge(b_arg, t)
                    wait(act, y_full, t - 2)
                    nc.scalar.activation(sb_w[:, 1 - par, :], sb_hit[:, 1 - par, :], ACT.Exp).then_inc(b_w, 1)
                if s3:
                    act.wait_ge(y_full, t - 1)
                    nc.scalar.copy(proj2[:, :, bass.ds(t * P + (Q2 - 2 * P), P)],
                                   ps[:, 2 * par, 0:T].rearrange("p (t d) -> p t d", t=TB)).then_inc(y_done, 1)
            skewed(act, SBH, stick)
            turn_hi_of("y2", 8, act_hi)
            chunks("up", 4, 2)
            turn_hi_of("merged", 8, act_hi)
            chunks("w_o", 2, 2)
            act.wait_ge(ev("x4_done"), 1)
            square_sums(normed2, "sq4")
            turn_hi_of("h3", 8, act_hi, scale=fnorm)
            p = ph["ffn_in"]

            def hid_hi_of(j):
                for b in range(2):
                    g = turns["hid"] + b
                    act.wait_ge(turn_full, g + 1 + j * 2)
                    nc.scalar.copy(hid_hi[:, bass.ds(j * 4 + 2 * b, 2), :].rearrange("p k t -> p (k t)"),
                                   turn[g % 2]).then_inc(turn_hi, 1)

            def ffn_in(j, first):
                for q in range(2):
                    for k in range(8):
                        round_w(p.w0 + 4 + q * 8 + k, j, 16, 16)
                    if q == 0:
                        act.wait_ge(w_used, p.w0 + 8 + j * 16)
                        if not first:
                            act.wait_ge(turn_full, turns["hid"] + j * 2)
                        for tb in range(TB):
                            ins = nc.scalar.activation(hid[:, tb, :], acc[0][tb], ACT.Silu)
                        ins.then_inc(gate_ready, 1)
                        if not first:
                            hid_hi_of(j - 1)
            ffn_in(0, True)
            with act.Fori(1, 11) as j:
                ffn_in(j, False)
            hid_hi_of(10)
            pos_w[0] += 22 * 8
            p = ph["ffn_out"]

            def ffn_out(i):
                for j in range(4):
                    round_w(p.w0 + 4 + j, i, 4, 4)
            repeat(act, 22, ffn_out)
            pos_w[0] += 88
            act.wait_ge(ev("x5_done"), 1)
            square_sums(normed2, "sq5")
            turn_hi_of("h4", 8, act_hi, scale=pnorm)
            turn_hi_of("p", 1, pT_hi)
            p = ph["ple_in"]
            for c in range(4):
                advance(p.w0 + 9 * c + 8 + 4)
                act.wait_ge(w_used, p.w0 + 9 * c + 8)
                wait(act, ev("x_final"), c)
                for tb in range(TB):
                    ins = nc.scalar.activation(ple[:, tb, :], acc[0][tb], ACT.Sigmoid)
                ins.then_inc(pair_read[0], 1)

        @block.vector
        def _(dve):
            V = nc.vector
            pos_s = [0]
            links = [0]

            def link(ins):
                links[0] += 1
                ins.then_inc(dve_chain, 1)
                dve.wait_ge(dve_chain, links[0])

            w_of = {}
            for s, k in enumerate(kinds):
                if k == "W":
                    w_of[s] = len(w_of)

            def split(s0, i=0, ns=0, nw=0):
                w0 = w_of[s0]
                dve.wait_ge(hi_ready, w0 + 1 + i * nw)
                V.tensor_tensor(w_lo[:, w0 % SPLIT, :], raw[:, s0 % RAW, :],
                                w_hi[:, w0 % SPLIT, :].bitcast(F32), ALU.subtract).then_inc(slot_done, 1)

            def modulate(s0, target, kt, apart, i=0, ns=0):
                dve.wait_ge(loaded[s0 % RAW], 16 * (s0 // RAW + 1) + i * (16 * (ns // RAW)))
                wait(dve, slot_done, s0 - apart + 1 + i * ns)
                V.scalar_tensor_tensor(out=target, in0=raw[:, s0 % RAW, :], scalar=cond[:, bass.ds(kt, 1)],
                                       in1=target, op0=ALU.mult, op1=ALU.add).then_inc(slot_done, 1)

            def advance(w_to):
                while pos_s[0] < len(kinds) and w_of[pos_s[0]] < w_to:
                    split(pos_s[0])
                    pos_s[0] += 1

            def chunks(name, bodies, per, read=None, mod=None):
                p = ph[name]
                assert pos_s[0] == p.slot0 + 4, name

                def body(i):
                    for q in range(per):
                        m = 0
                        for j in range(4, p.per + 4):
                            s0 = p.slot0 + q * p.per + j
                            if j < p.per and p.seq[j] == "M":
                                target, kt, apart = mod(i * per + q, m)
                                modulate(s0, target, kt, apart, i, per * p.per)
                                m += 1
                            else:
                                split(s0, i, per * p.per, per * p.ws)
                        if read:
                            read(i, q)
                repeat(dve, bodies, body)
                pos_s[0] += bodies * per * p.per

            def acc_cols(m):
                return mod_acc[:, m % 4 * SLOT:(m % 4 + 1) * SLOT]

            def row_cols(m):
                return mod_row[:, m % 2 * SLOT:(m % 2 + 1) * SLOT]

            def add_chunk(p, gated, signal=None):
                def read(i, q):
                    c = p.chunk0 + q
                    dve.wait_ge(w_used, p.w0 + (q + 1) * p.ws + i * (2 * p.ws))
                    col = bass.ds((i * 2 + q) * N, N)
                    for tb in range(TB):
                        if gated:
                            V.tensor_tensor(resid[:, tb, :], acc[c % 2][tb], mod_row[:, col], ALU.mult).then_inc(
                                ev(p.name + "_gated"), 1)
                            dve.wait_ge(ev(p.name + "_gated"), 2 * q + tb + 1 + i * 4)
                            ins = V.tensor_tensor(x[:, tb, col], x[:, tb, col], resid[:, tb, :], ALU.add)
                        else:
                            ins = V.tensor_tensor(x[:, tb, col], acc[c % 2][tb], x[:, tb, col], ALU.add)
                        if tb == TB - 1:
                            ins.then_inc(pair_read[c % 2], 1)
                return read

            def all_read(p):
                for q in range(2):
                    dve.wait_ge(pair_read[q], (p.chunk0 + p.chunks) // 2)

            def rsqrt(sums, y, scale):
                n = y.shape[1]
                half, sq = newton[:, 0, 0:n], newton[:, 1, 0:n]
                link(V.tensor_scalar(half, sums, scale, EPS, ALU.mult, ALU.add))
                link(V.tensor_scalar(sq.bitcast(I32), half.bitcast(I32), 1, None, ALU.logical_shift_right))
                link(V.tensor_scalar(y.bitcast(I32), sq.bitcast(I32), -1.0, float(0x5F3759DF), ALU.mult, ALU.add))
                link(V.tensor_scalar(half, half, -0.5, None, ALU.mult))
                for _ in range(3):
                    link(V.tensor_tensor(sq, y, y, ALU.mult))
                    link(V.tensor_tensor(sq, sq, half, ALU.mult))
                    link(V.scalar_tensor_tensor(out=y, in0=sq, scalar=1.5, in1=y, op0=ALU.add, op1=ALU.mult))

            def normalize(sq, dst, done):
                dve.wait_ge(ev(sq), 1)
                rsqrt(sumsq, rstd, 1.0 / D)
                for tb in range(TB):
                    V.tensor_scalar(dst[:, tb, :], x[:, tb, :], rstd[:, tb:tb + 1], None, ALU.mult).then_inc(ev(done), 1)

            def turn_lo_of(name, banks, hi, lo, scale=None):
                for b in range(banks):
                    g = turns[name] + b
                    dve.wait_ge(turn_hi, g + 1)
                    if scale is None:
                        V.tensor_tensor(lo[:, 2 * b:2 * b + 2, :].rearrange("p k t -> p (k t)"), turn[g % 2],
                                        hi[:, 2 * b:2 * b + 2, :].rearrange("p k t -> p (k t)").bitcast(F32),
                                        ALU.subtract).then_inc(turn_done, 1)
                    else:
                        for k in range(2):
                            ins = V.scalar_tensor_tensor(
                                out=lo[:, 2 * b + k, :], in0=turn[g % 2][:, k * T:(k + 1) * T],
                                scalar=scale[:, 2 * b + k:2 * b + k + 1], in1=hi[:, 2 * b + k, :].bitcast(F32),
                                op0=ALU.mult, op1=ALU.subtract)
                        ins.then_inc(turn_done, 1)

            def turn_half_of(name, banks, dst, scale=None):
                for b in range(banks):
                    g = turns[name] + b
                    dve.wait_ge(turn_hi, g + 1)
                    if scale is None:
                        ins = V.tensor_copy(dst(b), turn[g % 2][:, T:2 * T])
                    else:
                        ins = V.tensor_scalar(dst(b), turn[g % 2][:, T:2 * T], scale(b), None, ALU.mult)
                    ins.then_inc(turn_done, 1)

            def turn_affine_of(name, layer):
                for b in range(9):
                    if b < 8:
                        g = turns[name] + b
                        dve.wait_ge(turn_full, g + 1)
                        wait(dve, turn_done, g - 1)
                        for k in range(2):
                            ct = 2 * b + k
                            ins = V.tensor_scalar(turned[:, b % 2, k * T:(k + 1) * T], turn[g % 2][:, k * T:(k + 1) * T],
                                                  scale1[:, ct:ct + 1], shift[:, ct:ct + 1], ALU.mult, ALU.add)
                        ins.then_inc(turn_affine, 1)
                    if b > 0:
                        g = turns[name] + b - 1
                        dve.wait_ge(turn_hi, g + 1)
                        V.tensor_tensor(act_lo[:, 2 * b - 2:2 * b, :].rearrange("p k t -> p (k t)"),
                                        turned[:, (b - 1) % 2, :],
                                        act_hi[:, 2 * b - 2:2 * b, :].rearrange("p k t -> p (k t)").bitcast(F32),
                                        ALU.subtract).then_inc(turn_done, 1)

            def mod_columns(layer, gain):
                dve.wait_ge(ev(f"cols{layer}_read"), 1)
                link(V.tensor_copy(shift, rest[0][:, 0:16]))
                link(V.scalar_tensor_tensor(out=scale1, in0=rest[0][:, 16:32], scalar=1.0, in1=gain,
                                            op0=ALU.add, op1=ALU.mult))

            dve.wait_ge(ev("vecT"), 1)
            V.tensor_copy(vec[:, 0:122], rest[0][:, 0:122]).then_inc(ev("vec"), 1)
            dve.wait_ge(ev("vec"), 1)
            link(V.tensor_scalar(qgs, qg, HD ** -0.5, None, ALU.mult))
            link(V.tensor_copy(pos, pos_i[:, :]))
            ang, red, turns_n, tmp = (rope_a[:, i, :, :] for i in range(4))
            for tb in range(TB):
                link(V.tensor_scalar(ang[:, tb, :], freq, pos[:, tb:tb + 1], None, ALU.mult))
            link(V.tensor_scalar(turns_n, ang, 1.0 / TWO_PI, ROUND, ALU.mult, ALU.add))
            link(V.tensor_scalar(turns_n, turns_n, ROUND, None, ALU.subtract))
            for part in TWO_PI_PARTS:
                link(V.scalar_tensor_tensor(out=ang, in0=turns_n, scalar=-part, in1=ang, op0=ALU.mult, op1=ALU.add))
            link(V.tensor_scalar(ang, ang, PI_IN, -PI_IN, ALU.min, ALU.max))
            link(V.tensor_scalar(red, ang, np.pi / 2, None, ALU.add))
            link(V.tensor_scalar(tmp, red, np.pi, -TWO_PI, ALU.is_gt, ALU.mult))
            link(V.tensor_tensor(red, red, tmp, ALU.add))
            V.tensor_scalar(red, red, PI_IN, -PI_IN, ALU.min, ALU.max).then_inc(ev("angles"), 1)

            dve.wait_ge(ev("cond"), 1)
            dve.wait_ge(ev("acc0_start"), 16)
            for j in range(4):
                modulate(j, acc_cols(j), 0, 4)
            normalize("sq0", normed, "normed0")
            with dve.Fori(1, KT) as i:
                for j in range(4):
                    modulate(j, acc_cols(j), i, 4, i, 4)
            pos_s[0] = 64
            for _ in range(4):
                split(pos_s[0])
                pos_s[0] += 1
            mod_columns(0, norm0)
            turn_affine_of("h0", 0)
            dve.wait_ge(ev("row0_start"), 16)
            chunks("pool_v", 2, 2, mod=lambda c, m: (row_cols(m), c * 4 + m // 2, 3))
            dve.wait_ge(ev("acc1_start"), 16)
            chunks("pool_g", 2, 2, mod=lambda c, m: (acc_cols(m), c * 2 + m // 4, 6))
            turn_lo_of("pooled", 8, act_hi, act_lo)
            p = ph["grp"]
            for g in range(4):
                advance(p.w0 + 2 * g + 6)
                c = p.chunk0 + g
                dve.wait_ge(w_used, p.w0 + 2 * g + 2)
                for tb in range(TB):
                    ins = V.tensor_tensor(u_nat[:, tb, g * N:(g + 1) * N], acc[c % 2][tb],
                                          gate_nat[:, tb, g * N:(g + 1) * N], ALU.mult)
                ins.then_inc(pair_read[c % 2], 1)
            turn_lo_of("mixed", 8, act_hi, act_lo, pscale)
            dve.wait_ge(ev("gate0_row"), 4)
            chunks("pool_out", 2, 2, add_chunk(ph["pool_out"], True), lambda c, m: (acc_cols(m), c * 2 + m // 4 + 8, 6))
            all_read(ph["pool_out"])
            V.engine_nop().then_inc(ev("x1_done"), 1)
            mod_columns(1, norm1)
            normalize("sq1", normed, "normed1")
            turn_affine_of("h1", 1)
            dve.wait_ge(ev("row1_start"), 16)
            chunks("attn_qkv", 6, 2, mod=lambda c, m: (row_cols(m), c, 10))
            chunks("attn_gate", 2, 2, mod=lambda c, m: (row_cols(m), c + 12, 10))
            chunks("attn_qi", 1, 2)
            advance(ph["attn_out"].w0 + 4)

            dve.wait_ge(ev("rope"), 1)
            dve.wait_ge(ev("rest_read"), 1)
            dve.wait_ge(pair_read[0], (ph["attn_qi"].chunk0 + 2) // 2)
            dve.wait_ge(pair_read[1], (ph["attn_qi"].chunk0 + 2) // 2)

            def rotate(tb, col, heads, width, half, f0):
                y = proj1[:, tb, col:col + heads * width].rearrange("p (h w) -> p h w", h=heads)
                x1, x2 = y[:, :, 0:half], y[:, :, half:2 * half]
                cos = rope_c[:, tb, f0:f0 + half].unsqueeze(1).to_broadcast([P, heads, half])
                sin = rope_s[:, tb, f0:f0 + half].unsqueeze(1).to_broadcast([P, heads, half])
                t = [rope_t[:, k, 0:heads * half].rearrange("p (h w) -> p h w", h=heads) for k in range(4)]
                V.tensor_tensor(t[0], x1, cos, ALU.mult)
                V.tensor_tensor(t[1], x2, sin, ALU.mult)
                V.tensor_tensor(t[2], x2, cos, ALU.mult)
                link(V.tensor_tensor(t[3], x1, sin, ALU.mult))
                V.tensor_tensor(x1, t[0], t[1], ALU.subtract)
                link(V.tensor_tensor(x2, t[2], t[3], ALU.add))

            for tb in range(TB):
                rotate(tb, QI, IH + 1, ID, IROT // 2, ROT // 2)
            for k in range(2):
                V.tensor_copy(ki_twice[:, :, k * ID:(k + 1) * ID], proj1[:, :, KI:KI + ID])
            link(V.tensor_scalar(proj1[:, :, WI:WI + IH], proj1[:, :, WI:WI + IH], (IH * ID) ** -0.5, None, ALU.mult))
            V.tensor_copy(work[:, :], hidden).then_inc(ev("index_in"), 1)
            for tb in range(TB):
                rotate(tb, Q1, 2 * HEADS, HD, ROT // 2, 0)
            V.engine_nop().then_inc(ev("qk_in"), 1)
            turn_half_of("qi", 4, lambda b: qiT[:, 2 * b + 1, :])
            dve.wait_ge(turn_hi, turns["ki"] + 1)
            V.engine_nop().then_inc(turn_done, 1)
            for h in range(IH):
                dve.wait_ge(i_relu, h + 1)
                wait(dve, i_done, h)
                for tb, (c0, c1) in enumerate(((0, P), (P, 384))):
                    ins = V.scalar_tensor_tensor(out=work[:, c0:c1], in0=relu[:, h % 2, c0:c1],
                                                 scalar=proj1[:, tb, WI + h:WI + h + 1], in1=work[:, c0:c1],
                                                 op0=ALU.mult, op1=ALU.add)
                ins.then_inc(i_done, 1)
            dve.wait_ge(i_done, IH)
            turn_half_of("qk1", 16, lambda b: (qT if b % 2 == 0 else kT)[:, b // 2 * 2 + 1, :])
            for tb, (c0, c1) in enumerate(((0, P), (P, 384))):
                for _ in range(TOPK // 8):
                    link(V.max(out=best, in_=work[:, c0:c1]))
                    link(V.match_replace(out=work[:, c0:c1], in_to_replace=best, in_values=work[:, c0:c1],
                                         imm_value=TAKEN))
            link(V.tensor_scalar(amask[:, :], work[:, :], TAKEN, -LOW, ALU.is_equal, ALU.mult))
            link(V.scalar_tensor_tensor(out=amask[:, :], in0=amask[:, :], scalar=LOW, in1=hidden,
                                        op0=ALU.add, op1=ALU.min))

            def attend(t, par, s1, s2, s3):
                if s1:
                    dve.wait_ge(s_full, t + 1)
                    wait(dve, p_ready, t - 1)
                    V.scalar_tensor_tensor(out=logit[:, par, :], in0=rest[par][:, 0:384], scalar=HD ** -0.5,
                                           in1=amask[:, :], op0=ALU.mult, op1=ALU.add).then_inc(s_read, 1)
                    dve.wait_ge(s_read, t + 1)
                    for tb, (c0, c1) in enumerate(((0, P), (P, 384))):
                        V.tensor_reduce(top[:, 2 * par + tb:2 * par + tb + 1], logit[:, par, c0:c1], AX_X,
                                        ALU.max).then_inc(l_max, 1)
                    dve.wait_ge(l_max, t * 2 + 2)
                    V.tensor_scalar(ntop[:, 2 * par:2 * par + 2], top[:, 2 * par:2 * par + 2], -1.0, None,
                                    ALU.mult).then_inc(l_ready, 1)
                if s3:
                    dve.wait_ge(o_full, t - 1)
                    V.reciprocal(rden[:, 2 * par:2 * par + 2], den[:, 2 * par:2 * par + 2]).then_inc(r_ready, 1)
                    dve.wait_ge(r_ready, t - 1)
                    for tb in range(TB):
                        ins = V.scalar_tensor_tensor(
                            out=proj1[:, tb, bass.ds(t * P - 2 * P, P)], in0=ps[:, 2 * par, tb * P:(tb + 1) * P],
                            scalar=rden[:, 2 * par + tb:2 * par + tb + 1],
                            in1=proj1[:, tb, bass.ds(t * P + (G1 - 2 * P), P)], op0=ALU.mult, op1=ALU.mult)
                    ins.then_inc(o_done, 1)
            skewed(dve, HEADS, attend)
            turn_lo_of("o1", 8, act_hi, act_lo)
            dve.wait_ge(ev("gate1_row"), 4)
            chunks("attn_out", 2, 2, add_chunk(ph["attn_out"], True))
            all_read(ph["attn_out"])
            V.engine_nop().then_inc(ev("x2_done"), 1)
            dve.wait_ge(ev("sq2"), 1)
            rsqrt(sumsq, rstd, 1.0 / D)
            dve.wait_ge(ev("final_row"), 16)
            for tb in range(TB):
                V.scalar_tensor_tensor(out=x[:, tb, :], in0=x[:, tb, :], scalar=rstd[:, tb:tb + 1], in1=row[:, :],
                                       op0=ALU.mult, op1=ALU.mult).then_inc(ev("x3_half"), 1)
            dve.wait_ge(ev("x3_half"), 2)
            V.engine_nop().then_inc(ev("x3_done"), 1)
            normalize("sq3", normed2, "normed3")
            turn_lo_of("h2", 8, act_hi, act_lo, anorm)
            chunks("in_uv", 2, 2)
            chunks("in_qkv", 3, 2)
            chunks("in_gates", 4, 2)
            V.engine_nop().then_inc(ev("tmp_free"), 1)
            for tb in range(TB):
                y = proj2[:, tb, S2:V2].rearrange("p (g c) -> p g c", c=P)
                dve.wait_ge(ev("squares"), tb + 1)
                s, r = ssq2[:, 24 * tb:24 * tb + 24], rs2[:, 24 * tb:24 * tb + 24]
                V.tensor_reduce(s, squares[:, :].rearrange("p (g c) -> p g c", c=P), AX_X, ALU.add).then_inc(
                    ev("squares_sum"), 1)
                dve.wait_ge(ev("squares_sum"), tb + 1)
                rsqrt(s, r, 1.0 / P)
                link(V.tensor_tensor(y, y, r.unsqueeze(2).to_broadcast([P, 24, P]), ALU.mult))
            dve.wait_ge(ev("sgu_row"), 16)
            for tb in range(TB):
                V.tensor_tensor(proj2[:, tb, S2:Q2], proj2[:, tb, S2:Q2], sgu_row[:, :], ALU.mult).then_inc(
                    ev("sgu_in"), 1)
            for n in range(4):
                dve.wait_ge(ev("sgu_full"), n + 1)
                tb, g0 = n // 2, n % 2 * 4
                for g in range(g0, g0 + 4):
                    u = proj2[:, tb, g * P:(g + 1) * P]
                    ins = V.scalar_tensor_tensor(out=u, in0=rest[n % 2][:, (g - g0) * P:(g - g0 + 1) * P],
                                                 scalar=bs[:, g:g + 1], in1=u, op0=ALU.add, op1=ALU.mult)
                ins.then_inc(ev("sgu_read"), 1)
            turn_half_of("qk2", 8, lambda b: (q2T if b < 4 else k2T)[:, b % 4 * 2 + 1, :],
                         scale=lambda b: qgs if b < 4 else kg)

            def stick(t, par, s1, s2, s3):
                if s2:
                    dve.wait_ge(b_tail, t)
                    V.tensor_tensor(sb_hit[:, 1 - par, :], turn[1 - par][:, 0:384], sb_hit[:, 1 - par, :],
                                    ALU.add).then_inc(b_arg, 1)
                if s1:
                    dve.wait_ge(b_log, t + 1)
                    wait(dve, b_tail, t - 1)
                    wait(dve, b_w, t - 1)
                    V.scalar_tensor_tensor(out=sb_miss[:, par, :], in0=rest[par][:, 0:384], scalar=0.0,
                                           in1=sb_log[:, par, :], op0=ALU.max, op1=ALU.add).then_inc(b_sum, 1)
                    V.scalar_tensor_tensor(out=sb_hit[:, par, :], in0=rest[par][:, 0:384], scalar=0.0,
                                           in1=sb_log[:, par, :], op0=ALU.min, op1=ALU.subtract).then_inc(z_read, 1)
                    dve.wait_ge(b_sum, t + 1)
                    V.tensor_tensor(sb_miss[:, par, :], sb_miss[:, par, :], nstrict, ALU.mult).then_inc(b_miss, 1)
                if s2:
                    dve.wait_ge(b_w, t)
                    V.tensor_tensor(sb_w[:, 1 - par, :], sb_w[:, 1 - par, :], strict, ALU.mult).then_inc(b_mask, 1)
            skewed(dve, SBH, stick)
            turn_lo_of("y2", 8, act_hi, act_lo)
            p = ph["up"]

            def merge(i, q):
                dve.wait_ge(w_used, p.w0 + 4 * q + 4 + i * 8)
                for tb in range(TB):
                    g = proj2[:, tb, bass.ds(i * N + (GA, GB)[q], N)]
                    ins = V.tensor_tensor(g, acc[q][tb], g, ALU.mult)
                    if q == 1:
                        ins.then_inc(ev("up_gated"), 1)
                        dve.wait_ge(ev("up_gated"), tb + 1 + i * 2)
                        dve.wait_ge(pair_read[0], p.chunk0 // 2 + 1 + i)
                        ga = proj2[:, tb, bass.ds(i * N + GA, N)]
                        ins = V.tensor_tensor(ga, ga, g, ALU.add)
                ins.then_inc(pair_read[q], 1)
            chunks("up", 4, 2, merge)
            turn_lo_of("merged", 8, act_hi, act_lo)
            chunks("w_o", 2, 2, add_chunk(ph["w_o"], False))
            all_read(ph["w_o"])
            V.engine_nop().then_inc(ev("x4_done"), 1)
            normalize("sq4", normed2, "normed4")
            turn_lo_of("h3", 8, act_hi, act_lo, fnorm)
            p = ph["ffn_in"]

            def hid_lo_of(j):
                for b in range(2):
                    g = turns["hid"] + b
                    dve.wait_ge(turn_hi, g + 1 + j * 2)
                    kts = bass.ds(j * 4 + 2 * b, 2)
                    V.tensor_tensor(hid_lo[:, kts, :].rearrange("p k t -> p (k t)"), turn[g % 2],
                                    hid_hi[:, kts, :].rearrange("p k t -> p (k t)").bitcast(F32),
                                    ALU.subtract).then_inc(turn_done, 1)

            def ffn_in(j, first):
                for q in range(2):
                    for k in range(8):
                        split(p.slot0 + 4 + q * 8 + k, j, 16, 16)
                    if q == 0 and not first:
                        hid_lo_of(j - 1)
                    if q == 1:
                        dve.wait_ge(w_used, p.w0 + 16 + j * 16)
                        dve.wait_ge(gate_ready, j + 1)
                        for tb in range(TB):
                            ins = V.tensor_tensor(hid[:, tb, :], acc[1][tb], hid[:, tb, :], ALU.mult)
                        ins.then_inc(hid_ready, 1)
            ffn_in(0, True)
            with dve.Fori(1, 11) as j:
                ffn_in(j, False)
            hid_lo_of(10)
            pos_s[0] += 22 * 8
            p = ph["ffn_out"]

            def ffn_out(i):
                for j in range(4):
                    split(p.slot0 + 4 + j, i, 4, 4)
            repeat(dve, 22, ffn_out)
            pos_s[0] += 88
            dve.wait_ge(w_used, p.w0 + 88)
            for tb in range(TB):
                for n in range(4):
                    cols = slice(n * N, (n + 1) * N)
                    ins = V.tensor_tensor(x[:, tb, cols], ps[:, 4 * tb + n], x[:, tb, cols], ALU.add)
            ins.then_inc(ev("x5_done"), 1)
            dve.wait_ge(ev("x5_done"), 1)
            normalize("sq5", normed2, "normed5")
            turn_lo_of("h4", 8, act_hi, act_lo, pnorm)
            turn_lo_of("p", 1, pT_hi, pT_lo)
            p = ph["ple_in"]
            for c in range(4):
                advance(p.w0 + 9 * c + 9 + 4)
                dve.wait_ge(w_used, p.w0 + 9 * c + 9)
                dve.wait_ge(pair_read[0], pairs_before + c + 1)
                cols = slice(c * N, (c + 1) * N)
                for tb in range(TB):
                    ins = V.tensor_tensor(ple[:, tb, :], acc[1][tb], ple[:, tb, :], ALU.mult)
                ins.then_inc(pair_read[1], 1)
                dve.wait_ge(pair_read[1], pairs_before + c + 1)
                for tb in range(TB):
                    ins = V.tensor_tensor(x[:, tb, cols], x[:, tb, cols], ple[:, tb, :], ALU.add)
                ins.then_inc(ev("x_final"), 1)

        @block.tensor
        def _(pe):
            M = nc.tensor.matmul

            def three(dst, hi_t, lo_t, w, cols, first, last):
                wh, wl = w_hi[:, w, cols], w_lo[:, w, cols]
                M(dst, hi_t, wh, start=first, stop=False)
                M(dst, hi_t, wl, start=False, stop=False)
                return M(dst, lo_t, wh, start=False, stop=last)

            def chunk(p, q, i, per, kts, turned_at):
                c = p.chunk0 + q
                wait(pe, pair_read[c % 2], c // 2 + i * (per // 2))
                js = p.w_at
                for n in range(len(kts) // 2):
                    pe.wait_ge(slot_done, p.slot0 + q * p.per + js[n] + 1 + i * (per * p.per))
                    w0 = p.w0 + q * p.ws + n
                    for k in range(2):
                        kt = kts[2 * n + k]
                        if kt % 2 == 0:
                            pe.wait_ge(turn_done, turned_at + kt // 2 + 1)
                        for tb in range(TB):
                            t = slice(tb * P, (tb + 1) * P)
                            ins = three(acc[c % 2][tb], act_hi[:, kt, t], act_lo[:, kt, t], w0 % SPLIT,
                                        slice(k * N, (k + 1) * N), n == 0 and k == 0,
                                        n == len(kts) // 2 - 1 and k == 1)
                            if k == 1 and tb == 1:
                                ins.then_inc(w_used, 1)

            def chunks(name, bodies, per, turned, kts=range(KT)):
                p = ph[name]

                def body(i):
                    for q in range(per):
                        chunk(p, q, i, per, kts, turns[turned])
                repeat(pe, bodies, body)

            def turn_bank(g, tiles, i=0, ni=0):
                wait(pe, turn_done, g - 1 + i * ni)
                for n, tile in enumerate(tiles):
                    ins = nc.tensor.transpose(turn[g % 2][:, n * P:(n + 1) * P], tile, ident)
                ins.then_inc(turn_full, 1)

            def turn_all(name, src, kt0=0, kts=KT, waits=None):
                for b in range(kts // 2):
                    if waits:
                        waits(b)
                    turn_bank(turns[name] + b, [src(tb, 2 * b + k) for k in range(2) for tb in range(TB)])

            def columns_of(name, layer):
                for j in range(32):
                    ins = M(rest[0][:, j:j + 1], mod_acc[:, j * P:(j + 1) * P], ones[:, 0:1], start=True, stop=True)
                ins.then_inc(ev(name), 1)

            def gate_row(name, after):
                pe.wait_ge(slot_done, after)
                for c in range(4):
                    wait(pe, ev(name + "_row"), c - 1)
                    M(rest[c % 2], ones, mod_row[:, c * N:(c + 1) * N], start=True, stop=True).then_inc(
                        ev(name + "_full"), 1)

            tile = lambda buf: (lambda tb, kt: buf[:, tb, kt * P:(kt + 1) * P])

            pe.wait_ge(ev("const_in"), 16)
            pe.wait_ge(ev("vec_in"), 16 * (len(vec_sources) + 1))
            nc.tensor.transpose(rest[0][:, 0:122], vec_rows[0:122, :], ident[0:122, 0:122]).then_inc(ev("vecT"), 1)
            pe.wait_ge(ev("vec"), 1)
            pe.wait_ge(slot_done, 64)
            columns_of("cols0_read", 0)
            pe.wait_ge(ev("normed0"), 2)
            turn_all("h0", tile(normed))
            chunks("pool_v", 2, 2, "h0")
            chunks("pool_g", 2, 2, "h0")
            gate_row("gate0", ph["pool_g"].slot0)
            pe.wait_ge(ev("mix_in"), 16)
            for q in range(2):
                pe.wait_ge(pair_read[q], (ph["pool_g"].chunk0 + 4) // 2)
            for b in range(8):
                g = turns["pooled"] + b
                wait(pe, turn_done, g - 1)
                for k in range(2):
                    ct = 2 * b + k
                    c = slice(ct * P, (ct + 1) * P)
                    M(turn[g % 2][:, k * T:(k + 1) * T], v_nat[:, 0, c], pool_mix[:, 0, ct // 4, :], start=True, stop=False)
                    ins = M(turn[g % 2][:, k * T + P:(k + 1) * T], v_nat[:, 1, c], pool_mix[:, 1, ct // 4, P:T],
                            start=False, stop=True)
                ins.then_inc(turn_full, 1)
            for g in range(4):
                chunk(ph["grp"], g, 0, 4, range(4 * g, 4 * g + 4), turns["pooled"])
            for q in range(2):
                pe.wait_ge(pair_read[q], (ph["grp"].chunk0 + 4) // 2)
            turn_all("mixed", tile(u_nat))
            chunks("pool_out", 2, 2, "mixed")
            pe.wait_ge(slot_done, ph["attn_qkv"].slot0)
            columns_of("cols1_read", 1)
            pe.wait_ge(ev("normed1"), 2)
            turn_all("h1", tile(normed))
            chunks("attn_qkv", 6, 2, "h1")
            chunks("attn_gate", 2, 2, "h1")
            chunks("attn_qi", 1, 2, "h1")
            p = ph["attn_rest"]
            w80 = PROJ1 - KI
            for j in range(2):
                pe.wait_ge(slot_done, p.slot0 + j + 1)
                for tb in range(TB):
                    for k in range(8):
                        kt, t = 8 * j + k, slice(tb * P, (tb + 1) * P)
                        ins = three(rest[tb][:, 0:w80], act_hi[:, kt, t], act_lo[:, kt, t], (p.w0 + j) % SPLIT,
                                    slice(k * w80, (k + 1) * w80), kt == 0, kt == KT - 1)
                ins.then_inc(w_used, 1)
            pe.wait_ge(ev("rest_read"), 1)
            gate_row("gate1", ph["attn_rest"].slot0)
            pe.wait_ge(ev("index_in"), 1)
            turn_all("qi", lambda tb, kt: proj1[:, tb, QI + kt * P:QI + (kt + 1) * P], kts=8)
            turn_bank(turns["ki"], [ki_twice[:, tb, :] for tb in range(TB)])
            pe.wait_ge(turn_done, turns["ki"] + 1)
            pe.wait_ge(ev("gate1_row"), 4)
            for h in range(IH):
                wait(pe, i_relu, h - 1)
                r = slice(h % 2 * ID, (h % 2 + 1) * ID)
                M(rest[h % 2][:, 0:P], qiT[r, h // 2, 0:P], kiT[r, 0:P], start=True, stop=True)
                M(rest[h % 2][:, P:384], qiT[r, h // 2, P:T], kiT[r, :], start=True, stop=True).then_inc(i_full, 1)
            pe.wait_ge(ev("qk_in"), 1)
            pe.wait_ge(i_relu, IH)
            for b in range(16):
                col = (Q1, K1)[b % 2] + b // 2 * T
                turn_bank(turns["qk1"] + b, [proj1[:, tb, col + k * P:col + (k + 1) * P]
                                             for k in range(2) for tb in range(TB)])
            pe.wait_ge(turn_done, turns["qk1"] + 16)

            def attend(t, par, s1, s2, s3):
                if s1:
                    pe.wait_ge(q_copied, t + 1)
                    wait(pe, s_read, t - 1)
                    q = head_in[:, par, :]
                    k = kT[:, bass.ds(t, 1), :].rearrange("p a t -> p (a t)")
                    M(rest[par][:, 0:P], q[:, 0:P], k[:, 0:P], start=True, stop=True)
                    M(rest[par][:, P:384], q[:, P:T], k, start=True, stop=True).then_inc(s_full, 1)
                if s2:
                    pe.wait_ge(p_ready, t)
                    wait(pe, pt_ready, t - 2)
                    for n in range(3):
                        ins = nc.tensor.transpose(turn[1 - par][:, n * P:(n + 1) * P],
                                                  prob[:, 1 - par, n * P:(n + 1) * P], ident)
                    ins.then_inc(pt_full, 1)
                if s3:
                    pe.wait_ge(pt_ready, t - 1)
                    wait(pe, o_done, t - 3)
                    v = [proj1[:, tb, bass.ds(t * P + (V1 - 2 * P), P)] for tb in range(TB)]
                    o = ps[:, 2 * par, :]
                    M(o[:, 0:P], probT[:, par, 0:P], v[0], start=True, stop=True)
                    M(o[:, P:T], probT[:, par, P:2 * P], v[0], start=True, stop=False)
                    M(o[:, P:T], probT[:, par, 2 * P:384], v[1], start=False, stop=True).then_inc(o_full, 1)
            skewed(pe, HEADS, attend)
            pe.wait_ge(o_done, HEADS)
            turn_all("o1", tile(proj1))
            chunks("attn_out", 2, 2, "o1")
            pe.wait_ge(ev("normed3"), 2)
            turn_all("h2", tile(normed2))
            chunks("in_uv", 2, 2, "h2")
            chunks("in_qkv", 3, 2, "h2")
            chunks("in_gates", 4, 2, "h2")
            pe.wait_ge(ev("w_s_low"), 1)
            for b in range(2):
                for g in range(4):
                    ins = nc.tensor.transpose(rest[b][:, g * P:(g + 1) * P], w_s[:, 4 * b + g, :], ident)
                ins.then_inc(ev("ws_turned"), 1)
            pe.wait_ge(ev("w_sT"), 2)
            pe.wait_ge(ev("sgu_in"), 2)
            for n in range(4):
                wait(pe, ev("sgu_read"), n - 1)
                tb, g0 = n // 2, n % 2 * 4
                for g in range(g0, g0 + 4):
                    ins = M(rest[n % 2][:, (g - g0) * P:(g - g0 + 1) * P], w_sT[:, g, :],
                            proj2[:, tb, S2 + g * P:S2 + (g + 1) * P], start=True, stop=True)
                ins.then_inc(ev("sgu_full"), 1)
            for b in range(8):
                col = (Q2, K2)[b // 4] + b % 4 * T
                turn_bank(turns["qk2"] + b, [proj2[:, tb, col + k * P:col + (k + 1) * P]
                                             for k in range(2) for tb in range(TB)])
            pe.wait_ge(turn_done, turns["qk2"] + 8)
            pe.wait_ge(ev("sgu_read"), 4)

            def stick(t, par, s1, s2, s3):
                if s1:
                    pe.wait_ge(k_copied, t + 1)
                    wait(pe, z_read, t - 1)
                    q = q2T[:, bass.ds(t, 1), :].rearrange("p a t -> p (a t)")
                    k = head_in[:, par, :]
                    M(rest[par][:, 0:T], k[:, 0:P], q, start=True, stop=True)
                    M(rest[par][:, T:384], k[:, P:T], q[:, P:T], start=True, stop=True).then_inc(z_full, 1)
                if s2:
                    pe.wait_ge(b_miss, t)
                    wait(pe, b_arg, t - 2)
                    miss, tail = sb_miss[:, 1 - par, :], turn[1 - par]
                    M(tail[:, 0:T], later, miss[:, 0:T], start=True, stop=False)
                    M(tail[:, P:T], ones, miss[:, T:384], start=False, stop=True)
                    M(tail[:, T:384], later, miss[:, T:384], start=True, stop=True).then_inc(b_tail, 1)
                if s3:
                    pe.wait_ge(b_mask, t - 1)
                    wait(pe, y_done, t - 3)
                    v = [proj2[:, tb, bass.ds(t * P + (V2 - 2 * P), P)] for tb in range(TB)]
                    y, w = ps[:, 2 * par, :], sb_w[:, par, :]
                    M(y[:, 0:P], w[:, 0:P], v[0], start=True, stop=True)
                    M(y[:, P:T], w[:, P:T], v[0], start=True, stop=False)
                    M(y[:, P:T], w[:, T:384], v[1], start=False, stop=True).then_inc(y_full, 1)
            skewed(pe, SBH, stick)
            pe.wait_ge(y_done, SBH)
            turn_all("y2", lambda tb, kt: proj2[:, tb, (kt * P if kt < 8 else Q2 + kt * P - 1024):][:, 0:P])
            p = ph["up"]

            def up(i):
                chunk(p, 0, i, 2, range(8), turns["y2"])
                chunk(p, 1, i, 2, range(8, 16), turns["y2"])
            repeat(pe, 4, up)
            for q in range(2):
                pe.wait_ge(pair_read[q], (p.chunk0 + 8) // 2)
            turn_all("merged", lambda tb, kt: proj2[:, tb, GA + kt * P:GA + (kt + 1) * P])
            chunks("w_o", 2, 2, "merged")
            pe.wait_ge(ev("normed4"), 2)
            turn_all("h3", tile(normed2))
            p = ph["ffn_in"]

            def turn_hid(j):
                pe.wait_ge(hid_ready, j + 1)
                for b in range(2):
                    turn_bank(turns["hid"] + b, [hid[:, tb, (2 * b + k) * P:(2 * b + k + 1) * P]
                                                 for k in range(2) for tb in range(TB)], j, 2)

            def ffn_in(j, first):
                for q in range(2):
                    if not first:
                        pe.wait_ge((gate_ready, hid_ready)[q], j)
                    ffn_chunk(j, q)
                    if q == 0 and not first:
                        turn_hid(j - 1)

            def ffn_chunk(j, q):
                for n in range(8):
                    pe.wait_ge(slot_done, p.slot0 + q * 8 + n + 1 + j * 16)
                    for k in range(2):
                        kt = 2 * n + k
                        if k == 0:
                            pe.wait_ge(turn_done, turns["h3"] + n + 1)
                        for tb in range(TB):
                            t = slice(tb * P, (tb + 1) * P)
                            ins = three(acc[q][tb], act_hi[:, kt, t], act_lo[:, kt, t], (p.w0 + n) % SPLIT,
                                        slice(k * N, (k + 1) * N), kt == 0, kt == KT - 1)
                    ins.then_inc(w_used, 1)

            for q in range(2):
                pe.wait_ge(pair_read[q], p.chunk0 // 2)
            ffn_in(0, True)
            with pe.Fori(1, 11) as j:
                ffn_in(j, False)
            turn_hid(10)
            p = ph["ffn_out"]
            pe.wait_ge(turn_done, turns["h4"])

            def ffn_out(i, first, last):
                for q in range(2):
                    pe.wait_ge(hid_copied, i * 2 + (q + 1))
                    for j in range(2):
                        pe.wait_ge(slot_done, p.slot0 + 2 * q + j + 1 + i * 4)
                        w0 = p.w0 + 2 * q + j
                        for tb in range(TB):
                            hi, lo = (hid_at[:, q, k, tb * P:(tb + 1) * P] for k in range(2))
                            for n in range(2):
                                ins = three(ps[:, 4 * tb + 2 * j + n], hi, lo, w0 % SPLIT,
                                            slice(n * N, (n + 1) * N), first and q == 0, last and q == 1)
                        ins.then_inc(w_used, 1)
            ffn_out(0, True, False)
            with pe.Fori(1, HKT // 2 - 1) as i:
                ffn_out(i, False, False)
            ffn_out(HKT // 2 - 1, False, True)
            pe.wait_ge(ev("normed5"), 2)
            turn_all("h4", tile(normed2))
            pe.wait_ge(ev("p_in"), 16)
            turn_bank(turns["p"], [p_nat[:, tb, k * P:(k + 1) * P] for k in range(2) for tb in range(TB)])
            p = ph["ple_in"]
            for c in range(4):
                for q in range(2):
                    pe.wait_ge(pair_read[q], pairs_before + c)
                    for n in range(8 if q == 0 else 1):
                        s = 9 * c + (n if q == 0 else 8)
                        pe.wait_ge(slot_done, p.slot0 + s + 1)
                        for k in range(2):
                            kt = 2 * n + k
                            if k == 0:
                                pe.wait_ge(turn_done, (turns["h4"] + n + 1) if q == 0 else turns["p"] + 1)
                            hi, lo = (act_hi, act_lo) if q == 0 else (pT_hi, pT_lo)
                            for tb in range(TB):
                                t = slice(tb * P, (tb + 1) * P)
                                ins = three(acc[q][tb], hi[:, kt, t], lo[:, kt, t], (p.w0 + s) % SPLIT,
                                            slice(k * N, (k + 1) * N), kt == 0, kt == (KT - 1 if q == 0 else 1))
                        ins.then_inc(w_used, 1)



_INS = ["x", "c", "positions", "norm_g", "mod_w", "mod_b", "pool_w_in", "pool_w_grp", "pool_scale", "pool_w_out",
        "attn_w_in", "attn_w_out", "final_g", "p_2", "attn_norm_g_2", "w_in_2", "sgu_norm_g_2", "w_s_2", "b_s_2",
        "q_norm_g_2", "k_norm_g_2", "w_up_a_2", "w_up_b_2", "w_o_2", "ffn_norm_g_2", "w_ffn_in_2",
        "w_ffn_out_2", "ple_norm_g_2", "w_ple_gate_2", "w_ple_2"]


def tables():
    r, c = np.arange(P)[:, None], np.arange(P)[None, :]
    zero, one = np.zeros((P, P)), np.ones((P, P))
    low = np.where(c <= r, 0.0, LOW)
    before = (r < c) * 1.0
    hidden = np.concatenate([low, zero, low], 1)
    strict = np.concatenate([before, one, before], 1)
    theta = 500000.0
    freq = np.concatenate([np.float32(theta) ** (-np.arange(rot // 2, dtype=np.float32) * 2.0 / rot)
                           for rot in (ROT, IROT)])
    const = np.concatenate([np.eye(P), one, (r > c) * 1.0, hidden, strict, -strict,
                            np.broadcast_to(freq, (P, HALVES))], 1).astype(np.float32)
    s, t = np.arange(T)[:, None], np.arange(T)[None, :]
    mix = [((s <= t) & (s > t - w)) / np.minimum(t + 1, w) - (s == t) for w in (2, 4, 8, 16)]
    mix = np.stack(mix).astype(np.float32).reshape(4, TB, P, T).transpose(2, 1, 0, 3)
    return np.ascontiguousarray(const), np.ascontiguousarray(mix)


def kernel(**inputs):
    import concourse.bacc as _bacc
    from concourse.bass_utils import run_bass_kernel_spmd as _run

    nc = _bacc.Bacc("TRN2", target_bir_lowering=False, num_devices=1)
    arrays, args = {}, []
    const, mix = tables()
    for name, a in [(n, inputs[n]) for n in _INS] + [("const", const), ("pool_mix", mix)]:
        a = np.ascontiguousarray(a)
        arrays[f"in_{name}"] = a
        args.append(nc.dram_tensor(f"in_{name}", a.shape, mybir.dt.from_np(a.dtype), kind="ExternalInput").ap())
    out = nc.dram_tensor("out_0", (1, T, D), F32, kind="ExternalOutput").ap()
    build(nc, *args, out)
    r = _run(nc, [arrays], core_ids=[0])
    return r.results[0]["out_0"]
```

```python
import numpy as np

import concourse.bass as bass
from concourse import mybir

F32 = mybir.dt.float32
F32R = mybir.dt.float32r
I32 = mybir.dt.int32
ALU = mybir.AluOpType
ACT = mybir.ActivationFunctionType
AX_X = mybir.AxisListType.X

P = 128
T = 256
TB = T // P
D = 2048
KT = D // P
N = 512
SLOT = 1024
RAW = 4
SPLIT = 4
EPS = 1e-6
HEADS, HD = 16, 128
IH, ID = 16, 64
ROT, IROT = HD // 4, ID // 4
HALVES = ROT // 2 + IROT // 2
TOPK = 64
SBH = 8
SGU = 8
HID = 5632
HKT = HID // P
LOW = -3.0e38
TAKEN = -3.4e38
X5_ORDER = ((0, 0), (1, 0), (1, 1), (0, 1), (0, 2), (1, 2), (0, 3), (1, 3))
TWO_PI = 2 * np.pi
PI_IN = 3.1415925
TWO_PI_PARTS = (6.28125, 1.93500518798828125e-3, 3.019915981e-7)
ROUND = 1.5 * 2.0 ** 23

Q1, K1, V1, G1, QI, KI, WI, PROJ1 = 0, 2048, 4096, 6144, 8192, 9216, 9280, 9296
U2, S2, Q2, K2, V2, GA, GB, PROJ2 = 0, 1024, 2048, 3072, 4096, 5120, 7168, 9216

PHASES = [
    ("mod0", 16, "MMMM"),
    ("pool_v", 4, "WWWWWMMWMMWMMWMM"),
    ("pool_g", 4, "WWWWWMMWMMWMMWMM"),
    ("grp", 4, "WW"),
    ("pool_out", 4, "WWWWWMMWMMWMMWMM"),
    ("attn_idx", 2, "WWWWWMMWMMWMMWMM"),
    ("attn_rest", 1, "WW"),
    ("attn_v", 4, "WWWWWMWMWMWM"),
    ("attn_qk", 8, "WWWWWWWW"),
    ("attn_gate", 4, "WWWWWWWW"),
    ("attn_out", 4, "WWWWWWWW"),
    ("in_uv", 4, "WWWWWWWW"),
    ("in_qkv", 6, "WWWWWWWW"),
    ("in_gates", 8, "WWWWWWWW"),
    ("up", 8, "WWWW"),
    ("w_o", 4, "WWWWWWWW"),
    ("ffn_in", 22, "WWWWWWWW"),
    ("ffn_out", 44, "WW"),
    ("ple_in", 4, "WWWWWWWWW"),
]


class Phase:
    def __init__(self, name, chunks, seq, slot0, w0, chunk0):
        self.name, self.chunks, self.seq = name, chunks, seq
        self.slot0, self.w0, self.chunk0 = slot0, w0, chunk0
        self.per = len(seq)
        self.w_at = [j for j, k in enumerate(seq) if k == "W"]
        self.ws = len(self.w_at)


def plan():
    phases, slot, w, chunk = {}, 0, 0, 0
    for name, chunks, seq in PHASES:
        phases[name] = Phase(name, chunks, seq, slot, w, chunk)
        slot += chunks * len(seq)
        w += chunks * seq.count("W")
        if name == "ple_in":
            chunk += 2 * chunks
        elif name not in ("mod0", "attn_rest", "ffn_out"):
            chunk += chunks
    return phases


def build(nc, x_in, c, positions, norm_g, mod_w, mod_b, pool_w_in, pool_w_grp, pool_scale, pool_w_out,
          attn_w_in, attn_w_out, final_g, p_in, attn_norm_g, w_in, sgu_norm_g, w_s_in, b_s, q_norm_g,
          k_norm_g, w_up_a, w_up_b, w_o, ffn_norm_g, w_ffn_in, w_ffn_out, ple_norm_g, w_ple_gate, w_ple,
          const_in, pool_mix_in, out):
    ph = plan()
    kinds = "".join(seq * chunks for _, chunks, seq in PHASES)

    base = (nc.sbuf_base + 63) // 64 * 64
    K = 1024

    def at(name, kib, shape, dt=F32):
        return nc.alloc_sbuf_tensor_at(name, shape, dt, offset=base + int(kib * K))

    x = at("x", 0, [P, TB, D])
    raw = at("raw", 16, [P, RAW, SLOT])
    w_hi = at("w_hi", 32, [P, SPLIT, SLOT], F32R)
    w_lo = at("w_lo", 48, [P, SPLIT, SLOT], F32R)
    act_hi = at("act_hi", 64, [P, KT, T], F32R)
    act_lo = at("act_lo", 80, [P, KT, T], F32R)
    mod_row = at("mod_row", 96, [P, D])
    const = at("const", 104, [P, 3 * P + 3 * 384 + HALVES])
    vec_rows = at("vec_rows", 112, [P, P])
    vec = at("vec", 112.5, [P, P])
    small = at("small", 113, [P, 192])
    WORK = 114
    TMP = WORK + 73
    v_nat = at("v_nat", WORK, [P, TB, D])
    gate_nat = at("gate_nat", WORK + 16, [P, TB, D])
    u_nat = at("u_nat", WORK + 32, [P, TB, D])
    normed = at("normed", WORK + 32, [P, TB, D])
    pool_mix = at("pool_mix", WORK + 48, [P, TB, 4, T])
    mod_acc = at("mod_acc", WORK + 56, [P, 2 * D])
    turned = at("turned", TMP, [P, 2, 2 * T])
    resid = at("resid", TMP + 4, [P, TB, N])
    proj1 = at("proj1", WORK, [P, TB, PROJ1])
    qiT = at("qiT", TMP, [P, IH // 2, T])
    kiT = at("kiT", TMP + 8, [P, T])
    ki_twice = at("ki_twice", TMP + 9, [P, TB, P])
    relu = at("relu", TMP + 10, [P, 2, 384])
    rope_t = at("rope_t", TMP + 13.25, [P, 4, (IH + 1) * IROT // 2])
    rope_a = at("rope_a", TMP + 8, [P, 4, TB, HALVES])
    rope_s = at("rope_s", 110.5, [P, TB, HALVES])
    rope_c = at("rope_c", 110.75, [P, TB, HALVES])
    work = at("work", TMP + 15.5, [P, 384])
    amask = at("amask", TMP + 17, [P, 384])
    logit = at("logit", TMP, [P, 384])
    prob = at("prob", TMP + 1.5, [P, 384])
    probT = at("probT", TMP + 3, [P, 384])
    head_in = at("head_in", TMP + 4.5, [P, 2, TB, P])
    headT = at("headT", TMP + 6.5, [P, 2, T])
    row = at("row", WORK + 64, [P, D])
    o1_hi = at("o1_hi", WORK + 8, [P, KT, T], F32R)
    o1_lo = at("o1_lo", WORK + 44.3125, [P, KT, T], F32R)
    before_gain = at("before_gain", TMP + 8, [P, TB, N])
    junk = at("junk", TMP + 12, [P, TB, N])
    normed2 = at("normed2", WORK, [P, TB, D])
    proj2 = at("proj2", WORK, [P, TB, PROJ2])
    squares = at("squares", TMP, [P, 3072])
    sgu_row = at("sgu_row", TMP + 13, [P, 1024])
    w_s = at("w_s", 96, [P, SGU, P])
    w_sT = at("w_sT", 100, [P, SGU, P])
    sb_abs = at("sb_abs", TMP, [P, 384])
    sb_log = at("sb_log", TMP + 1.5, [P, 384])
    sb_miss = at("sb_miss", TMP + 3, [P, 384])
    head_in2 = at("head_in2", TMP + 4.5, [P, 2, TB, P])
    headT2 = at("headT2", TMP + 6.5, [P, 2, T])
    sb_hit = at("sb_hit", TMP + 8.5, [P, 2, 384])
    sb_w = at("sb_w", TMP + 11.5, [P, 384])
    merged_hi = at("merged_hi", WORK, [P, KT, T], F32R)
    merged_lo = at("merged_lo", WORK + 36, [P, KT, T], F32R)
    hid_hi = at("hid_hi", WORK, [P, HKT, T], F32R)
    hid_lo = at("hid_lo", WORK + 44, [P, HKT, T], F32R)
    hid = at("hid", WORK + 88, [P, TB, N])
    hid_at = at("hid_at", 96, [P, 2, 2, T], F32R)
    pT_hi = at("pT_hi", WORK + 32, [P, 2, T], F32R)
    pT_lo = at("pT_lo", WORK + 34, [P, 2, T], F32R)
    p_nat = at("p_nat", WORK + 36, [P, TB, T])
    ple = at("ple", WORK + 40, [P, TB, N])
    assert (WORK + 92) * K <= nc.sbuf_bytes_remaining

    ident, ones = const[:, 0:P], const[:, P:2 * P]
    later = const[:, 2 * P:3 * P]
    o = 3 * P
    hidden = const[:, o:o + 384]
    strict = const[:, o + 384:o + 768]
    nstrict = const[:, o + 768:o + 1152]
    freq = const[:, o + 1152:o + 1152 + HALVES]
    norm0, norm1, pscale, anorm, fnorm, pnorm, ccol = (vec[:, 16 * i:16 * i + 16] for i in range(7))
    qg, kg, bs = vec[:, 112:113], vec[:, 113:114], vec[:, 114:122]
    cond = small[:, 0:16]
    shift, scale1 = small[:, 16:32], small[:, 32:48]
    sumsq, rstd = small[:, 48:50], small[:, 50:52]
    pos = small[:, 52:54]
    rfinal, rnext, sumnext = small[:, 54:56], small[:, 70:72], small[:, 72:74]
    colsum = small[:, 96:112]
    best = small[:, 56:64]
    qgs = small[:, 80:81]
    top, ntop, rden = (small[:, 64 + 2 * i:66 + 2 * i] for i in range(3))
    den = small[:, 84:92]
    ssq2, rs2 = small[:, 96:144], small[:, 144:192]
    newton = at("newton", 111, [P, 2, 24])
    pos_i = at("pos_i", 113.875, [P, TB], I32)

    ps = nc.alloc_psum_tensor("ps", [P, 8, N], F32)
    acc = [[ps[:, 0], ps[:, 1]], [ps[:, 2], ps[:, 3]]]
    turn = [ps[:, 4], ps[:, 5]]
    rest = [ps[:, 6], ps[:, 7]]
    mixes = [turn[1], rest[1]]

    def sem(name):
        return nc.alloc_semaphore(name)

    loaded = [sem(f"loaded{i}") for i in range(RAW)]
    hi_ready = sem("hi_ready")
    slot_done = sem("slot_done")
    w_used = sem("w_used")
    pair_read = [sem("pair_read0"), sem("pair_read1")]
    turn_full = sem("turn_full")
    turn_affine = sem("turn_affine")
    turn_hi = sem("turn_hi")
    turn_done = sem("turn_done")
    rope_mul, rope_add = sem("rope_mul"), sem("rope_add")
    in_ready, qk_full, qk_ready = map(sem, ("in_ready", "qk_full", "qk_ready"))
    s_full, s_read, l_max, l_ready, p_ready = map(sem, ("s_full", "s_read", "l_max", "l_ready", "p_ready"))
    pt_full, pt_ready, o_full, r_ready, o_done = map(sem, ("pt_full", "pt_ready", "o_full", "r_ready", "o_done"))
    z_full, z_read, b_abs, b_log, b_sum, b_miss = map(sem, ("z_full", "z_read", "b_abs", "b_log", "b_sum", "b_miss"))
    b_tail, b_arg, b_w, b_mask, y_full, y_done = map(sem, ("b_tail", "b_arg", "b_w", "b_mask", "y_full", "y_done"))
    i_full, i_relu, i_done = map(sem, ("i_full", "i_relu", "i_done"))
    hid_copied = sem("hid_copied")
    in2_ready, qk2_full, qk2_ready = map(sem, ("in2_ready", "qk2_full", "qk2_ready"))
    gate_ready = sem("gate_ready")
    hid_ready = sem("hid_ready")
    act_chain, dve_chain = sem("act_chain"), sem("dve_chain")
    stored = sem("stored")
    events = {}

    def ev(name):
        if name not in events:
            events[name] = sem(name)
        return events[name]

    def wait(eng, s, value):
        if not (isinstance(value, int) and value <= 0):
            eng.wait_ge(s, value)

    def repeat(eng, n, body):
        if n == 1:
            body(0)
        elif n > 1:
            with eng.Fori(0, n) as i:
                body(i)

    def runs(t, heads=HEADS):
        return not isinstance(t, int) or 0 <= t < heads

    def at_heads(first, *steps):
        def hook(i, c, j):
            for where, step in steps:
                if j % 4 == where:
                    k = 2 * c + j // 4
                    step(i * 4 + (first + k), k % 4)
        return hook

    turns, n_turns = {}, 0
    for name, banks in (("h0", 8), ("pooled", 8), ("mixed", 8), ("h1", 8), ("qi", 4), ("ki", 1),
                        ("o1", 8), ("h2", 8), ("y2", 8), ("merged", 8), ("h3", 8), ("hid", 22),
                        ("h4", 8), ("p", 1)):
        turns[name] = n_turns
        n_turns += banks

    def behind(lead, step):
        def hook(i, c, j):
            if c == 0 and j + lead < 8:
                step(j + lead)
        return hook

    def hooks(*several):
        def hook(i, c, j):
            for h in several:
                h(i, c, j)
        return hook

    def streamed(offset, step, c0=0):
        def hook(i, c, j):
            if c > c0 and j - offset in (2, 4):
                step(2 * (c - 1) + (j - offset) // 4)
        return hook

    def last_two(offset, step):
        def hook(i, c, j):
            if c == 0 and j - offset in (2, 4):
                step(6 + (j - offset) // 4)
        return hook

    def columns_read(eng, p, c):
        eng.wait_ge(pair_read[c % 2], (p.chunk0 + c) // 2 + 1)

    def raw2(r, nk=2, cols=N):
        return raw[:, r, 0:nk * cols].rearrange("p (k n) -> p k n", k=nk)

    x_t = x_in.rearrange("b (t p) d -> p (b t) d", p=P)
    out_t = out.rearrange("b (t p) d -> p (b t) d", p=P)
    pairs_before = ph["ffn_in"].chunk0 // 2
    by_channel = lambda v: v.rearrange("l (k c) -> (l k) c", c=P)
    vec_sources = [by_channel(v) for v in (norm_g, pool_scale, attn_norm_g, ffn_norm_g, ple_norm_g, c, q_norm_g,
                                           k_norm_g)] + [b_s[0]]

    with nc.Block() as block:
        @block.sync
        def _(sp):
            def load(s0, n, i, src, shape=None):
                r = s0 % RAW
                wait(sp, slot_done, s0 - RAW + 1 + i * n)
                dst = raw[:, r, :] if shape is None else raw2(r, *shape)
                sp.dma_start(dst, src).then_inc(loaded[r], 16)

            def rows(w, k0, nk, col, cols):
                return w[bass.ds(k0 * P, nk * P), bass.ds(col, cols)].rearrange("(k p) n -> p k n", p=P)

            def product(name, w, bodies, per, col0=0, mod=None, col=lambda i, q, per: (i * per + q) * N):
                p = ph[name]

                def body(i):
                    for q in range(per):
                        k = m = 0
                        for j, kind in enumerate(p.seq):
                            s0 = p.slot0 + q * p.per + j
                            if kind == "W":
                                src = rows(w, k, 2, col(i, q, per) + col0, N)
                                load(s0, per * p.per, i, src, (2, N))
                                k += 2
                            else:
                                load(s0, per * p.per, i, mod(i * per + q, m))
                                m += 1
                repeat(sp, bodies, body)

            def mod_rows(layer, kt, col):
                return mod_w[layer, bass.ds(kt * P, P), bass.ds(col, SLOT)]

            def mod0(i):
                for j in range(4):
                    load(j, 4, i, mod_rows(0, i, j * SLOT))

            for j in range(4):
                load(j, 4, 0, mod_rows(0, 0, j * SLOT))
            with sp.Fori(1, KT) as i:
                mod0(i)
            product("pool_v", pool_w_in[0], 2, 2, mod=lambda c, m: mod_rows(0, c * 4 + m // 2, 2 * D + m % 2 * SLOT))
            product("pool_g", pool_w_in[0], 2, 2, D, lambda c, m: mod_rows(1, c * 2 + m // 4, m % 4 * SLOT))
            for g in range(4):
                for j in range(2):
                    load(ph["grp"].slot0 + 2 * g + j, 0, 0, rows(pool_w_grp[0, g], 2 * j, 2, 0, N), (2, N))
            product("pool_out", pool_w_out[0], 2, 2, mod=lambda c, m: mod_rows(1, c * 2 + m // 4 + 8, m % 4 * SLOT))
            gate1 = lambda kt, m: mod_rows(1, kt, 2 * D + m % 2 * SLOT)
            product("attn_idx", attn_w_in[0], 1, 2, QI, lambda c, m: gate1(4 * c + m // 2, m))
            w80 = PROJ1 - KI
            for j in range(2):
                load(ph["attn_rest"].slot0 + j, 0, 0, rows(attn_w_in[0], 8 * j, 8, KI, w80), (8, w80))
            product("attn_v", attn_w_in[0], 1, 4, V1, lambda c, m: gate1(8 + 2 * c + m // 2, m))
            product("attn_qk", attn_w_in[0], 4, 2, Q1, col=lambda i, q, per: i * N + q * K1)
            product("attn_gate", attn_w_in[0], 2, 2, G1)
            product("attn_out", attn_w_out[0], 2, 2)
            product("in_uv", w_in[0], 2, 2)
            product("in_qkv", w_in[0], 3, 2, 4 * N)
            product("in_gates", w_in[0], 4, 2, 10 * N)
            p = ph["up"]

            def up(i):
                for q, w in enumerate((w_up_a, w_up_b)):
                    for j in range(4):
                        load(p.slot0 + 4 * q + j, 8, i, rows(w[0], 2 * j, 2, i * N, N), (2, N))
            repeat(sp, 4, up)
            product("w_o", w_o[0], 2, 2)
            p = ph["ffn_in"]

            def ffn_in(i):
                for q in range(2):
                    for j in range(8):
                        load(p.slot0 + 8 * q + j, 16, i, rows(w_ffn_in[0], 2 * j, 2, i * N + q * HID, N), (2, N))
            repeat(sp, 11, ffn_in)
            p = ph["ffn_out"]

            def ffn_out(i):
                for q in range(2):
                    for j in range(2):
                        load(p.slot0 + 2 * q + j, 4, i,
                             w_ffn_out[0, bass.ds((i * 2 + q) * P, P), j * SLOT:(j + 1) * SLOT])
            repeat(sp, HKT // 2, ffn_out)
            p = ph["ple_in"]
            for c in range(4):
                for j in range(9):
                    w, k = (w_ple_gate[0], 2 * j) if j < 8 else (w_ple[0], 0)
                    load(p.slot0 + 9 * c + j, 0, 0, rows(w, k, 2, c * N, N), (2, N))
            for c in range(4):
                sp.wait_ge(ev("x_final"), c + 1)
                sp.dma_start(out_t[:, :, c * N:(c + 1) * N], x[:, :, c * N:(c + 1) * N]).then_inc(stored, 16)
            sp.wait_ge(stored, 64)

        @block.gpsimd
        def _(pool):
            def row_start(buf, width, src, name):
                pool.memset(buf, 0.0).then_inc(ev(name + "_zero"), 1)
                pool.wait_ge(ev(name + "_zero"), 1)
                pool.dma_start(buf[0:1, :], src).then_inc(ev(name), 16)

            b0, b1 = mod_b[0:1, :], mod_b[1:2, :]
            row_start(mod_acc[:, :], 2 * D, b0[:, 0:2 * D], "acc0_start")
            row_start(mod_row[:, :], D, b0[:, 2 * D:3 * D], "row0_start")
            pool.wait_ge(ev("cols0_read"), 1)
            row_start(mod_acc[:, :], 2 * D, b1[:, 0:2 * D], "acc1_start")
            pool.wait_ge(ev("x1_done"), 1)
            row_start(mod_row[:, :], D, b1[:, 2 * D:3 * D], "row1_start")
            pool.wait_ge(ev("masked"), 1)

            def copy_heads(i):
                pool.wait_ge(rope_add, i * 4 + 6)
                for r in range(4):
                    wait(pool, qk_full, i * 4 + r)
                    for k in range(2):
                        ins = pool.tensor_copy(head_in[:, k, :, :], proj1[:, :, bass.ds(i * 4 * P + (r * P + k * K1), P)])
                    ins.then_inc(in_ready, 1)
            copy_heads(0)
            with pool.Fori(1, HEADS // 4) as i:
                copy_heads(i)
            for n in range(3):
                pool.wait_ge(o_done, 4 * n + 4)
                pool.wait_ge(pair_read[n % 2], (ph["attn_gate"].chunk0 + n) // 2 + 1)
                cols = slice(n * N, (n + 1) * N)
                pool.tensor_tensor(proj1[:, :, cols], proj1[:, :, cols], proj1[:, :, G1 + n * N:G1 + (n + 1) * N],
                                   ALU.mult).then_inc(ev("o_gated"), 1)
            pool.wait_ge(ev("o_gated"), 3)
            pool.wait_ge(ev("o_last"), 1)
            pool.dma_start(row[:, :], final_g.rearrange("(a d) -> a d", a=1).partition_broadcast(P)).then_inc(
                ev("final_row"), 16)
            pool.wait_ge(ev("x2_done"), 1)
            pool.wait_ge(ev("sq2"), 8)
            pool.dma_start(w_s[:, :, :], w_s_in[0].rearrange("g t s -> t g s")).then_inc(ev("w_s_in"), 16)
            pool.wait_ge(ev("w_s_in"), 16)
            pool.affine_select(out=w_s[:, :, :], in_=w_s[:, :, :], compare_op=ALU.is_ge, fill=0.0, base=0,
                               pattern=[[0, SGU], [-1, P]], channel_multiplier=1).then_inc(ev("w_s_low"), 1)
            pool.dma_start(sgu_row[:, :], sgu_norm_g.rearrange("a g c -> a (g c)").partition_broadcast(P)).then_inc(
                ev("sgu_row"), 16)
            pool.wait_ge(ev("qk_normed"), 2)

            def copy_head2(t):
                wait(pool, qk2_full, t)
                for k in range(2):
                    ins = pool.tensor_copy(head_in2[:, k, :, :], proj2[:, :, bass.ds(t * P + (Q2, K2)[k], P)])
                ins.then_inc(in2_ready, 1)
            copy_head2(0)
            with pool.Fori(1, SBH) as t:
                copy_head2(t)

            def hid_copy(i, first=False):
                for q in range(2):
                    kt = i * 2 + q
                    if not first:
                        pool.wait_ge(w_used, ph["ffn_out"].w0 + 2 * q - 2 + i * 4)
                    pool.tensor_copy(hid_at[:, q, 0, :], hid_hi[:, bass.ds(kt, 1), :].rearrange(
                        "p a t -> p (a t)").bitcast(F32))
                    pool.tensor_copy(hid_at[:, q, 1, :], hid_lo[:, bass.ds(kt, 1), :].rearrange(
                        "p a t -> p (a t)").bitcast(F32)).then_inc(hid_copied, 1)
            pool.wait_ge(turn_done, turns["h4"])
            hid_copy(0, True)
            with pool.Fori(1, HKT // 2) as i:
                hid_copy(i)
            pool.wait_ge(ev("x5_cols"), 8)
            pool.dma_start(p_nat[:, :, :], p_in[0].rearrange("b (t q) c -> q (b t) c", q=P)).then_inc(ev("p_in"), 16)

        @block.scalar
        def _(act):
            pos_w = [0]
            links = [0]

            def link(ins):
                links[0] += 1
                ins.then_inc(act_chain, 1)
                act.wait_ge(act_chain, links[0])

            w_slots = [s for s, k in enumerate(kinds) if k == "W"]

            def round_w(w0, i=0, nw=0, ns=0):
                s0 = w_slots[w0]
                act.wait_ge(loaded[s0 % RAW], 16 * (s0 // RAW + 1) + i * (16 * (ns // RAW)))
                wait(act, w_used, w0 - SPLIT + 1 + i * nw)
                nc.scalar.copy(w_hi[:, w0 % SPLIT, :], raw[:, s0 % RAW, :]).then_inc(hi_ready, 1)

            def advance(to):
                while pos_w[0] < min(to, len(w_slots)):
                    round_w(pos_w[0])
                    pos_w[0] += 1

            def chunks(name, bodies, per, read=None, c0=0, hook=None):
                p = ph[name]
                assert pos_w[0] == p.w0 + c0 * p.ws + 4, name

                def body(i):
                    for q in range(per):
                        for j in range(p.ws):
                            round_w(p.w0 + 4 + (c0 + q) * p.ws + j, i, per * p.ws, per * p.per)
                            if hook:
                                hook(i, c0 + q, j)
                        if read:
                            read(i, c0 + q, per)
                repeat(act, bodies, body)
                pos_w[0] += bodies * per * p.ws

            def read_pair(p, func, dst, col=lambda i, q, per: (i * per + q) * N, scaled=None):
                def read(i, q, per):
                    c = p.chunk0 + q
                    if scaled:
                        act.wait_ge(ev(scaled), 1)
                    act.wait_ge(w_used, p.w0 + (q + 1) * p.ws + i * (per * p.ws))
                    for tb in range(TB):
                        ins = nc.scalar.activation(dst(tb, col(i, q, per)), acc[c % 2][tb], func,
                                                   scale=rstd[:, tb:tb + 1] if scaled else 1.0)
                    ins.then_inc(pair_read[c % 2], 1)
                return read

            def turn_hi_of(name, banks, hi, source="plain", scale=None, at_bank=0):
                for b in range(at_bank, at_bank + banks):
                    g = turns[name] + b
                    if source == "affine":
                        act.wait_ge(turn_affine, (b + 1) + (8 if name == "h1" else 0))
                    else:
                        act.wait_ge(turn_full, g + 1)
                    src = turned[:, b % 2, :] if source == "affine" else turn[g % 2]
                    if source == "half":
                        nc.scalar.activation(hi(b), src[:, 0:T], ACT.Copy,
                                             scale=1.0 if scale is None else scale(b)).then_inc(turn_hi, 1)
                    elif scale is None:
                        nc.scalar.copy(hi[:, 2 * b:2 * b + 2, :].rearrange("p k t -> p (k t)"), src).then_inc(turn_hi, 1)
                    else:
                        for k in range(2):
                            ins = nc.scalar.activation(hi[:, 2 * b + k, :], src[:, k * T:(k + 1) * T], ACT.Copy,
                                                       scale=scale[:, 2 * b + k:2 * b + k + 1])
                        ins.then_inc(turn_hi, 1)

            def square_sums(scratch, name):
                for tb in range(TB):
                    ins = nc.scalar.activation(scratch[:, tb, :], x[:, tb, :], ACT.Square,
                                               accum_out=sumsq[:, tb:tb + 1])
                ins.then_inc(ev(name), 1)

            def column_squares(p, name, *srcs):
                def step(c):
                    columns_read(act, p, c)
                    for k, src in enumerate(srcs):
                        wait(act, ev(name), c * len(srcs) + k)
                        for tb in range(TB):
                            at_sum = 8 * k + 4 * tb + c
                            ins = nc.scalar.activation(junk[:, tb, :], src(tb, c), ACT.Square,
                                                       accum_out=colsum[:, at_sum:at_sum + 1])
                        ins.then_inc(ev(name), 1)
                return step

            x_cols = lambda tb, c: x[:, tb, c * N:(c + 1) * N]

            def squares_behind(step):
                def hook(i, c, j):
                    if c > 0 and j == 2:
                        step(c - 1)
                return hook

            def last_squares(step):
                def hook(i, c, j):
                    if c == 0 and j == 2:
                        step(3)
                return hook

            def read_row(name):
                def hook(i, c, j):
                    if c == 0 and j % 2 == 1:
                        row_chunk(name, j // 2)
                return hook

            def row_chunk(name, c):
                act.wait_ge(ev(name + "_full"), c + 1)
                nc.scalar.copy(mod_row[:, c * N:(c + 1) * N], rest[c % 2]).then_inc(ev(name + "_row"), 1)

            act.dma_start(x[:, :, :], x_t).then_inc(ev("x_in"), 16)
            act.dma_start(const[:, :], const_in).then_inc(ev("const_in"), 16)
            at_row = 0
            for src in vec_sources:
                n = src.shape[0]
                act.dma_start(vec_rows[at_row:at_row + n, :], src).then_inc(ev("vec_in"), 16)
                at_row += n
            act.dma_start(pos_i[:, :], positions.rearrange("b (t p) -> p (b t)", p=P),
                          allow_slow_non_contiguous=True).then_inc(ev("vec_in"), 16)
            act.dma_start(pool_mix[:, :, :, :], pool_mix_in).then_inc(ev("mix_in"), 16)

            act.wait_ge(ev("vec"), 1)
            nc.scalar.activation(cond, ccol, ACT.Silu).then_inc(ev("cond"), 1)
            act.wait_ge(ev("angles"), 1)
            nc.scalar.activation(rope_s[:, :, :], rope_a[:, 0, :, :], ACT.Sin)
            nc.scalar.activation(rope_c[:, :, :], rope_a[:, 1, :, :], ACT.Sin).then_inc(ev("rope"), 1)
            act.wait_ge(ev("x_in"), 16)
            square_sums(normed, "sq0")
            advance(4)
            affine = lambda name: (lambda b: turn_hi_of(name, 1, act_hi, "affine", at_bank=b))
            plain = lambda name, hi=act_hi, scale=None: (lambda b: turn_hi_of(name, 1, hi, scale=scale, at_bank=b))
            turn_hi_of("h0", 3, act_hi, "affine")
            chunks("pool_v", 1, 4, hook=behind(3, affine("h0")), read=read_pair(ph["pool_v"], ACT.Copy, lambda tb, col: v_nat[:, tb, bass.ds(col, N)]))
            chunks("pool_g", 1, 4, read_pair(ph["pool_g"], ACT.Silu, lambda tb, col: gate_nat[:, tb, bass.ds(col, N)]),
                   hook=read_row("gate0"))
            turn_hi_of("pooled", 2, act_hi)

            def pooled_behind(i, c, j):
                if 2 * c + j < 6:
                    turn_hi_of("pooled", 1, act_hi, at_bank=2 * c + j + 2)
            chunks("grp", 1, 4, hook=pooled_behind)
            turn_hi_of("mixed", 2, act_hi, scale=pscale)
            squares1 = column_squares(ph["pool_out"], "sq1", x_cols)
            chunks("pool_out", 1, 4, hook=hooks(behind(2, plain("mixed", scale=pscale)), squares_behind(squares1)))
            squares1(3)
            act.wait_ge(ev("rstd1"), 1)
            for c in range(4):
                nc.scalar.activation(normed[:, 1, c * N:(c + 1) * N], x[:, 1, c * N:(c + 1) * N], ACT.Copy,
                                     scale=rstd[:, 1:2]).then_inc(ev("normed1_b"), 1)
            turn_hi_of("h1", 3, act_hi, "affine")
            into1 = lambda c: (lambda tb, col: proj1[:, tb, bass.ds(col + c, N)])
            chunks("attn_idx", 1, 2, read_pair(ph["attn_idx"], ACT.Copy, into1(QI)), hook=behind(3, affine("h1")))
            advance(ph["attn_v"].w0 + 4)
            act.wait_ge(w_used, ph["attn_rest"].w0 + 2)
            nc.scalar.copy(proj1[:, :, KI:PROJ1], ps[:, 6:8, 0:PROJ1 - KI]).then_inc(ev("rest_read"), 1)

            def turn_index(i, c, j):
                if 3 <= j < 7:
                    turn_hi_of("qi", 1, lambda b: qiT[:, 2 * (j - 3), :], "half", at_bank=j - 3)
                elif j == 7:
                    turn_hi_of("ki", 1, lambda b: kiT[:, :], "half")

            def index_heads(i, c, j):
                k = (c - 1) * 8 + j
                if k % 3 == 1:
                    for h in (k // 3 * 2, k // 3 * 2 + 1):
                        act.wait_ge(i_full, h + 1)
                        wait(act, i_done, h - 1)
                        nc.scalar.activation(relu[:, h % 2, :], rest[h % 2][:, 0:384], ACT.Relu).then_inc(i_relu, 1)

            read_v = read_pair(ph["attn_v"], ACT.Copy, into1(V1))
            chunks("attn_v", 1, 1, read_v, hook=turn_index)
            chunks("attn_v", 1, 3, read_v, c0=1, hook=index_heads)
            read_qk = read_pair(ph["attn_qk"], ACT.Copy, into1(Q1),
                                lambda i, q, per: q // 2 * N + q % 2 * K1 + i * (per // 2 * N))
            chunks("attn_qk", 1, 2, read_qk, hook=read_row("gate1"))

            def copies(t, r):
                if runs(t):
                    act.wait_ge(qk_full, t + 1)
                    wait(act, s_full, t)
                    if isinstance(t, int) and t == 0:
                        act.wait_ge(ev("masked"), 1)
                    nc.scalar.copy(headT[:, :, :].rearrange("p k t -> p (k t)"), turn[0]).then_inc(qk_ready, 1)
                if runs(t - 2):
                    wait(act, pt_full, t - 1)
                    wait(act, o_full, t - 2)
                    nc.scalar.copy(probT[:, :], turn[1][:, 0:384]).then_inc(pt_ready, 1)

            def exponentials(t, r):
                if runs(t - 1):
                    wait(act, l_ready, t)
                    wait(act, pt_full, t - 1)
                    wait(act, o_done, t - 4)
                    for tb, (c0, c1) in enumerate(((0, P), (P, 384))):
                        d = 2 * ((r - 1) % 4) + tb
                        ins = nc.scalar.activation(prob[:, c0:c1], logit[:, c0:c1], ACT.Exp,
                                                   bias=ntop[:, tb:tb + 1], accum_out=den[:, d:d + 1])
                    ins.then_inc(p_ready, 1)
            chunks("attn_qk", 1, 6, read_qk, 2, at_heads(-5, (1, copies), (3, exponentials)))
            chunks("attn_gate", 1, 4, read_pair(ph["attn_gate"], ACT.Silu, into1(G1)), 0,
                   at_heads(11, (1, copies), (3, exponentials)))
            turn_hi_of("o1", 2, o1_hi)
            squares2 = column_squares(ph["attn_out"], "sq2", lambda tb, c: before_gain[:, tb, :], x_cols)
            h2 = plain("h2", scale=anorm)
            chunks("attn_out", 1, 4, hook=hooks(behind(2, plain("o1", o1_hi)), squares_behind(squares2), streamed(1, h2)))
            into2 = lambda c: (lambda tb, col: proj2[:, tb, bass.ds(col + c, N)])
            chunks("in_uv", 1, 4, read_pair(ph["in_uv"], ACT.Gelu_apprx_tanh, into2(U2), scaled="rstd2"),
                   hook=hooks(last_squares(squares2), last_two(1, h2)))
            chunks("in_qkv", 3, 2, read_pair(ph["in_qkv"], ACT.Copy, into2(Q2), scaled="rstd2"))

            def square_groups(i, c, j):
                if j == 0:
                    wait(act, ev("squares_sum"), c)
                    nc.scalar.activation(squares[:, :], proj2[:, c, S2:V2], ACT.Square).then_inc(ev("squares"), 1)
                if c == 0 and j == 2:
                    for b in range(2):
                        act.wait_ge(ev("ws_turned"), b + 1)
                        nc.scalar.copy(w_sT[:, 4 * b:4 * b + 4, :].rearrange("p g t -> p (g t)"), rest[b]).then_inc(
                            ev("w_sT"), 1)

            def logs(t, r):
                if runs(t, SBH):
                    act.wait_ge(qk2_full, t + 1)
                    wait(act, z_full, t)
                    for k, gain in enumerate((qgs, kg)):
                        ins = nc.scalar.activation(headT2[:, k, :], turn[0][:, k * T:(k + 1) * T], ACT.Copy, scale=gain)
                    ins.then_inc(qk2_ready, 1)
                if runs(t - 3, SBH):
                    act.wait_ge(y_full, t - 2)
                    nc.scalar.copy(proj2[:, :, bass.ds(t * P + (Q2 - 3 * P), P)],
                                   rest[1][:, 0:T].rearrange("p (t d) -> p t d", t=TB)).then_inc(y_done, 1)
                if runs(t - 1, SBH):
                    act.wait_ge(z_full, t)
                    wait(act, b_log, t - 1)
                    nc.scalar.activation(sb_abs[:, :], rest[0][:, 0:384], ACT.Abs).then_inc(b_abs, 1)
                    act.wait_ge(b_abs, t * 2 - 1)
                    nc.scalar.activation(sb_abs[:, :], sb_abs[:, :], ACT.Exp, scale=-1.0).then_inc(b_abs, 1)
                    act.wait_ge(b_abs, t * 2)
                    wait(act, z_read, t - 1)
                    nc.scalar.activation(sb_log[:, :], sb_abs[:, :], ACT.Ln, bias=1.0).then_inc(b_log, 1)

            def weights(t, r):
                if runs(t - 2, SBH):
                    act.wait_ge(b_arg, t - 1)
                    wait(act, y_full, t - 2)
                    nc.scalar.activation(sb_w[:, :], sb_hit[:, t % 2, :], ACT.Exp).then_inc(b_w, 1)
            read_gates = read_pair(ph["in_gates"], ACT.Sigmoid, into2(GA), lambda i, q, per: q * N, "rstd2")
            chunks("in_gates", 1, 2, read_gates, 0, square_groups)
            chunks("in_gates", 1, 6, read_gates, 2, at_heads(-5, (1, logs), (3, weights)))
            turn_hi_of("y2", 2, act_hi)

            def y2_behind(i, c, j):
                if 4 * c + j < 6:
                    turn_hi_of("y2", 1, act_hi, at_bank=4 * c + j + 2)

            def merged_behind(i, c, j):
                if c == 3 and j in (0, 2):
                    b, g = j // 2, turns["merged"] + j // 2
                    act.wait_ge(turn_full, g + 1 + i * 2)
                    nc.scalar.copy(merged_hi[:, bass.ds(i * 4 + 2 * b, 2), :].rearrange("p k t -> p (k t)"),
                                   turn[g % 2]).then_inc(turn_hi, 1)
            chunks("up", 1, 2, hook=y2_behind)
            chunks("up", 3, 2, c0=2, hook=merged_behind)
            squares4 = column_squares(ph["w_o"], "sq4", x_cols)
            h3 = plain("h3", scale=fnorm)
            chunks("w_o", 1, 4, hook=hooks(last_two(1, plain("merged", merged_hi)), squares_behind(squares4),
                                           streamed(1, h3)))
            p = ph["ffn_in"]

            def hid_hi_of(j):
                for b in range(2):
                    g = turns["hid"] + b
                    act.wait_ge(turn_full, g + 1 + j * 2)
                    nc.scalar.copy(hid_hi[:, bass.ds(j * 4 + 2 * b, 2), :].rearrange("p k t -> p (k t)"),
                                   turn[g % 2]).then_inc(turn_hi, 1)

            def ffn_in(j, first):
                for q in range(2):
                    for k in range(8):
                        round_w(p.w0 + 4 + q * 8 + k, j, 16, 16)
                        if first:
                            hooks(last_squares(squares4), last_two(1, h3))(0, q, k)
                    if q == 0:
                        act.wait_ge(w_used, p.w0 + 8 + j * 16)
                        act.wait_ge(ev("rstd4"), 1)
                        if not first:
                            act.wait_ge(turn_full, turns["hid"] + j * 2)
                        for tb in range(TB):
                            ins = nc.scalar.activation(hid[:, tb, :], acc[0][tb], ACT.Silu, scale=rstd[:, tb:tb + 1])
                        ins.then_inc(gate_ready, 1)
                        if not first:
                            hid_hi_of(j - 1)
            ffn_in(0, True)
            with act.Fori(1, 11) as j:
                ffn_in(j, False)
            hid_hi_of(10)
            pos_w[0] += 22 * 8
            p = ph["ffn_out"]

            def ffn_out(i):
                for j in range(4):
                    round_w(p.w0 + 4 + j, i, 4, 4)
            repeat(act, 22, ffn_out)
            pos_w[0] += 88
            turn_hi_of("h4", 2, act_hi, scale=pnorm)
            p = ph["ple_in"]
            h4 = behind(2, plain("h4", scale=pnorm))
            for c in range(4):
                for j in range(9):
                    advance(p.w0 + 9 * c + 4 + j + 1)
                    if j < 8:
                        h4(0, c, j)
                    if c == 0 and j == 6:
                        square_sums(normed2, "sq5")
                    if c == 0 and j == 7:
                        turn_hi_of("p", 1, pT_hi)
                        act.wait_ge(ev("rstd5"), 1)
                act.wait_ge(w_used, p.w0 + 9 * c + 8)
                wait(act, ev("x_final"), c)
                for tb in range(TB):
                    ins = nc.scalar.activation(ple[:, tb, :], acc[0][tb], ACT.Sigmoid, scale=rstd[:, tb:tb + 1])
                ins.then_inc(pair_read[0], 1)

        @block.vector
        def _(dve):
            V = nc.vector
            pos_s = [0]
            links = [0]

            def link(ins):
                links[0] += 1
                ins.then_inc(dve_chain, 1)
                dve.wait_ge(dve_chain, links[0])

            w_of = {}
            for s, k in enumerate(kinds):
                if k == "W":
                    w_of[s] = len(w_of)

            def split(s0, i=0, ns=0, nw=0):
                w0 = w_of[s0]
                dve.wait_ge(hi_ready, w0 + 1 + i * nw)
                V.tensor_tensor(w_lo[:, w0 % SPLIT, :], raw[:, s0 % RAW, :],
                                w_hi[:, w0 % SPLIT, :].bitcast(F32), ALU.subtract).then_inc(slot_done, 1)

            def modulate(s0, target, kt, apart, i=0, ns=0):
                dve.wait_ge(loaded[s0 % RAW], 16 * (s0 // RAW + 1) + i * (16 * (ns // RAW)))
                wait(dve, slot_done, s0 - apart + 1 + i * ns)
                V.scalar_tensor_tensor(out=target, in0=raw[:, s0 % RAW, :], scalar=cond[:, bass.ds(kt, 1)],
                                       in1=target, op0=ALU.mult, op1=ALU.add).then_inc(slot_done, 1)

            def advance(w_to):
                while pos_s[0] < len(kinds) and w_of[pos_s[0]] < w_to:
                    split(pos_s[0])
                    pos_s[0] += 1

            def chunks(name, bodies, per, read=None, mod=None, c0=0, hook=None):
                p = ph[name]
                assert pos_s[0] == p.slot0 + c0 * p.per + 4, name

                def body(i):
                    for q in range(per):
                        m = w = 0
                        for j in range(4, p.per + 4):
                            s0 = p.slot0 + (c0 + q) * p.per + j
                            if j < p.per and p.seq[j] == "M":
                                target, kt, apart = mod(i * per + c0 + q, m)
                                modulate(s0, target, kt, apart, i, per * p.per)
                                m += 1
                            else:
                                split(s0, i, per * p.per, per * p.ws)
                                if hook:
                                    hook(i, c0 + q, w)
                                w += 1
                        if read:
                            read(i, c0 + q)
                repeat(dve, bodies, body)
                pos_s[0] += bodies * per * p.per

            def acc_cols(m):
                return mod_acc[:, m % 4 * SLOT:(m % 4 + 1) * SLOT]

            def row_cols(m):
                return mod_row[:, m % 2 * SLOT:(m % 2 + 1) * SLOT]

            def add_chunk(p, gated, gain=False):
                def read(i, q):
                    c = p.chunk0 + q
                    dve.wait_ge(w_used, p.w0 + (q + 1) * p.ws + i * (2 * p.ws))
                    col = bass.ds((i * 2 + q) * N, N)
                    for tb in range(TB):
                        if gated:
                            V.tensor_tensor(resid[:, tb, :], acc[c % 2][tb], mod_row[:, col], ALU.mult).then_inc(
                                ev(p.name + "_gated"), 1)
                            dve.wait_ge(ev(p.name + "_gated"), 2 * q + tb + 1 + i * 4)
                            if gain:
                                wait(dve, ev("sq2"), 2 * q)
                                V.tensor_tensor(before_gain[:, tb, :], x[:, tb, col], resid[:, tb, :],
                                                ALU.add).then_inc(ev("x2_summed"), 1)
                                dve.wait_ge(ev("x2_summed"), 2 * q + tb + 1)
                                ins = V.tensor_tensor(x[:, tb, col], before_gain[:, tb, :], row[:, col], ALU.mult)
                            else:
                                ins = V.tensor_tensor(x[:, tb, col], x[:, tb, col], resid[:, tb, :], ALU.add)
                        else:
                            ins = V.tensor_tensor(x[:, tb, col], acc[c % 2][tb], x[:, tb, col], ALU.add)
                        if tb == TB - 1:
                            ins.then_inc(pair_read[c % 2], 1)
                return read

            def rsqrt(sums, y, scale):
                n = y.shape[1]
                half, sq = newton[:, 0, 0:n], newton[:, 1, 0:n]
                link(V.tensor_scalar(half, sums, scale, EPS, ALU.mult, ALU.add))
                link(V.tensor_scalar(sq.bitcast(I32), half.bitcast(I32), 1, None, ALU.logical_shift_right))
                link(V.tensor_scalar(y.bitcast(I32), sq.bitcast(I32), -1.0, float(0x5F3759DF), ALU.mult, ALU.add))
                link(V.tensor_scalar(half, half, -0.5, None, ALU.mult))
                for _ in range(3):
                    link(V.tensor_tensor(sq, y, y, ALU.mult))
                    link(V.tensor_tensor(sq, sq, half, ALU.mult))
                    link(V.scalar_tensor_tensor(out=y, in0=sq, scalar=1.5, in1=y, op0=ALU.add, op1=ALU.mult))

            def normalize(sq, dst, done):
                dve.wait_ge(ev(sq), 1)
                rsqrt(sumsq, rstd, 1.0 / D)
                for tb in range(TB):
                    V.tensor_scalar(dst[:, tb, :], x[:, tb, :], rstd[:, tb:tb + 1], None, ALU.mult).then_inc(ev(done), 1)

            def token_sums(k, dst):
                link(V.tensor_reduce(dst, colsum[:, 8 * k:8 * k + 8].rearrange("p (t c) -> p t c", t=TB), AX_X, ALU.add))

            def turn_lo_of(name, banks, hi, lo, scale=None, at_bank=0):
                for b in range(at_bank, at_bank + banks):
                    g = turns[name] + b
                    dve.wait_ge(turn_hi, g + 1)
                    if scale is None:
                        V.tensor_tensor(lo[:, 2 * b:2 * b + 2, :].rearrange("p k t -> p (k t)"), turn[g % 2],
                                        hi[:, 2 * b:2 * b + 2, :].rearrange("p k t -> p (k t)").bitcast(F32),
                                        ALU.subtract).then_inc(turn_done, 1)
                    else:
                        for k in range(2):
                            ins = V.scalar_tensor_tensor(
                                out=lo[:, 2 * b + k, :], in0=turn[g % 2][:, k * T:(k + 1) * T],
                                scalar=scale[:, 2 * b + k:2 * b + k + 1], in1=hi[:, 2 * b + k, :].bitcast(F32),
                                op0=ALU.mult, op1=ALU.subtract)
                        ins.then_inc(turn_done, 1)

            plain = lambda name, hi=act_hi, lo=act_lo, scale=None: (
                lambda b: turn_lo_of(name, 1, hi, lo, scale, b))

            def affine_behind(name):
                def hook(i, c, j):
                    if c == 0 and j < 6:
                        turn_affine_of(name, j + 3, j + 4)
                return hook

            def turn_affine_of(name, b0, b1):
                for b in range(b0, b1):
                    if b < 8:
                        g = turns[name] + b
                        dve.wait_ge(turn_full, g + 1)
                        wait(dve, turn_done, g - 1)
                        for k in range(2):
                            ct = 2 * b + k
                            ins = V.tensor_scalar(turned[:, b % 2, k * T:(k + 1) * T], turn[g % 2][:, k * T:(k + 1) * T],
                                                  scale1[:, ct:ct + 1], shift[:, ct:ct + 1], ALU.mult, ALU.add)
                        ins.then_inc(turn_affine, 1)
                    if b > 0:
                        g = turns[name] + b - 1
                        dve.wait_ge(turn_hi, g + 1)
                        V.tensor_tensor(act_lo[:, 2 * b - 2:2 * b, :].rearrange("p k t -> p (k t)"),
                                        turned[:, (b - 1) % 2, :],
                                        act_hi[:, 2 * b - 2:2 * b, :].rearrange("p k t -> p (k t)").bitcast(F32),
                                        ALU.subtract).then_inc(turn_done, 1)

            def mod_columns(layer, gain):
                dve.wait_ge(ev(f"cols{layer}_read"), 1)
                link(V.tensor_copy(shift, rest[0][:, 0:16]))
                link(V.scalar_tensor_tensor(out=scale1, in0=rest[0][:, 16:32], scalar=1.0, in1=gain,
                                            op0=ALU.add, op1=ALU.mult))

            dve.wait_ge(ev("vecT"), 1)
            V.tensor_copy(vec[:, 0:122], rest[0][:, 0:122]).then_inc(ev("vec"), 1)
            dve.wait_ge(ev("vec"), 1)
            link(V.tensor_scalar(qgs, qg, HD ** -0.5, None, ALU.mult))
            link(V.tensor_copy(pos, pos_i[:, :]))
            ang, red, turns_n, tmp = (rope_a[:, i, :, :] for i in range(4))
            for tb in range(TB):
                link(V.tensor_scalar(ang[:, tb, :], freq, pos[:, tb:tb + 1], None, ALU.mult))
            link(V.tensor_scalar(turns_n, ang, 1.0 / TWO_PI, ROUND, ALU.mult, ALU.add))
            link(V.tensor_scalar(turns_n, turns_n, ROUND, None, ALU.subtract))
            for part in TWO_PI_PARTS:
                link(V.scalar_tensor_tensor(out=ang, in0=turns_n, scalar=-part, in1=ang, op0=ALU.mult, op1=ALU.add))
            link(V.tensor_scalar(ang, ang, PI_IN, -PI_IN, ALU.min, ALU.max))
            link(V.tensor_scalar(red, ang, np.pi / 2, None, ALU.add))
            link(V.tensor_scalar(tmp, red, np.pi, -TWO_PI, ALU.is_gt, ALU.mult))
            link(V.tensor_tensor(red, red, tmp, ALU.add))
            V.tensor_scalar(red, red, PI_IN, -PI_IN, ALU.min, ALU.max).then_inc(ev("angles"), 1)

            dve.wait_ge(ev("cond"), 1)
            dve.wait_ge(ev("acc0_start"), 16)
            for j in range(4):
                modulate(j, acc_cols(j), 0, 4)
            normalize("sq0", normed, "normed0")
            with dve.Fori(1, KT) as i:
                for j in range(4):
                    modulate(j, acc_cols(j), i, 4, i, 4)
            pos_s[0] = 64
            for _ in range(4):
                split(pos_s[0])
                pos_s[0] += 1
            mod_columns(0, norm0)
            turn_affine_of("h0", 0, 3)
            dve.wait_ge(ev("row0_start"), 16)
            chunks("pool_v", 1, 4, hook=affine_behind("h0"), mod=lambda c, m: (row_cols(m), c * 4 + m // 2, 3))
            dve.wait_ge(ev("acc1_start"), 16)
            chunks("pool_g", 1, 4, mod=lambda c, m: (acc_cols(m), c * 2 + m // 4, 6))
            turn_lo_of("pooled", 2, act_hi, act_lo)
            p = ph["grp"]

            def pooled_behind(i, c, j):
                if 2 * c + j < 6:
                    turn_lo_of("pooled", 1, act_hi, act_lo, at_bank=2 * c + j + 2)

            def gate_group(i, g):
                c = p.chunk0 + g
                dve.wait_ge(w_used, p.w0 + 2 * g + 2)
                for tb in range(TB):
                    ins = V.tensor_tensor(u_nat[:, tb, g * N:(g + 1) * N], acc[c % 2][tb],
                                          gate_nat[:, tb, g * N:(g + 1) * N], ALU.mult)
                ins.then_inc(pair_read[c % 2], 1)
            chunks("grp", 1, 4, gate_group, hook=pooled_behind)
            turn_lo_of("mixed", 2, act_hi, act_lo, pscale)
            dve.wait_ge(ev("gate0_row"), 4)
            chunks("pool_out", 1, 4, add_chunk(ph["pool_out"], True), lambda c, m: (acc_cols(m), c * 2 + m // 4 + 8, 6),
                   hook=behind(2, plain("mixed", scale=pscale)))
            V.engine_nop().then_inc(ev("x1_done"), 1)
            mod_columns(1, norm1)
            dve.wait_ge(ev("sq1"), 4)
            token_sums(0, sumsq)
            rsqrt(sumsq, rstd, 1.0 / D)
            V.engine_nop().then_inc(ev("rstd1"), 1)
            for c in range(4):
                V.tensor_scalar(normed[:, 0, c * N:(c + 1) * N], x[:, 0, c * N:(c + 1) * N], rstd[:, 0:1], None,
                                ALU.mult).then_inc(ev("normed1"), 1)
            turn_affine_of("h1", 0, 3)
            dve.wait_ge(ev("row1_start"), 16)
            gate_rows = lambda kt, m: (row_cols(m), kt, 3)
            chunks("attn_idx", 1, 2, hook=affine_behind("h1"), mod=lambda c, m: gate_rows(4 * c + m // 2, m))
            advance(ph["attn_v"].w0 + 4)

            def rotate(tb, col, heads, width, half, f0, k, i=0):
                y = proj1[:, tb, bass.ds(col, heads * width)].rearrange("p (h w) -> p h w", h=heads)
                x1, x2 = y[:, :, 0:half], y[:, :, half:2 * half]
                cos = rope_c[:, tb, f0:f0 + half].unsqueeze(1).to_broadcast([P, heads, half])
                sin = rope_s[:, tb, f0:f0 + half].unsqueeze(1).to_broadcast([P, heads, half])
                t = [rope_t[:, n, 0:heads * half].rearrange("p (h w) -> p h w", h=heads) for n in range(4)]
                wait(dve, rope_add, k + i * 4)
                V.tensor_tensor(t[0], x1, cos, ALU.mult)
                V.tensor_tensor(t[1], x2, sin, ALU.mult)
                V.tensor_tensor(t[2], x2, cos, ALU.mult)
                V.tensor_tensor(t[3], x1, sin, ALU.mult).then_inc(rope_mul, 1)
                dve.wait_ge(rope_mul, k + 1 + i * 4)
                V.tensor_tensor(x1, t[0], t[1], ALU.subtract)
                V.tensor_tensor(x2, t[2], t[3], ALU.add).then_inc(rope_add, 1)

            def rotate_heads(i, q):
                if q % 2 == 1:
                    n = q // 2
                    for k in range(2):
                        dve.wait_ge(pair_read[k], ph["attn_qk"].chunk0 // 2 + n + 1 + i)
                    for k in range(2):
                        for tb in range(TB):
                            rotate(tb, i * N + (n * N + k * K1), 4, HD, ROT // 2, 0, 2 + 4 * n + 2 * k + tb, i)

            def index_inputs(i, c, j):
                if j == 0:
                    dve.wait_ge(ev("rope"), 1)
                    dve.wait_ge(ev("rest_read"), 1)
                    for q in range(2):
                        dve.wait_ge(pair_read[q], (ph["attn_idx"].chunk0 + 2) // 2)
                    for tb in range(TB):
                        rotate(tb, QI, IH + 1, ID, IROT // 2, ROT // 2, tb)
                    dve.wait_ge(rope_add, 2)
                    for k in range(2):
                        V.tensor_copy(ki_twice[:, :, k * ID:(k + 1) * ID], proj1[:, :, KI:KI + ID])
                    V.tensor_scalar(proj1[:, :, WI:WI + IH], proj1[:, :, WI:WI + IH], (IH * ID) ** -0.5, None, ALU.mult)
                    V.tensor_copy(work[:, :], hidden).then_inc(ev("index_in"), 1)
                elif 3 <= j < 7:
                    dve.wait_ge(turn_hi, turns["qi"] + j - 2)
                    V.tensor_copy(qiT[:, 2 * (j - 3) + 1, :], turn[(turns["qi"] + j - 3) % 2][:, T:2 * T]).then_inc(
                        turn_done, 1)
                elif j == 7:
                    dve.wait_ge(turn_hi, turns["ki"] + 1)
                    V.engine_nop().then_inc(turn_done, 1)

            def index_heads(i, c, j):
                k = (c - 1) * 8 + j
                if k == 0:
                    dve.wait_ge(ev("index_in"), 1)
                if k % 3 == 1:
                    for h in (k // 3 * 2, k // 3 * 2 + 1):
                        dve.wait_ge(i_relu, h + 1)
                        wait(dve, i_done, h)
                        for tb, (c0, c1) in enumerate(((0, P), (P, 384))):
                            ins = V.scalar_tensor_tensor(out=work[:, c0:c1], in0=relu[:, h % 2, c0:c1],
                                                         scalar=proj1[:, tb, WI + h:WI + h + 1], in1=work[:, c0:c1],
                                                         op0=ALU.mult, op1=ALU.add)
                        ins.then_inc(i_done, 1)

            def top_keys(i, c, j):
                c0, c1 = ((0, P), (P, 384))[c]
                if c == 0 and j == 0:
                    dve.wait_ge(i_done, IH)
                link(V.max(out=best, in_=work[:, c0:c1]))
                link(V.match_replace(out=work[:, c0:c1], in_to_replace=best, in_values=work[:, c0:c1],
                                     imm_value=TAKEN))
                if c == 1 and j == 7:
                    link(V.tensor_scalar(amask[:, :], work[:, :], TAKEN, -LOW, ALU.is_equal, ALU.mult))
                    V.scalar_tensor_tensor(out=amask[:, :], in0=amask[:, :], scalar=LOW, in1=hidden,
                                           op0=ALU.add, op1=ALU.min).then_inc(ev("masked"), 1)
                    dve.wait_ge(ev("masked"), 1)

            gate_rows4 = lambda c, m: (row_cols(m), 8 + 2 * c + m // 2, 4)
            chunks("attn_v", 1, 1, mod=gate_rows4, hook=index_inputs)
            chunks("attn_v", 1, 3, mod=gate_rows4, c0=1, hook=index_heads)
            chunks("attn_qk", 1, 2, rotate_heads, hook=top_keys)

            def attend(t, r):
                if runs(t - 1):
                    wait(dve, s_full, t)
                    wait(dve, p_ready, t - 1)
                    V.scalar_tensor_tensor(out=logit[:, :], in0=rest[0][:, 0:384], scalar=HD ** -0.5,
                                           in1=amask[:, :], op0=ALU.mult, op1=ALU.add).then_inc(s_read, 1)
                    dve.wait_ge(s_read, t)
                    for tb, (c0, c1) in enumerate(((0, P), (P, 384))):
                        V.tensor_reduce(top[:, tb:tb + 1], logit[:, c0:c1], AX_X, ALU.max).then_inc(l_max, 1)
                    dve.wait_ge(l_max, t * 2)
                    V.tensor_scalar(ntop, top, -1.0, None, ALU.mult).then_inc(l_ready, 1)
                if runs(t - 3):
                    dve.wait_ge(o_full, t - 2)
                    wait(dve, o_done, t - 3)
                    d = 2 * ((r - 3) % 4)
                    V.reciprocal(rden, den[:, d:d + 2]).then_inc(r_ready, 1)
                    dve.wait_ge(r_ready, t - 2)
                    for tb in range(TB):
                        ins = V.tensor_scalar(proj1[:, tb, bass.ds(t * P - 3 * P, P)], rest[1][:, tb * P:(tb + 1) * P],
                                              rden[:, tb:tb + 1], None, ALU.mult)
                    ins.then_inc(o_done, 1)
            chunks("attn_qk", 1, 6, rotate_heads, c0=2, hook=at_heads(-5, (2, attend)))
            chunks("attn_gate", 1, 4, hook=at_heads(11, (2, attend)))
            dve.wait_ge(pair_read[1], (ph["attn_gate"].chunk0 + 3) // 2 + 1)
            dve.wait_ge(o_done, HEADS)
            V.tensor_tensor(proj1[:, :, 3 * N:D], proj1[:, :, 3 * N:D], proj1[:, :, G1 + 3 * N:QI], ALU.mult).then_inc(
                ev("o_last"), 1)
            turn_lo_of("o1", 2, o1_hi, o1_lo)
            dve.wait_ge(ev("gate1_row"), 4)
            dve.wait_ge(ev("final_row"), 16)
            h2 = plain("h2", scale=anorm)
            chunks("attn_out", 1, 4, add_chunk(ph["attn_out"], True, True),
                   hook=hooks(behind(2, plain("o1", o1_hi, o1_lo)), streamed(1, h2)))
            V.engine_nop().then_inc(ev("x2_done"), 1)

            def norm_twice(i, c, j):
                if c == 0 and j == 6:
                    dve.wait_ge(ev("sq2"), 8)
                    token_sums(0, sumsq)
                    rsqrt(sumsq, rfinal, 1.0 / D)
                    token_sums(1, sumnext)
                    for _ in range(2):
                        link(V.tensor_tensor(sumnext, sumnext, rfinal, ALU.mult))
                    rsqrt(sumnext, rnext, 1.0 / D)
                    V.tensor_tensor(rstd, rfinal, rnext, ALU.mult).then_inc(ev("rstd2"), 1)
                if c == 1 and j in (2, 4):
                    tb = j // 2 - 1
                    V.tensor_scalar(x[:, tb, :], x[:, tb, :], rfinal[:, tb:tb + 1], None, ALU.mult).then_inc(
                        ev("x3_done"), 1)
            chunks("in_uv", 1, 4, hook=hooks(last_two(1, h2), norm_twice))
            chunks("in_qkv", 3, 2)

            def norm_groups(i, c, j):
                y = proj2[:, c, S2:V2].rearrange("p (g c) -> p g c", c=P)
                s, r = ssq2[:, 24 * c:24 * c + 24], rs2[:, 24 * c:24 * c + 24]
                if j == 2:
                    dve.wait_ge(ev("squares"), c + 1)
                    V.tensor_reduce(s, squares[:, :].rearrange("p (g c) -> p g c", c=P), AX_X, ALU.add).then_inc(
                        ev("squares_sum"), 1)
                    dve.wait_ge(ev("squares_sum"), c + 1)
                    rsqrt(s, r, 1.0 / P)
                if j == 3:
                    V.tensor_tensor(y, y, r.unsqueeze(2).to_broadcast([P, 24, P]), ALU.mult).then_inc(
                        ev("qk_normed"), 1)
                if c == 1 and j == 4:
                    dve.wait_ge(ev("sgu_row"), 16)
                    dve.wait_ge(ev("qk_normed"), 2)
                    for tb in range(TB):
                        V.tensor_tensor(proj2[:, tb, S2:Q2], proj2[:, tb, S2:Q2], sgu_row[:, :], ALU.mult).then_inc(
                            ev("sgu_in"), 1)

            def gate_spatial(i, c, j):
                if c == 2 and j in (1, 3):
                    for n in (j - 1, j):
                        dve.wait_ge(ev("sgu_full"), n + 1)
                        tb, g0 = n // 2, n % 2 * 4
                        for g in range(g0, g0 + 4):
                            u = proj2[:, tb, g * P:(g + 1) * P]
                            ins = V.scalar_tensor_tensor(out=u, in0=mixes[n % 2][:, (g - g0) * P:(g - g0 + 1) * P],
                                                         scalar=bs[:, g:g + 1], in1=u, op0=ALU.add, op1=ALU.mult)
                        ins.then_inc(ev("sgu_read"), 1)

            def sticks(t, r):
                if runs(t - 2, SBH):
                    dve.wait_ge(b_tail, t - 1)
                    V.tensor_tensor(sb_hit[:, t % 2, :], turn[1][:, 0:384], sb_hit[:, t % 2, :],
                                    ALU.add).then_inc(b_arg, 1)
                if runs(t - 1, SBH):
                    dve.wait_ge(b_log, t)
                    wait(dve, b_tail, t - 1)
                    wait(dve, b_w, t - 2)
                    V.scalar_tensor_tensor(out=sb_miss[:, :], in0=rest[0][:, 0:384], scalar=0.0,
                                           in1=sb_log[:, :], op0=ALU.max, op1=ALU.add).then_inc(b_sum, 1)
                    V.scalar_tensor_tensor(out=sb_hit[:, (t - 1) % 2, :], in0=rest[0][:, 0:384], scalar=0.0,
                                           in1=sb_log[:, :], op0=ALU.min, op1=ALU.subtract).then_inc(z_read, 1)
                    dve.wait_ge(b_sum, t)
                    V.tensor_tensor(sb_miss[:, :], sb_miss[:, :], nstrict, ALU.mult).then_inc(b_miss, 1)

            def mask(t, r):
                if runs(t - 2, SBH):
                    dve.wait_ge(b_w, t - 1)
                    V.tensor_tensor(sb_w[:, :], sb_w[:, :], strict, ALU.mult).then_inc(b_mask, 1)
            heads2 = at_heads(-5, (2, sticks), (3, mask))

            def spatial_and_heads(i, c, j):
                gate_spatial(i, c, j)
                heads2(i, c, j)
            chunks("in_gates", 1, 2, hook=norm_groups)
            chunks("in_gates", 1, 6, c0=2, hook=spatial_and_heads)
            turn_lo_of("y2", 2, act_hi, act_lo)
            p = ph["up"]

            def y2_behind(i, c, j):
                if 4 * c + j < 6:
                    turn_lo_of("y2", 1, act_hi, act_lo, at_bank=4 * c + j + 2)

            def merged_behind(i, c, j):
                if c == 3 and j in (0, 2):
                    b, g = j // 2, turns["merged"] + j // 2
                    dve.wait_ge(turn_hi, g + 1 + i * 2)
                    kts = bass.ds(i * 4 + 2 * b, 2)
                    V.tensor_tensor(merged_lo[:, kts, :].rearrange("p k t -> p (k t)"), turn[g % 2],
                                    merged_hi[:, kts, :].rearrange("p k t -> p (k t)").bitcast(F32),
                                    ALU.subtract).then_inc(turn_done, 1)

            def merge(i, q):
                n = q // 2
                dve.wait_ge(w_used, p.w0 + 4 * q + 4 + i * 8)
                for tb in range(TB):
                    g = proj2[:, tb, bass.ds(i * N + (n * N + (GA, GB)[q % 2]), N)]
                    ins = V.tensor_tensor(g, acc[q % 2][tb], g, ALU.mult)
                    if q % 2 == 1:
                        ins.then_inc(ev("up_gated"), 1)
                        dve.wait_ge(ev("up_gated"), tb + 1 + 2 * n + i * 2)
                        dve.wait_ge(pair_read[0], p.chunk0 // 2 + 1 + n + i)
                        ga = proj2[:, tb, bass.ds(i * N + (n * N + GA), N)]
                        ins = V.tensor_tensor(ga, ga, g, ALU.add)
                ins.then_inc(pair_read[q % 2], 1)
            chunks("up", 1, 2, merge, hook=y2_behind)
            chunks("up", 3, 2, merge, c0=2, hook=merged_behind)
            h3 = plain("h3", scale=fnorm)
            dve.wait_ge(ev("x3_done"), 2)
            chunks("w_o", 1, 4, add_chunk(ph["w_o"], False),
                   hook=hooks(last_two(1, plain("merged", merged_hi, merged_lo)), streamed(1, h3)))

            def norm4(i, c, j):
                if c == 0 and j == 6:
                    dve.wait_ge(ev("sq4"), 4)
                    token_sums(0, sumsq)
                    rsqrt(sumsq, rstd, 1.0 / D)
                    V.engine_nop().then_inc(ev("rstd4"), 1)
            p = ph["ffn_in"]

            def hid_lo_of(j):
                for b in range(2):
                    g = turns["hid"] + b
                    dve.wait_ge(turn_hi, g + 1 + j * 2)
                    kts = bass.ds(j * 4 + 2 * b, 2)
                    V.tensor_tensor(hid_lo[:, kts, :].rearrange("p k t -> p (k t)"), turn[g % 2],
                                    hid_hi[:, kts, :].rearrange("p k t -> p (k t)").bitcast(F32),
                                    ALU.subtract).then_inc(turn_done, 1)

            def ffn_in(j, first):
                for q in range(2):
                    for k in range(8):
                        split(p.slot0 + 4 + q * 8 + k, j, 16, 16)
                        if first:
                            hooks(last_two(1, h3), norm4)(0, q, k)
                    if q == 0 and not first:
                        hid_lo_of(j - 1)
                    if q == 1:
                        dve.wait_ge(w_used, p.w0 + 16 + j * 16)
                        dve.wait_ge(gate_ready, j + 1)
                        for tb in range(TB):
                            ins = V.scalar_tensor_tensor(out=hid[:, tb, :], in0=acc[1][tb], scalar=rstd[:, tb:tb + 1],
                                                         in1=hid[:, tb, :], op0=ALU.mult, op1=ALU.mult)
                        ins.then_inc(hid_ready, 1)
            ffn_in(0, True)
            with dve.Fori(1, 11) as j:
                ffn_in(j, False)
            hid_lo_of(10)
            pos_s[0] += 22 * 8
            p = ph["ffn_out"]

            def ffn_out(i):
                for j in range(4):
                    split(p.slot0 + 4 + j, i, 4, 4)
            repeat(dve, 22, ffn_out)
            pos_s[0] += 88
            dve.wait_ge(w_used, p.w0 + 88)
            for tb, n in X5_ORDER:
                cols = slice(n * N, (n + 1) * N)
                V.tensor_tensor(x[:, tb, cols], ps[:, 4 * tb + n], x[:, tb, cols], ALU.add).then_inc(ev("x5_cols"), 1)
            turn_lo_of("h4", 2, act_hi, act_lo, pnorm)
            p = ph["ple_in"]
            h4 = behind(2, plain("h4", scale=pnorm))
            for c in range(4):
                for j in range(9):
                    advance(p.w0 + 9 * c + 4 + j + 1)
                    if j < 8:
                        h4(0, c, j)
                    if c == 0 and j == 7:
                        turn_lo_of("p", 1, pT_hi, pT_lo)
                        dve.wait_ge(ev("sq5"), 1)
                        rsqrt(sumsq, rstd, 1.0 / D)
                        V.engine_nop().then_inc(ev("rstd5"), 1)
                dve.wait_ge(w_used, p.w0 + 9 * c + 9)
                dve.wait_ge(pair_read[0], pairs_before + c + 1)
                cols = slice(c * N, (c + 1) * N)
                for tb in range(TB):
                    ins = V.tensor_tensor(ple[:, tb, :], acc[1][tb], ple[:, tb, :], ALU.mult)
                ins.then_inc(pair_read[1], 1)
                dve.wait_ge(pair_read[1], pairs_before + c + 1)
                for tb in range(TB):
                    ins = V.tensor_tensor(x[:, tb, cols], x[:, tb, cols], ple[:, tb, :], ALU.add)
                ins.then_inc(ev("x_final"), 1)

        @block.tensor
        def _(pe):
            M = nc.tensor.matmul

            def three(dst, hi_t, lo_t, w, cols, first, last):
                wh, wl = w_hi[:, w, cols], w_lo[:, w, cols]
                M(dst, hi_t, wh, start=first, stop=False)
                M(dst, hi_t, wl, start=False, stop=False)
                return M(dst, lo_t, wh, start=False, stop=last)

            def chunk(p, q, i, per, kts, turned_at, hook=None, split_acts=(act_hi, act_lo)):
                c = p.chunk0 + q
                hi_t, lo_t = split_acts
                wait(pe, pair_read[c % 2], c // 2 + i * (per // 2))
                js = p.w_at
                for n in range(len(kts) // 2):
                    pe.wait_ge(slot_done, p.slot0 + q * p.per + js[n] + 1 + i * (per * p.per))
                    w0 = p.w0 + q * p.ws + n
                    for k in range(2):
                        kt = kts[2 * n + k]
                        if kt % 2 == 0:
                            pe.wait_ge(turn_done, turned_at + kt // 2 + 1)
                        for tb in range(TB):
                            t = slice(tb * P, (tb + 1) * P)
                            ins = three(acc[c % 2][tb], hi_t[:, kt, t], lo_t[:, kt, t], w0 % SPLIT,
                                        slice(k * N, (k + 1) * N), n == 0 and k == 0,
                                        n == len(kts) // 2 - 1 and k == 1)
                            if k == 1 and tb == 1:
                                ins.then_inc(w_used, 1)
                    if hook:
                        hook(i, q, n)

            def chunks(name, bodies, per, turned, kts=range(KT), c0=0, hook=None, split_acts=(act_hi, act_lo)):
                p = ph[name]

                def body(i):
                    for q in range(per):
                        chunk(p, c0 + q, i, per, kts, turns[turned], hook, split_acts)
                repeat(pe, bodies, body)

            def turn_bank(g, tiles, i=0, ni=0):
                wait(pe, turn_done, g - 1 + i * ni)
                for n, tile in enumerate(tiles):
                    ins = nc.tensor.transpose(turn[g % 2][:, n * P:(n + 1) * P], tile, ident)
                ins.then_inc(turn_full, 1)

            def turner(name, src, waits=None):
                def step(b):
                    if waits:
                        waits(b)
                    turn_bank(turns[name] + b, [src(tb, 2 * b + k) for k in range(2) for tb in range(TB)])
                return step

            def turn_first(n, step):
                for b in range(n):
                    step(b)

            def added(name):
                return lambda b: columns_read(pe, ph[name], b // 2)

            def columns_of(name, layer):
                for j in range(32):
                    ins = M(rest[0][:, j:j + 1], mod_acc[:, j * P:(j + 1) * P], ones[:, 0:1], start=True, stop=True)
                ins.then_inc(ev(name), 1)

            def sum_row(name, after):
                def hook(i, c, n):
                    if c == 0 and n % 2 == 0:
                        row_chunk(name, n // 2, after)
                return hook

            def row_chunk(name, c, after):
                if c == 0:
                    pe.wait_ge(slot_done, after)
                wait(pe, ev(name + "_row"), c - 1)
                M(rest[c % 2], ones, mod_row[:, c * N:(c + 1) * N], start=True, stop=True).then_inc(
                    ev(name + "_full"), 1)

            tile = lambda buf: (lambda tb, kt: buf[:, tb, kt * P:(kt + 1) * P])

            pe.wait_ge(ev("const_in"), 16)
            pe.wait_ge(ev("vec_in"), 16 * (len(vec_sources) + 1))
            nc.tensor.transpose(rest[0][:, 0:122], vec_rows[0:122, :], ident[0:122, 0:122]).then_inc(ev("vecT"), 1)
            pe.wait_ge(ev("vec"), 1)
            pe.wait_ge(slot_done, 64)
            columns_of("cols0_read", 0)
            pe.wait_ge(ev("normed0"), 2)
            h0 = turner("h0", tile(normed))
            turn_first(3, h0)
            chunks("pool_v", 1, 4, "h0", hook=behind(3, h0))
            chunks("pool_g", 1, 4, "h0", hook=sum_row("gate0", ph["pool_g"].slot0))
            pe.wait_ge(ev("mix_in"), 16)

            def pool_bank(b):
                g = turns["pooled"] + b
                wait(pe, turn_done, g - 1)
                columns_read(pe, ph["pool_v"], b // 2)
                for k in range(2):
                    ct = 2 * b + k
                    c = slice(ct * P, (ct + 1) * P)
                    M(turn[g % 2][:, k * T:(k + 1) * T], v_nat[:, 0, c], pool_mix[:, 0, ct // 4, :], start=True, stop=False)
                    ins = M(turn[g % 2][:, k * T + P:(k + 1) * T], v_nat[:, 1, c], pool_mix[:, 1, ct // 4, P:T],
                            start=False, stop=True)
                ins.then_inc(turn_full, 1)

            def pooled_behind(i, g, n):
                if 2 * g + n < 6:
                    pool_bank(2 * g + n + 2)
            turn_first(2, pool_bank)
            for g in range(4):
                chunk(ph["grp"], g, 0, 4, range(4 * g, 4 * g + 4), turns["pooled"], pooled_behind)
            mixed = turner("mixed", tile(u_nat), added("grp"))
            turn_first(2, mixed)
            chunks("pool_out", 1, 4, "mixed", hook=behind(2, mixed))
            pe.wait_ge(slot_done, ph["attn_idx"].slot0)
            columns_of("cols1_read", 1)

            def normed1(b):
                pe.wait_ge(ev("normed1"), b // 2 + 1)
                pe.wait_ge(ev("normed1_b"), b // 2 + 1)
            h1 = turner("h1", tile(normed), normed1)
            turn_first(3, h1)
            chunks("attn_idx", 1, 2, "h1", hook=behind(3, h1))
            p = ph["attn_rest"]
            w80 = PROJ1 - KI
            for j in range(2):
                pe.wait_ge(slot_done, p.slot0 + j + 1)
                for tb in range(TB):
                    for k in range(8):
                        kt, t = 8 * j + k, slice(tb * P, (tb + 1) * P)
                        ins = three(rest[tb][:, 0:w80], act_hi[:, kt, t], act_lo[:, kt, t], (p.w0 + j) % SPLIT,
                                    slice(k * w80, (k + 1) * w80), kt == 0, kt == KT - 1)
                ins.then_inc(w_used, 1)

            def turn_index(i, c, n):
                if n == 2:
                    pe.wait_ge(ev("index_in"), 1)
                if 2 <= n < 6:
                    b = n - 2
                    turn_bank(turns["qi"] + b, [proj1[:, tb, QI + (2 * b + k) * P:QI + (2 * b + k + 1) * P]
                                                for k in range(2) for tb in range(TB)])
                elif n == 6:
                    turn_bank(turns["ki"], [ki_twice[:, tb, :] for tb in range(TB)])

            def index_heads(i, c, n):
                k = (c - 1) * 8 + n
                if k == 0:
                    pe.wait_ge(turn_done, turns["ki"] + 1)
                    pe.wait_ge(ev("rest_read"), 1)
                if k % 3 == 0:
                    for h in (k // 3 * 2, k // 3 * 2 + 1):
                        wait(pe, i_relu, h - 1)
                        r = slice(h % 2 * ID, (h % 2 + 1) * ID)
                        M(rest[h % 2][:, 0:P], qiT[r, h // 2, 0:P], kiT[r, 0:P], start=True, stop=True)
                        M(rest[h % 2][:, P:384], qiT[r, h // 2, P:T], kiT[r, :], start=True, stop=True).then_inc(
                            i_full, 1)

            def index_read(i, c, n):
                if c == 0 and n == 0:
                    pe.wait_ge(i_relu, IH)
            chunks("attn_v", 1, 1, "h1", hook=turn_index)
            chunks("attn_v", 1, 3, "h1", c0=1, hook=index_heads)
            chunks("attn_qk", 1, 2, "h1", hook=hooks(index_read, sum_row("gate1", ph["attn_qk"].slot0)))

            def attend(t, r):
                if runs(t - 1):
                    wait(pe, qk_ready, t)
                    wait(pe, s_read, t - 1)
                    if isinstance(t, int) and t == 1:
                        pe.wait_ge(ev("gate1_row"), 4)
                    q, k = headT[:, 0, :], headT[:, 1, :]
                    M(rest[0][:, 0:P], q[:, 0:P], k[:, 0:P], start=True, stop=True)
                    M(rest[0][:, P:384], q[:, P:T], k, start=True, stop=True).then_inc(s_full, 1)
                if runs(t - 2):
                    wait(pe, p_ready, t - 1)
                    wait(pe, pt_ready, t - 2)
                    for n in range(3):
                        ins = nc.tensor.transpose(turn[1][:, n * P:(n + 1) * P], prob[:, n * P:(n + 1) * P], ident)
                    ins.then_inc(pt_full, 1)
                if runs(t - 3):
                    wait(pe, pt_ready, t - 2)
                    wait(pe, o_done, t - 3)
                    v = [proj1[:, tb, bass.ds(t * P + (V1 - 3 * P), P)] for tb in range(TB)]
                    o = rest[1]
                    M(o[:, 0:P], probT[:, 0:P], v[0], start=True, stop=True)
                    M(o[:, P:T], probT[:, P:2 * P], v[0], start=True, stop=False)
                    M(o[:, P:T], probT[:, 2 * P:384], v[1], start=False, stop=True).then_inc(o_full, 1)
                if runs(t):
                    pe.wait_ge(in_ready, t + 1)
                    wait(pe, qk_ready, t)
                    for n in range(4):
                        ins = nc.tensor.transpose(turn[0][:, n * P:(n + 1) * P], head_in[:, n // 2, n % 2, :], ident)
                    ins.then_inc(qk_full, 1)
            chunks("attn_qk", 1, 6, "h1", c0=2, hook=at_heads(-5, (0, attend)))
            chunks("attn_gate", 1, 4, "h1", hook=at_heads(11, (0, attend)))
            pe.wait_ge(o_done, HEADS)

            def gated(b):
                pe.wait_ge(ev("o_gated"), min(b // 2 + 1, 3))
                if b == 6:
                    pe.wait_ge(ev("o_last"), 1)
            o1 = turner("o1", tile(proj1), gated)
            turn_first(2, o1)
            h2 = turner("h2", tile(x), added("attn_out"))
            chunks("attn_out", 1, 4, "o1", hook=hooks(behind(2, o1), streamed(0, h2)), split_acts=(o1_hi, o1_lo))
            chunks("in_uv", 1, 4, "h2", hook=last_two(0, h2))
            chunks("in_qkv", 3, 2, "h2")

            def turn_ws(i, c, n):
                if c == 0 and n == 1:
                    pe.wait_ge(ev("w_s_low"), 1)
                    for b in range(2):
                        for g in range(4):
                            ins = nc.tensor.transpose(rest[b][:, g * P:(g + 1) * P], w_s[:, 4 * b + g, :], ident)
                        ins.then_inc(ev("ws_turned"), 1)

            def mix_spatial(i, c, n):
                if c == 2 and n == 0:
                    pe.wait_ge(ev("w_sT"), 2)
                    pe.wait_ge(ev("sgu_in"), 2)
                    pe.wait_ge(turn_done, turns["y2"])
                if c == 2 and n in (0, 2):
                    for m in (n, n + 1):
                        wait(pe, ev("sgu_read"), m - 1)
                        tb, g0 = m // 2, m % 2 * 4
                        for g in range(g0, g0 + 4):
                            ins = M(mixes[m % 2][:, (g - g0) * P:(g - g0 + 1) * P], w_sT[:, g, :],
                                    proj2[:, tb, S2 + g * P:S2 + (g + 1) * P], start=True, stop=True)
                        ins.then_inc(ev("sgu_full"), 1)

            def stick(t, r):
                if runs(t - 1, SBH):
                    wait(pe, qk2_ready, t)
                    wait(pe, z_read, t - 1)
                    q, k = headT2[:, 0, :], headT2[:, 1, :]
                    M(rest[0][:, 0:T], k[:, 0:P], q, start=True, stop=True)
                    M(rest[0][:, T:384], k[:, P:T], q[:, P:T], start=True, stop=True).then_inc(z_full, 1)
                if runs(t - 2, SBH):
                    pe.wait_ge(b_miss, t - 1)
                    wait(pe, b_arg, t - 2)
                    if t == 2:
                        pe.wait_ge(ev("sgu_read"), 4)
                    tail = turn[1]
                    M(tail[:, 0:T], later, sb_miss[:, 0:T], start=True, stop=False)
                    M(tail[:, P:T], ones, sb_miss[:, T:384], start=False, stop=True)
                    M(tail[:, T:384], later, sb_miss[:, T:384], start=True, stop=True).then_inc(b_tail, 1)
                if runs(t - 3, SBH):
                    pe.wait_ge(b_mask, t - 2)
                    wait(pe, y_done, t - 3)
                    v = [proj2[:, tb, bass.ds(t * P + (V2 - 3 * P), P)] for tb in range(TB)]
                    y = rest[1]
                    M(y[:, 0:P], sb_w[:, 0:P], v[0], start=True, stop=True)
                    M(y[:, P:T], sb_w[:, P:T], v[0], start=True, stop=False)
                    M(y[:, P:T], sb_w[:, T:384], v[1], start=False, stop=True).then_inc(y_full, 1)
                if runs(t, SBH):
                    pe.wait_ge(in2_ready, t + 1)
                    wait(pe, qk2_ready, t)
                    for n in range(4):
                        ins = nc.tensor.transpose(turn[0][:, n * P:(n + 1) * P], head_in2[:, n // 2, n % 2, :], ident)
                    ins.then_inc(qk2_full, 1)
            heads2 = at_heads(-5, (0, stick))

            def spatial_and_heads(i, c, n):
                mix_spatial(i, c, n)
                heads2(i, c, n)
            chunks("in_gates", 1, 2, "h2", hook=turn_ws)
            chunks("in_gates", 1, 6, "h2", c0=2, hook=spatial_and_heads)

            def y_b_done(b):
                if b == 4:
                    pe.wait_ge(y_done, SBH)
            y2 = turner("y2", lambda tb, kt: proj2[:, tb, (kt * P if kt < 8 else Q2 + kt * P - 1024):][:, 0:P], y_b_done)

            def y2_behind(i, c, n):
                if 4 * c + n < 6:
                    y2(4 * c + n + 2)

            def merged_behind(i, c, n):
                if (c, n) in ((2, 3), (3, 1)):
                    b = c - 2
                    pe.wait_ge(pair_read[1], ph["up"].chunk0 // 2 + 1 + i)
                    turn_bank(turns["merged"] + b,
                              [proj2[:, tb, GA + i * N + (2 * b + k) * P:][:, 0:P]
                               for k in range(2) for tb in range(TB)], i, 2)
            turn_first(2, y2)
            p = ph["up"]

            def up(i, c0, hook):
                chunk(p, c0, i, 2, range(8), turns["y2"], hook)
                chunk(p, c0 + 1, i, 2, range(8, 16), turns["y2"], hook)
            up(0, 0, y2_behind)
            for i in range(3):
                up(i, 2, merged_behind)

            def merged_read(b):
                pe.wait_ge(pair_read[1], p.chunk0 // 2 + 4)
            merged = turner("merged", lambda tb, kt: proj2[:, tb, GA + kt * P:GA + (kt + 1) * P], merged_read)
            h3 = turner("h3", tile(x), added("w_o"))
            chunks("w_o", 1, 4, "merged", hook=hooks(last_two(0, merged), streamed(0, h3)),
                   split_acts=(merged_hi, merged_lo))
            p = ph["ffn_in"]

            def turn_hid(j):
                pe.wait_ge(hid_ready, j + 1)
                for b in range(2):
                    turn_bank(turns["hid"] + b, [hid[:, tb, (2 * b + k) * P:(2 * b + k + 1) * P]
                                                 for k in range(2) for tb in range(TB)], j, 2)

            def ffn_in(j, first):
                for q in range(2):
                    if not first:
                        pe.wait_ge((gate_ready, hid_ready)[q], j)
                    ffn_chunk(j, q)
                    if q == 0 and not first:
                        turn_hid(j - 1)

            def ffn_chunk(j, q):
                for n in range(8):
                    pe.wait_ge(slot_done, p.slot0 + q * 8 + n + 1 + j * 16)
                    for k in range(2):
                        kt = 2 * n + k
                        if k == 0:
                            pe.wait_ge(turn_done, turns["h3"] + n + 1)
                        for tb in range(TB):
                            t = slice(tb * P, (tb + 1) * P)
                            ins = three(acc[q][tb], act_hi[:, kt, t], act_lo[:, kt, t], (p.w0 + n) % SPLIT,
                                        slice(k * N, (k + 1) * N), kt == 0, kt == KT - 1)
                    ins.then_inc(w_used, 1)
                    if isinstance(j, int):
                        last_two(0, h3)(0, q, n)

            for q in range(2):
                pe.wait_ge(pair_read[q], p.chunk0 // 2)
            ffn_in(0, True)
            with pe.Fori(1, 11) as j:
                ffn_in(j, False)
            turn_hid(10)
            p = ph["ffn_out"]
            pe.wait_ge(turn_done, turns["h4"])

            def ffn_out(i, first, last):
                for q in range(2):
                    pe.wait_ge(hid_copied, i * 2 + (q + 1))
                    for j in range(2):
                        pe.wait_ge(slot_done, p.slot0 + 2 * q + j + 1 + i * 4)
                        w0 = p.w0 + 2 * q + j
                        for tb in range(TB):
                            hi, lo = (hid_at[:, q, k, tb * P:(tb + 1) * P] for k in range(2))
                            for n in range(2):
                                ins = three(ps[:, 4 * tb + 2 * j + n], hi, lo, w0 % SPLIT,
                                            slice(n * N, (n + 1) * N), first and q == 0, last and q == 1)
                        ins.then_inc(w_used, 1)
            ffn_out(0, True, False)
            with pe.Fori(1, HKT // 2 - 1) as i:
                ffn_out(i, False, False)
            ffn_out(HKT // 2 - 1, False, True)

            def x5_columns(b):
                pe.wait_ge(ev("x5_cols"), (3, 4, 6, 8)[b // 2])
            h4 = turner("h4", tile(x), x5_columns)
            turn_first(2, h4)
            pe.wait_ge(ev("x5_cols"), 4)
            h4_behind = behind(2, h4)
            p = ph["ple_in"]
            for c in range(4):
                for q in range(2):
                    pe.wait_ge(pair_read[q], pairs_before + c)
                    for n in range(8 if q == 0 else 1):
                        s = 9 * c + (n if q == 0 else 8)
                        pe.wait_ge(slot_done, p.slot0 + s + 1)
                        for k in range(2):
                            kt = 2 * n + k
                            if k == 0:
                                pe.wait_ge(turn_done, (turns["h4"] + n + 1) if q == 0 else turns["p"] + 1)
                            hi, lo = (act_hi, act_lo) if q == 0 else (pT_hi, pT_lo)
                            for tb in range(TB):
                                t = slice(tb * P, (tb + 1) * P)
                                ins = three(acc[q][tb], hi[:, kt, t], lo[:, kt, t], (p.w0 + s) % SPLIT,
                                            slice(k * N, (k + 1) * N), kt == 0, kt == (KT - 1 if q == 0 else 1))
                        ins.then_inc(w_used, 1)
                        if c == 0 and q == 0:
                            h4_behind(0, 0, n)
                            if n == 6:
                                pe.wait_ge(ev("p_in"), 16)
                                turn_bank(turns["p"], [p_nat[:, tb, k * P:(k + 1) * P]
                                                       for k in range(2) for tb in range(TB)])



_INS = ["x", "c", "positions", "norm_g", "mod_w", "mod_b", "pool_w_in", "pool_w_grp", "pool_scale", "pool_w_out",
        "attn_w_in", "attn_w_out", "final_g", "p_2", "attn_norm_g_2", "w_in_2", "sgu_norm_g_2", "w_s_2", "b_s_2",
        "q_norm_g_2", "k_norm_g_2", "w_up_a_2", "w_up_b_2", "w_o_2", "ffn_norm_g_2", "w_ffn_in_2",
        "w_ffn_out_2", "ple_norm_g_2", "w_ple_gate_2", "w_ple_2"]


def tables():
    r, c = np.arange(P)[:, None], np.arange(P)[None, :]
    zero, one = np.zeros((P, P)), np.ones((P, P))
    low = np.where(c <= r, 0.0, LOW)
    before = (r < c) * 1.0
    hidden = np.concatenate([low, zero, low], 1)
    strict = np.concatenate([before, one, before], 1)
    theta = 500000.0
    freq = np.concatenate([np.float32(theta) ** (-np.arange(rot // 2, dtype=np.float32) * 2.0 / rot)
                           for rot in (ROT, IROT)])
    const = np.concatenate([np.eye(P), one, (r > c) * 1.0, hidden, strict, -strict,
                            np.broadcast_to(freq, (P, HALVES))], 1).astype(np.float32)
    s, t = np.arange(T)[:, None], np.arange(T)[None, :]
    mix = [((s <= t) & (s > t - w)) / np.minimum(t + 1, w) - (s == t) for w in (2, 4, 8, 16)]
    mix = np.stack(mix).astype(np.float32).reshape(4, TB, P, T).transpose(2, 1, 0, 3)
    return np.ascontiguousarray(const), np.ascontiguousarray(mix)


def kernel(**inputs):
    import concourse.bacc as _bacc
    from concourse.bass_utils import run_bass_kernel_spmd as _run

    nc = _bacc.Bacc("TRN2", target_bir_lowering=False, num_devices=1)
    arrays, args = {}, []
    const, mix = tables()
    for name, a in [(n, inputs[n]) for n in _INS] + [("const", const), ("pool_mix", mix)]:
        a = np.ascontiguousarray(a)
        arrays[f"in_{name}"] = a
        args.append(nc.dram_tensor(f"in_{name}", a.shape, mybir.dt.from_np(a.dtype), kind="ExternalInput").ap())
    out = nc.dram_tensor("out_0", (1, T, D), F32, kind="ExternalOutput").ap()
    build(nc, *args, out)
    r = _run(nc, [arrays], core_ids=[0])
    return r.results[0]["out_0"]
```

```python
import numpy as np

import concourse.bass as bass
from concourse import mybir

F32 = mybir.dt.float32
F32R = mybir.dt.float32r
I32 = mybir.dt.int32
ALU = mybir.AluOpType
ACT = mybir.ActivationFunctionType
AX_X = mybir.AxisListType.X

P = 128
T = 256
TB = T // P
D = 2048
KT = D // P
N = 512
SLOT = 1024
RAW = 4
SPLIT = 4
EPS = 1e-6
HEADS, HD = 16, 128
IH, ID = 16, 64
ROT, IROT = HD // 4, ID // 4
HALVES = ROT // 2 + IROT // 2
TOPK = 64
SBH = 8
SGU = 8
HID = 5632
HKT = HID // P
LOW = -3.0e38
TAKEN = -3.4e38
X5_ORDER = ((0, 0), (1, 0), (1, 2), (1, 3), (0, 1), (1, 1), (0, 2), (0, 3))
X5_BANK = ((0, 1, 2, 3), (6, 7, 4, 5))
TWO_PI = 2 * np.pi
PI_IN = 3.1415925
TWO_PI_PARTS = (6.28125, 1.93500518798828125e-3, 3.019915981e-7)
ROUND = 1.5 * 2.0 ** 23

Q1, K1, V1, G1, QI, KI, WI, PROJ1 = 0, 2048, 4096, 6144, 8192, 9216, 9280, 9296
U2, S2, Q2, K2, V2, GA, GB, PROJ2 = 0, 1024, 2048, 3072, 4096, 5120, 7168, 9216

PHASES = [
    ("mod0", 16, "MMMM"),
    ("pool_v", 4, ("WWWWMMMWMMMWMMMWMMMW",) + ("WMWMWMWMWMWMWMW",) * 3),
    ("pool_g", 4, "WMWMWMWMWMWMWW"),
    ("grp", 4, "WMMWM"),
    ("pool_out", 4, ("WMWMWMWMWMWMWMW",) * 3 + ("WMWMWMWMWMWMWW",)),
    ("attn_idx", 2, "WWWWWMMMWMMWMMWM"),
    ("attn_rest", 1, "WW"),
    ("attn_v", 4, "WWWWWMWMWMWM"),
    ("attn_qk", 8, "WWWWWWWW"),
    ("attn_gate", 4, "WWWWWWWW"),
    ("attn_out", 4, "WWWWWWWW"),
    ("in_uv", 4, "WWWWWWWW"),
    ("in_qkv", 6, "WWWWWWWW"),
    ("in_gates", 8, "WWWWWWWW"),
    ("up", 8, "WWWW"),
    ("w_o", 4, "WWWWWWWW"),
    ("ffn_in", 22, "WWWWWWWW"),
    ("ffn_out", 44, "WW"),
    ("ple_in", 4, "WWWWWWWWW"),
]


class Phase:
    def __init__(self, name, chunks, seq, slot0, w0, chunk0):
        self.name, self.chunks = name, chunks
        self.seqs = seq if isinstance(seq, tuple) else (seq,) * chunks
        self.slot0, self.w0, self.chunk0 = slot0, w0, chunk0
        self.starts = [slot0 + sum(map(len, self.seqs[:c])) for c in range(chunks)]
        self.per = len(self.seqs[0])
        self.ws = self.seqs[0].count("W")


def plan():
    phases, slot, w, chunk = {}, 0, 0, 0
    for name, chunks, seq in PHASES:
        p = phases[name] = Phase(name, chunks, seq, slot, w, chunk)
        slot += sum(map(len, p.seqs))
        w += chunks * p.ws
        if name == "ple_in":
            chunk += 2 * chunks
        elif name not in ("mod0", "attn_rest", "ffn_out"):
            chunk += chunks
    return phases


def build(nc, x_in, c, positions, norm_g, mod_w, mod_b, pool_w_in, pool_w_grp, pool_scale, pool_w_out,
          attn_w_in, attn_w_out, final_g, p_in, attn_norm_g, w_in, sgu_norm_g, w_s_in, b_s, q_norm_g,
          k_norm_g, w_up_a, w_up_b, w_o, ffn_norm_g, w_ffn_in, w_ffn_out, ple_norm_g, w_ple_gate, w_ple,
          const_in, pool_mix_in, out):
    ph = plan()
    kinds = "".join("".join(ph[name].seqs) for name, _, _ in PHASES)

    base = (nc.sbuf_base + 63) // 64 * 64
    K = 1024

    def at(name, kib, shape, dt=F32):
        return nc.alloc_sbuf_tensor_at(name, shape, dt, offset=base + int(kib * K))

    x = at("x", 0, [P, TB, D])
    raw = at("raw", 16, [P, RAW, SLOT])
    w_hi = at("w_hi", 32, [P, SPLIT, SLOT], F32R)
    w_lo = at("w_lo", 48, [P, SPLIT, SLOT], F32R)
    act_hi = at("act_hi", 64, [P, KT, T], F32R)
    act_lo = at("act_lo", 80, [P, KT, T], F32R)
    mod_row = at("mod_row", 96, [P, D])
    const = at("const", 104, [P, 3 * P + 3 * 384 + HALVES])
    vec_rows = at("vec_rows", 112, [P, P])
    vec = at("vec", 112.5, [P, P])
    small = at("small", 113, [P, 192])
    WORK = 114
    TMP = WORK + 73
    v_nat = at("v_nat", WORK, [P, TB, D])
    gate_nat = at("gate_nat", WORK + 16, [P, TB, D])
    u_nat = at("u_nat", WORK + 32, [P, TB, D])
    normed = at("normed", WORK + 32, [P, TB, D])
    pool_mix = at("pool_mix", WORK + 48, [P, TB, 4, T])
    mod_acc = at("mod_acc", WORK + 56, [P, 2 * D])
    turned = at("turned", TMP, [P, 2, 2 * T])
    resid = at("resid", TMP + 4, [P, TB, N])
    proj1 = at("proj1", WORK, [P, TB, PROJ1])
    qiT = at("qiT", TMP, [P, IH // 2, T])
    kiT = at("kiT", TMP + 8, [P, T])
    ki_twice = at("ki_twice", TMP + 9, [P, TB, P])
    relu = at("relu", TMP + 10, [P, 2, 384])
    rope_t = at("rope_t", TMP + 13.25, [P, 4, (IH + 1) * IROT // 2])
    rope_a = at("rope_a", TMP + 8, [P, 4, TB, HALVES])
    rope_s = at("rope_s", 110.5, [P, TB, HALVES])
    rope_c = at("rope_c", 110.75, [P, TB, HALVES])
    work = at("work", TMP + 15.5, [P, 384])
    amask = at("amask", TMP + 17, [P, 384])
    logit = at("logit", TMP, [P, 384])
    prob = at("prob", TMP + 1.5, [P, 384])
    probT = at("probT", TMP + 3, [P, 384])
    head_in = at("head_in", TMP + 4.5, [P, 2, TB, P])
    headT = at("headT", TMP + 6.5, [P, 2, T])
    row = at("row", WORK + 64, [P, D])
    o1_hi = at("o1_hi", WORK + 8, [P, KT, T], F32R)
    o1_lo = at("o1_lo", WORK + 44.3125, [P, KT, T], F32R)
    before_gain = at("before_gain", TMP + 8, [P, TB, N])
    junk = at("junk", TMP + 12, [P, TB, N])
    normed2 = at("normed2", WORK, [P, TB, D])
    proj2 = at("proj2", WORK, [P, TB, PROJ2])
    squares = at("squares", TMP, [P, 3072])
    sgu_row = at("sgu_row", TMP + 13, [P, 1024])
    w_s = at("w_s", 96, [P, SGU, P])
    w_sT = at("w_sT", 100, [P, SGU, P])
    sb_abs = at("sb_abs", TMP, [P, 384])
    sb_log = at("sb_log", TMP + 1.5, [P, 384])
    sb_miss = at("sb_miss", TMP + 3, [P, 384])
    head_in2 = at("head_in2", TMP + 4.5, [P, 2, TB, P])
    headT2 = at("headT2", TMP + 6.5, [P, 2, T])
    sb_hit = at("sb_hit", TMP + 8.5, [P, 2, 384])
    sb_w = at("sb_w", TMP + 11.5, [P, 384])
    merged_hi = at("merged_hi", WORK, [P, KT, T], F32R)
    merged_lo = at("merged_lo", WORK + 36, [P, KT, T], F32R)
    hid_hi = at("hid_hi", WORK, [P, HKT, T], F32R)
    hid_lo = at("hid_lo", WORK + 44, [P, HKT, T], F32R)
    hid = at("hid", WORK + 88, [P, TB, N])
    hid_at = at("hid_at", 96, [P, 2, 2, T], F32R)
    pT_hi = at("pT_hi", WORK + 32, [P, 2, T], F32R)
    pT_lo = at("pT_lo", WORK + 34, [P, 2, T], F32R)
    p_nat = at("p_nat", WORK + 36, [P, TB, T])
    ple = at("ple", WORK + 40, [P, TB, N])
    assert (WORK + 92) * K <= nc.sbuf_bytes_remaining

    ident, ones = const[:, 0:P], const[:, P:2 * P]
    later = const[:, 2 * P:3 * P]
    o = 3 * P
    hidden = const[:, o:o + 384]
    strict = const[:, o + 384:o + 768]
    nstrict = const[:, o + 768:o + 1152]
    freq = const[:, o + 1152:o + 1152 + HALVES]
    norm0, norm1, pscale, anorm, fnorm, pnorm, ccol = (vec[:, 16 * i:16 * i + 16] for i in range(7))
    qg, kg, bs = vec[:, 112:113], vec[:, 113:114], vec[:, 114:122]
    cond = small[:, 0:16]
    shift, scale1 = small[:, 16:32], small[:, 32:48]
    sumsq, rstd = small[:, 48:50], small[:, 50:52]
    pos = small[:, 52:54]
    rfinal, rnext, sumnext = small[:, 54:56], small[:, 70:72], small[:, 72:74]
    colsum = small[:, 96:112]
    best = small[:, 56:64]
    qgs = small[:, 80:81]
    top, ntop, rden = (small[:, 64 + 2 * i:66 + 2 * i] for i in range(3))
    den = small[:, 84:92]
    ssq2, rs2 = small[:, 96:144], small[:, 144:192]
    newton = at("newton", 111, [P, 2, 24])
    pos_i = at("pos_i", 113.875, [P, TB], I32)

    ps = nc.alloc_psum_tensor("ps", [P, 8, N], F32)
    acc = [[ps[:, 0], ps[:, 1]], [ps[:, 2], ps[:, 3]]]
    turn = [ps[:, 4], ps[:, 5]]
    rest = [ps[:, 6], ps[:, 7]]
    mixes = [turn[1], rest[1]]

    def sem(name):
        return nc.alloc_semaphore(name)

    loaded = [sem(f"loaded{i}") for i in range(RAW)]
    hi_ready = sem("hi_ready")
    slot_done = sem("slot_done")
    w_used = sem("w_used")
    pair_read = [sem("pair_read0"), sem("pair_read1")]
    turn_full = sem("turn_full")
    turn_affine = sem("turn_affine")
    turn_hi = sem("turn_hi")
    turn_done = sem("turn_done")
    rope_mul, rope_add = sem("rope_mul"), sem("rope_add")
    in_ready, qk_full, qk_ready = map(sem, ("in_ready", "qk_full", "qk_ready"))
    s_full, s_read, l_max, l_ready, p_ready = map(sem, ("s_full", "s_read", "l_max", "l_ready", "p_ready"))
    pt_full, pt_ready, o_full, r_ready, o_done = map(sem, ("pt_full", "pt_ready", "o_full", "r_ready", "o_done"))
    z_full, z_read, b_abs, b_log, b_sum, b_miss = map(sem, ("z_full", "z_read", "b_abs", "b_log", "b_sum", "b_miss"))
    b_tail, b_arg, b_w, b_mask, y_full, y_done = map(sem, ("b_tail", "b_arg", "b_w", "b_mask", "y_full", "y_done"))
    i_full, i_relu, i_done = map(sem, ("i_full", "i_relu", "i_done"))
    hid_copied = sem("hid_copied")
    in2_ready, qk2_full, qk2_ready = map(sem, ("in2_ready", "qk2_full", "qk2_ready"))
    gate_ready = sem("gate_ready")
    hid_ready = sem("hid_ready")
    act_chain, dve_chain = sem("act_chain"), sem("dve_chain")
    stored = sem("stored")
    events = {}

    def ev(name):
        if name not in events:
            events[name] = sem(name)
        return events[name]

    def wait(eng, s, value):
        if not (isinstance(value, int) and value <= 0):
            eng.wait_ge(s, value)

    def repeat(eng, n, body):
        if n == 1:
            body(0)
        elif n > 1:
            with eng.Fori(0, n) as i:
                body(i)

    def runs(t, heads=HEADS):
        return not isinstance(t, int) or 0 <= t < heads

    def at_heads(first, *steps):
        def hook(i, c, j):
            for where, step in steps:
                if j % 4 == where:
                    k = 2 * c + j // 4
                    step(i * 4 + (first + k), k % 4)
        return hook

    w_slots = [s for s, k in enumerate(kinds) if k == "W"]
    m_slots = [s for s, k in enumerate(kinds) if k == "M"]
    m_holds = [(layer, kt, col) for layer in range(2) for cols in ((0, 1, 2, 3), (4, 5))
               for col in cols for kt in range(KT)]
    assert len(m_holds) == len(m_slots)
    m_of = {s: (layer, kt, col * SLOT) for s, (layer, kt, col) in zip(m_slots, m_holds)}
    ends = {(layer, row): m_slots[96 * layer + (96 if row else 64) - 1] + 1 for layer in range(2) for row in (0, 1)}

    turns, n_turns = {}, 0
    for name, banks in (("h0", 8), ("pooled", 8), ("mixed", 8), ("h1", 8), ("qi", 4), ("ki", 1),
                        ("o1", 8), ("h2", 8), ("y2", 8), ("merged", 8), ("h3", 8), ("hid", 22),
                        ("h4", 8), ("p", 1)):
        turns[name] = n_turns
        n_turns += banks

    def behind(lead, step):
        def hook(i, c, j):
            if c == 0 and j + lead < 8:
                step(j + lead)
        return hook

    def placed(step, bank, *places):
        def hook(i, c, j):
            if (c, j) in places:
                step(bank + places.index((c, j)))
        return hook

    def hooks(*several):
        def hook(i, c, j):
            for h in several:
                h(i, c, j)
        return hook

    def streamed(offset, step, c0=0):
        def hook(i, c, j):
            if c > c0 and j - offset in (2, 4):
                step(2 * (c - 1) + (j - offset) // 4)
        return hook

    def last_two(offset, step):
        def hook(i, c, j):
            if c == 0 and j - offset in (2, 4):
                step(6 + (j - offset) // 4)
        return hook

    def columns_read(eng, p, c):
        eng.wait_ge(pair_read[c % 2], (p.chunk0 + c) // 2 + 1)

    def raw2(r, nk=2, cols=N):
        return raw[:, r, 0:nk * cols].rearrange("p (k n) -> p k n", k=nk)

    x_t = x_in.rearrange("b (t p) d -> p (b t) d", p=P)
    out_t = out.rearrange("b (t p) d -> p (b t) d", p=P)
    pairs_before = ph["ffn_in"].chunk0 // 2
    by_channel = lambda v: v.rearrange("l (k c) -> (l k) c", c=P)
    vec_sources = [by_channel(v) for v in (norm_g, pool_scale, attn_norm_g, ffn_norm_g, ple_norm_g, c, q_norm_g,
                                           k_norm_g)] + [b_s[0]]

    with nc.Block() as block:
        @block.sync
        def _(sp):
            def load(s0, n, i, src, shape=None):
                r = s0 % RAW
                wait(sp, slot_done, s0 - RAW + 1 + i * n)
                dst = raw[:, r, :] if shape is None else raw2(r, *shape)
                sp.dma_start(dst, src).then_inc(loaded[r], 16)

            def rows(w, k0, nk, col, cols):
                return w[bass.ds(k0 * P, nk * P), bass.ds(col, cols)].rearrange("(k p) n -> p k n", p=P)

            def product(name, w, bodies, per, col0=0, col=lambda i, q, per: (i * per + q) * N):
                p = ph[name]

                def body(i):
                    for q in range(per):
                        k = 0
                        for j, kind in enumerate(p.seqs[q]):
                            s0 = p.starts[q] + j
                            if kind == "W":
                                src = rows(w, k, 2, col(i, q, per) + col0, N)
                                load(s0, per * p.per, i, src, (2, N))
                                k += 2
                            else:
                                load(s0, 0, 0, mod_rows(*m_of[s0]))
                repeat(sp, bodies, body)

            def mod_rows(layer, kt, col):
                return mod_w[layer, bass.ds(kt * P, P), bass.ds(col, SLOT)]

            for col in range(4):
                def mod0(i):
                    for j in range(4):
                        load(KT * col + j, 4, i, mod_rows(0, i * 4 + j, col * SLOT))
                if col == 0:
                    mod0(0)
                with sp.Fori(1 if col == 0 else 0, KT // 4) as i:
                    mod0(i)
            product("pool_v", pool_w_in[0], 1, 4)
            product("pool_g", pool_w_in[0], 1, 4, D)
            p = ph["grp"]
            for g in range(4):
                k = 0
                for j, kind in enumerate(p.seqs[g]):
                    s0 = p.starts[g] + j
                    if kind == "W":
                        load(s0, 0, 0, rows(pool_w_grp[0, g], k, 2, 0, N), (2, N))
                        k += 2
                    else:
                        load(s0, 0, 0, mod_rows(*m_of[s0]))
            product("pool_out", pool_w_out[0], 1, 4)
            product("attn_idx", attn_w_in[0], 1, 2, QI)
            w80 = PROJ1 - KI
            for j in range(2):
                load(ph["attn_rest"].slot0 + j, 0, 0, rows(attn_w_in[0], 8 * j, 8, KI, w80), (8, w80))
            product("attn_v", attn_w_in[0], 1, 4, V1)
            product("attn_qk", attn_w_in[0], 4, 2, Q1, col=lambda i, q, per: i * N + q * K1)
            product("attn_gate", attn_w_in[0], 2, 2, G1)
            product("attn_out", attn_w_out[0], 2, 2)
            product("in_uv", w_in[0], 2, 2)
            product("in_qkv", w_in[0], 3, 2, 4 * N)
            product("in_gates", w_in[0], 4, 2, 10 * N)
            p = ph["up"]

            def up(i):
                for q, w in enumerate((w_up_a, w_up_b)):
                    for j in range(4):
                        load(p.slot0 + 4 * q + j, 8, i, rows(w[0], 2 * j, 2, i * N, N), (2, N))
            repeat(sp, 4, up)
            product("w_o", w_o[0], 2, 2)
            p = ph["ffn_in"]

            def ffn_in(i):
                for q in range(2):
                    for j in range(8):
                        load(p.slot0 + 8 * q + j, 16, i, rows(w_ffn_in[0], 2 * j, 2, i * N + q * HID, N), (2, N))
            repeat(sp, 11, ffn_in)
            p = ph["ffn_out"]

            def ffn_out(i):
                for q in range(2):
                    for j in range(2):
                        load(p.slot0 + 2 * q + j, 4, i,
                             w_ffn_out[0, bass.ds((i * 2 + q) * P, P), j * SLOT:(j + 1) * SLOT])
            repeat(sp, HKT // 2, ffn_out)
            p = ph["ple_in"]
            for c in range(4):
                for j in range(9):
                    w, k = (w_ple_gate[0], 2 * j) if j < 8 else (w_ple[0], 0)
                    load(p.slot0 + 9 * c + j, 0, 0, rows(w, k, 2, c * N, N), (2, N))
            for c in range(4):
                sp.wait_ge(ev("x_final"), c + 1)
                sp.dma_start(out_t[:, :, c * N:(c + 1) * N], x[:, :, c * N:(c + 1) * N]).then_inc(stored, 16)
            sp.wait_ge(stored, 64)

        @block.gpsimd
        def _(pool):
            def row_start(buf, width, src, name):
                pool.memset(buf, 0.0).then_inc(ev(name + "_zero"), 1)
                pool.wait_ge(ev(name + "_zero"), 1)
                pool.dma_start(buf[0:1, :], src).then_inc(ev(name), 16)

            b0, b1 = mod_b[0:1, :], mod_b[1:2, :]
            row_start(mod_acc[:, :], 2 * D, b0[:, 0:2 * D], "acc0_start")
            row_start(mod_row[:, :], D, b0[:, 2 * D:3 * D], "row0_start")
            pool.wait_ge(ev("cols0_read"), 1)
            row_start(mod_acc[:, :], 2 * D, b1[:, 0:2 * D], "acc1_start")
            pool.wait_ge(ev("x1_done"), 1)
            row_start(mod_row[:, :], D, b1[:, 2 * D:3 * D], "row1_start")
            pool.wait_ge(ev("masked"), 1)

            def copy_heads(i):
                pool.wait_ge(rope_add, i * 4 + 6)
                for r in range(4):
                    wait(pool, qk_full, i * 4 + r)
                    for k in range(2):
                        ins = pool.tensor_copy(head_in[:, k, :, :], proj1[:, :, bass.ds(i * 4 * P + (r * P + k * K1), P)])
                    ins.then_inc(in_ready, 1)
            copy_heads(0)
            with pool.Fori(1, HEADS // 4) as i:
                copy_heads(i)
            for n in range(3):
                pool.wait_ge(o_done, 4 * n + 4)
                pool.wait_ge(pair_read[n % 2], (ph["attn_gate"].chunk0 + n) // 2 + 1)
                cols = slice(n * N, (n + 1) * N)
                pool.tensor_tensor(proj1[:, :, cols], proj1[:, :, cols], proj1[:, :, G1 + n * N:G1 + (n + 1) * N],
                                   ALU.mult).then_inc(ev("o_gated"), 1)
            pool.wait_ge(ev("o_gated"), 3)
            pool.wait_ge(ev("o_last"), 1)
            pool.dma_start(row[:, :], final_g.rearrange("(a d) -> a d", a=1).partition_broadcast(P)).then_inc(
                ev("final_row"), 16)
            pool.wait_ge(ev("x2_done"), 1)
            pool.wait_ge(ev("sq2"), 8)
            pool.dma_start(w_s[:, :, :], w_s_in[0].rearrange("g t s -> t g s")).then_inc(ev("w_s_in"), 16)
            pool.wait_ge(ev("w_s_in"), 16)
            pool.affine_select(out=w_s[:, :, :], in_=w_s[:, :, :], compare_op=ALU.is_ge, fill=0.0, base=0,
                               pattern=[[0, SGU], [-1, P]], channel_multiplier=1).then_inc(ev("w_s_low"), 1)
            pool.dma_start(sgu_row[:, :], sgu_norm_g.rearrange("a g c -> a (g c)").partition_broadcast(P)).then_inc(
                ev("sgu_row"), 16)
            pool.wait_ge(ev("qk_normed"), 2)

            def copy_head2(t):
                wait(pool, qk2_full, t)
                for k in range(2):
                    ins = pool.tensor_copy(head_in2[:, k, :, :], proj2[:, :, bass.ds(t * P + (Q2, K2)[k], P)])
                ins.then_inc(in2_ready, 1)
            copy_head2(0)
            with pool.Fori(1, SBH) as t:
                copy_head2(t)

            def hid_copy(i, first=False):
                for q in range(2):
                    kt = i * 2 + q
                    if not first:
                        pool.wait_ge(w_used, ph["ffn_out"].w0 + 2 * q - 2 + i * 4)
                    pool.tensor_copy(hid_at[:, q, 0, :], hid_hi[:, bass.ds(kt, 1), :].rearrange(
                        "p a t -> p (a t)").bitcast(F32))
                    pool.tensor_copy(hid_at[:, q, 1, :], hid_lo[:, bass.ds(kt, 1), :].rearrange(
                        "p a t -> p (a t)").bitcast(F32)).then_inc(hid_copied, 1)
            pool.wait_ge(turn_done, turns["hid"] + 2)
            hid_copy(0, True)
            pool.wait_ge(turn_done, turns["h4"])
            with pool.Fori(1, HKT // 2) as i:
                hid_copy(i)
            pool.wait_ge(ev("x5_cols"), 8)
            pool.dma_start(p_nat[:, :, :], p_in[0].rearrange("b (t q) c -> q (b t) c", q=P)).then_inc(ev("p_in"), 16)

        @block.scalar
        def _(act):
            pos_w = [0]
            links = [0]

            def link(ins):
                links[0] += 1
                ins.then_inc(act_chain, 1)
                act.wait_ge(act_chain, links[0])

            def round_w(w0, i=0, nw=0, ns=0):
                s0 = w_slots[w0]
                act.wait_ge(loaded[s0 % RAW], 16 * (s0 // RAW + 1) + i * (16 * (ns // RAW)))
                wait(act, w_used, w0 - SPLIT + 1 + i * nw)
                nc.scalar.copy(w_hi[:, w0 % SPLIT, :], raw[:, s0 % RAW, :]).then_inc(hi_ready, 1)

            def advance(to):
                while pos_w[0] < min(to, len(w_slots)):
                    round_w(pos_w[0])
                    pos_w[0] += 1

            def chunks(name, bodies, per, read=None, c0=0, hook=None):
                p = ph[name]
                assert pos_w[0] == p.w0 + c0 * p.ws + 4, name

                def body(i):
                    for q in range(per):
                        for j in range(p.ws):
                            round_w(p.w0 + 4 + (c0 + q) * p.ws + j, i, per * p.ws, per * p.per)
                            if hook:
                                hook(i, c0 + q, j)
                        if read:
                            read(i, c0 + q, per)
                repeat(act, bodies, body)
                pos_w[0] += bodies * per * p.ws

            def read_pair(p, func, dst, col=lambda i, q, per: (i * per + q) * N, scaled=None):
                def read(i, q, per):
                    c = p.chunk0 + q
                    if scaled:
                        act.wait_ge(ev(scaled), 1)
                    act.wait_ge(w_used, p.w0 + (q + 1) * p.ws + i * (per * p.ws))
                    for tb in range(TB):
                        ins = nc.scalar.activation(dst(tb, col(i, q, per)), acc[c % 2][tb], func,
                                                   scale=rstd[:, tb:tb + 1] if scaled else 1.0)
                    ins.then_inc(pair_read[c % 2], 1)
                return read

            def turn_hi_of(name, banks, hi, source="plain", scale=None, at_bank=0):
                for b in range(at_bank, at_bank + banks):
                    g = turns[name] + b
                    act.wait_ge(turn_full, g + 1)
                    src = turn[g % 2]
                    if source == "half":
                        nc.scalar.activation(hi(b), src[:, 0:T], ACT.Copy,
                                             scale=1.0 if scale is None else scale(b)).then_inc(turn_hi, 1)
                    elif source == "affine":
                        for k in range(2):
                            ct = 2 * b + k
                            ins = nc.scalar.activation(hi[:, ct, :], src[:, k * T:(k + 1) * T], ACT.Identity,
                                                       bias=shift[:, ct:ct + 1], scale=scale1[:, ct:ct + 1])
                        ins.then_inc(turn_hi, 1)
                    elif scale is None:
                        nc.scalar.copy(hi[:, 2 * b:2 * b + 2, :].rearrange("p k t -> p (k t)"), src).then_inc(turn_hi, 1)
                    else:
                        for k in range(2):
                            ins = nc.scalar.activation(hi[:, 2 * b + k, :], src[:, k * T:(k + 1) * T], ACT.Copy,
                                                       scale=scale[:, 2 * b + k:2 * b + k + 1])
                        ins.then_inc(turn_hi, 1)

            def square_sums(scratch, name):
                for tb in range(TB):
                    ins = nc.scalar.activation(scratch[:, tb, :], x[:, tb, :], ACT.Square,
                                               accum_out=sumsq[:, tb:tb + 1])
                ins.then_inc(ev(name), 1)

            def column_squares(p, name, *srcs):
                def step(c):
                    columns_read(act, p, c)
                    for k, src in enumerate(srcs):
                        wait(act, ev(name), c * len(srcs) + k)
                        for tb in range(TB):
                            at_sum = 8 * k + 4 * tb + c
                            ins = nc.scalar.activation(junk[:, tb, :], src(tb, c), ACT.Square,
                                                       accum_out=colsum[:, at_sum:at_sum + 1])
                        ins.then_inc(ev(name), 1)
                return step

            x_cols = lambda tb, c: x[:, tb, c * N:(c + 1) * N]

            def squares_behind(step):
                def hook(i, c, j):
                    if c > 0 and j == 2:
                        step(c - 1)
                return hook

            def last_squares(step):
                def hook(i, c, j):
                    if c == 0 and j == 2:
                        step(3)
                return hook

            def read_row(name, at_chunk=0):
                def hook(i, c, j):
                    if c == at_chunk and j % 2 == 1:
                        row_chunk(name, j // 2)
                return hook

            def row_chunk(name, c):
                act.wait_ge(ev(name + "_full"), c + 1)
                nc.scalar.copy(mod_row[:, c * N:(c + 1) * N], rest[c % 2]).then_inc(ev(name + "_row"), 1)

            at_row = 0
            for src in vec_sources:
                n = src.shape[0]
                act.dma_start(vec_rows[at_row:at_row + n, :], src).then_inc(ev("vec_in"), 16)
                at_row += n
            act.dma_start(pos_i[:, :], positions.rearrange("b (t p) -> p (b t)", p=P),
                          allow_slow_non_contiguous=True).then_inc(ev("vec_in"), 16)
            act.dma_start(const[:, :], const_in).then_inc(ev("const_in"), 16)
            act.dma_start(x[:, :, :], x_t).then_inc(ev("x_in"), 16)
            act.dma_start(pool_mix[:, :, :, :], pool_mix_in).then_inc(ev("mix_in"), 16)

            act.wait_ge(ev("vec"), 1)
            nc.scalar.activation(cond, ccol, ACT.Silu).then_inc(ev("cond"), 1)
            act.wait_ge(ev("angles"), 1)
            nc.scalar.activation(rope_s[:, :, :], rope_a[:, 0, :, :], ACT.Sin)
            nc.scalar.activation(rope_c[:, :, :], rope_a[:, 1, :, :], ACT.Sin).then_inc(ev("rope"), 1)
            act.wait_ge(ev("x_in"), 16)
            square_sums(normed, "sq0")
            act.wait_ge(ev("rstd0"), 1)
            for tb in range(TB):
                nc.scalar.activation(normed[:, tb, :], x[:, tb, :], ACT.Copy, scale=rstd[:, tb:tb + 1]).then_inc(
                    ev("normed0"), 1)
            advance(4)
            affine = lambda name: (lambda b: turn_hi_of(name, 1, act_hi, "affine", at_bank=b))
            plain = lambda name, hi=act_hi, scale=None: (lambda b: turn_hi_of(name, 1, hi, scale=scale, at_bank=b))
            act.wait_ge(ev("shift0"), 1)
            turn_hi_of("h0", 2, act_hi, "affine")
            chunks("pool_v", 1, 4, read_pair(ph["pool_v"], ACT.Copy, lambda tb, col: v_nat[:, tb, bass.ds(col, N)]),
                   hook=behind(2, affine("h0")))
            chunks("pool_g", 1, 4, read_pair(ph["pool_g"], ACT.Silu, lambda tb, col: gate_nat[:, tb, bass.ds(col, N)]),
                   hook=hooks(read_row("gate0", 2), placed(plain("pooled"), 0, *((3, j) for j in range(2, 8)))))
            mixed = plain("mixed", scale=pscale)
            chunks("grp", 1, 4, hook=hooks(placed(plain("pooled"), 6, (0, 1), (1, 0)),
                                           placed(mixed, 0, (2, 0), (2, 1), (3, 0), (3, 1))))
            mixed(4)
            mixed(5)
            squares1 = column_squares(ph["pool_out"], "sq1", x_cols)
            chunks("pool_out", 1, 4, hook=hooks(placed(mixed, 6, (0, 1), (0, 2)), squares_behind(squares1)))
            squares1(3)
            act.wait_ge(ev("rstd1"), 1)
            for c in range(4):
                nc.scalar.activation(normed[:, 1, c * N:(c + 1) * N], x[:, 1, c * N:(c + 1) * N], ACT.Copy,
                                     scale=rstd[:, 1:2]).then_inc(ev("normed1_b"), 1)
            act.wait_ge(ev("shift1"), 1)
            turn_hi_of("h1", 2, act_hi, "affine")
            into1 = lambda c: (lambda tb, col: proj1[:, tb, bass.ds(col + c, N)])
            chunks("attn_idx", 1, 2, read_pair(ph["attn_idx"], ACT.Copy, into1(QI)), hook=behind(2, affine("h1")))
            advance(ph["attn_v"].w0 + 4)
            act.wait_ge(w_used, ph["attn_rest"].w0 + 2)
            nc.scalar.copy(proj1[:, :, KI:PROJ1], ps[:, 6:8, 0:PROJ1 - KI]).then_inc(ev("rest_read"), 1)

            def turn_index(i, c, j):
                if 3 <= j < 7:
                    turn_hi_of("qi", 1, lambda b: qiT[:, 2 * (j - 3), :], "half", at_bank=j - 3)
                elif j == 7:
                    turn_hi_of("ki", 1, lambda b: kiT[:, :], "half")

            def index_heads(i, c, j):
                k = (c - 1) * 8 + j
                if k % 3 == 1:
                    for h in (k // 3 * 2, k // 3 * 2 + 1):
                        act.wait_ge(i_full, h + 1)
                        wait(act, i_done, h - 1)
                        nc.scalar.activation(relu[:, h % 2, :], rest[h % 2][:, 0:384], ACT.Relu).then_inc(i_relu, 1)

            read_v = read_pair(ph["attn_v"], ACT.Copy, into1(V1))
            chunks("attn_v", 1, 1, read_v, hook=turn_index)
            chunks("attn_v", 1, 3, read_v, c0=1, hook=index_heads)
            read_qk = read_pair(ph["attn_qk"], ACT.Copy, into1(Q1),
                                lambda i, q, per: q // 2 * N + q % 2 * K1 + i * (per // 2 * N))
            chunks("attn_qk", 1, 2, read_qk, hook=read_row("gate1"))

            def copies(t, r):
                if runs(t):
                    act.wait_ge(qk_full, t + 1)
                    wait(act, s_full, t)
                    if isinstance(t, int) and t == 0:
                        act.wait_ge(ev("masked"), 1)
                    nc.scalar.copy(headT[:, :, :].rearrange("p k t -> p (k t)"), turn[0]).then_inc(qk_ready, 1)
                if runs(t - 2):
                    wait(act, pt_full, t - 1)
                    wait(act, o_full, t - 2)
                    nc.scalar.copy(probT[:, :], turn[1][:, 0:384]).then_inc(pt_ready, 1)

            def exponentials(t, r):
                if runs(t - 1):
                    wait(act, l_ready, t)
                    wait(act, pt_full, t - 1)
                    wait(act, o_done, t - 4)
                    for tb, (c0, c1) in enumerate(((0, P), (P, 384))):
                        d = 2 * ((r - 1) % 4) + tb
                        ins = nc.scalar.activation(prob[:, c0:c1], logit[:, c0:c1], ACT.Exp,
                                                   bias=ntop[:, tb:tb + 1], accum_out=den[:, d:d + 1])
                    ins.then_inc(p_ready, 1)
            chunks("attn_qk", 1, 6, read_qk, 2, at_heads(-5, (1, copies), (3, exponentials)))
            chunks("attn_gate", 1, 4, read_pair(ph["attn_gate"], ACT.Silu, into1(G1)), 0,
                   hooks(at_heads(11, (1, copies), (3, exponentials)), placed(plain("o1", o1_hi), 0, (3, 5), (3, 6), (3, 7))))
            turn_hi_of("o1", 1, o1_hi, at_bank=3)
            squares2 = column_squares(ph["attn_out"], "sq2", lambda tb, c: before_gain[:, tb, :], x_cols)
            h2 = plain("h2", scale=anorm)
            chunks("attn_out", 1, 4, hook=hooks(behind(4, plain("o1", o1_hi)), squares_behind(squares2), streamed(1, h2)))
            into2 = lambda c: (lambda tb, col: proj2[:, tb, bass.ds(col + c, N)])
            chunks("in_uv", 1, 4, read_pair(ph["in_uv"], ACT.Gelu_apprx_tanh, into2(U2), scaled="rstd2"),
                   hook=hooks(last_squares(squares2), last_two(1, h2)))
            chunks("in_qkv", 3, 2, read_pair(ph["in_qkv"], ACT.Copy, into2(Q2), scaled="rstd2"))

            def square_groups(i, c, j):
                if j == 0:
                    wait(act, ev("squares_sum"), c)
                    nc.scalar.activation(squares[:, :], proj2[:, c, S2:V2], ACT.Square).then_inc(ev("squares"), 1)
                if c == 0 and j == 2:
                    for b in range(2):
                        act.wait_ge(ev("ws_turned"), b + 1)
                        nc.scalar.copy(w_sT[:, 4 * b:4 * b + 4, :].rearrange("p g t -> p (g t)"), rest[b]).then_inc(
                            ev("w_sT"), 1)

            def copies2(t, r):
                if runs(t, SBH):
                    act.wait_ge(qk2_full, t + 1)
                    wait(act, z_full, t)
                    for k, gain in enumerate((qgs, kg)):
                        ins = nc.scalar.activation(headT2[:, k, :], turn[0][:, k * T:(k + 1) * T], ACT.Copy, scale=gain)
                    ins.then_inc(qk2_ready, 1)
                if runs(t - 3, SBH):
                    act.wait_ge(y_full, t - 2)
                    nc.scalar.copy(proj2[:, :, bass.ds(t * P + (Q2 - 3 * P), P)],
                                   rest[1][:, 0:T].rearrange("p (t d) -> p t d", t=TB)).then_inc(y_done, 1)

            def logs(t, r):
                if runs(t - 1, SBH):
                    act.wait_ge(z_full, t)
                    wait(act, b_log, t - 1)
                    nc.scalar.activation(sb_abs[:, :], rest[0][:, 0:384], ACT.Abs).then_inc(b_abs, 1)
                    act.wait_ge(b_abs, t * 2 - 1)
                    nc.scalar.activation(sb_abs[:, :], sb_abs[:, :], ACT.Exp, scale=-1.0).then_inc(b_abs, 1)
                    act.wait_ge(b_abs, t * 2)
                    wait(act, z_read, t - 1)
                    nc.scalar.activation(sb_log[:, :], sb_abs[:, :], ACT.Ln, bias=1.0).then_inc(b_log, 1)

            def weights(t, r):
                if runs(t - 2, SBH):
                    act.wait_ge(b_arg, t - 1)
                    wait(act, y_full, t - 2)
                    nc.scalar.activation(sb_w[:, :], sb_hit[:, t % 2, :], ACT.Exp).then_inc(b_w, 1)
            read_gates = read_pair(ph["in_gates"], ACT.Sigmoid, into2(GA), lambda i, q, per: q * N, "rstd2")
            chunks("in_gates", 1, 2, read_gates, 0, square_groups)
            chunks("in_gates", 1, 6, read_gates, 2, hooks(at_heads(-5, (0, logs), (1, copies2), (3, weights)),
                                                          placed(plain("y2"), 0, (7, 5), (7, 6), (7, 7))))
            turn_hi_of("y2", 1, act_hi, at_bank=3)

            def merged_behind(i, c, j):
                if c == 3 and j in (0, 2):
                    b, g = j // 2, turns["merged"] + j // 2
                    act.wait_ge(turn_full, g + 1 + i * 2)
                    nc.scalar.copy(merged_hi[:, bass.ds(i * 4 + 2 * b, 2), :].rearrange("p k t -> p (k t)"),
                                   turn[g % 2]).then_inc(turn_hi, 1)
            chunks("up", 1, 2, hook=behind(4, plain("y2")))
            chunks("up", 3, 2, c0=2, hook=merged_behind)
            squares4 = column_squares(ph["w_o"], "sq4", x_cols)
            h3 = plain("h3", scale=fnorm)
            chunks("w_o", 1, 4, hook=hooks(last_two(1, plain("merged", merged_hi)), squares_behind(squares4),
                                           streamed(1, h3)))
            p = ph["ffn_in"]

            def hid_hi_of(j):
                for b in range(2):
                    g = turns["hid"] + b
                    act.wait_ge(turn_full, g + 1 + j * 2)
                    nc.scalar.copy(hid_hi[:, bass.ds(j * 4 + 2 * b, 2), :].rearrange("p k t -> p (k t)"),
                                   turn[g % 2]).then_inc(turn_hi, 1)

            def ffn_in(j, first):
                for q in range(2):
                    for k in range(8):
                        round_w(p.w0 + 4 + q * 8 + k, j, 16, 16)
                        if first:
                            hooks(last_squares(squares4), last_two(1, h3))(0, q, k)
                    if q == 0:
                        act.wait_ge(w_used, p.w0 + 8 + j * 16)
                        act.wait_ge(ev("rstd4"), 1)
                        if not first:
                            act.wait_ge(turn_full, turns["hid"] + j * 2)
                        for tb in range(TB):
                            ins = nc.scalar.activation(hid[:, tb, :], acc[0][tb], ACT.Silu, scale=rstd[:, tb:tb + 1])
                        ins.then_inc(gate_ready, 1)
                        if not first:
                            hid_hi_of(j - 1)
            ffn_in(0, True)
            with act.Fori(1, 11) as j:
                ffn_in(j, False)
            hid_hi_of(10)
            pos_w[0] += 22 * 8
            p = ph["ffn_out"]

            def ffn_out(i):
                for j in range(4):
                    round_w(p.w0 + 4 + j, i, 4, 4)
            repeat(act, 22, ffn_out)
            pos_w[0] += 88
            turn_hi_of("h4", 2, act_hi, scale=pnorm)
            p = ph["ple_in"]
            h4 = behind(2, plain("h4", scale=pnorm))
            for c in range(4):
                for j in range(9):
                    advance(p.w0 + 9 * c + 4 + j + 1)
                    if j < 8:
                        h4(0, c, j)
                    if c == 0 and j in (1, 3):
                        act.wait_ge(ev("x5_cols"), 8)
                        tb = j // 2
                        nc.scalar.activation(normed2[:, tb, :], x[:, tb, :], ACT.Square,
                                             accum_out=sumsq[:, tb:tb + 1]).then_inc(ev("sq5"), 1)
                    if c == 0 and j == 7:
                        turn_hi_of("p", 1, pT_hi)
                        act.wait_ge(ev("rstd5"), 1)
                act.wait_ge(w_used, p.w0 + 9 * c + 8)
                wait(act, ev("x_final"), c)
                for tb in range(TB):
                    ins = nc.scalar.activation(ple[:, tb, :], ps[:, 4 * (c % 2) + tb], ACT.Sigmoid, scale=rstd[:, tb:tb + 1])
                ins.then_inc(pair_read[0], 1)

        @block.vector
        def _(dve):
            V = nc.vector
            pos_s = [0]
            links = [0]

            def link(ins):
                links[0] += 1
                ins.then_inc(dve_chain, 1)
                dve.wait_ge(dve_chain, links[0])

            w_of = {}
            for s, k in enumerate(kinds):
                if k == "W":
                    w_of[s] = len(w_of)

            def split(s0, i=0, ns=0, nw=0):
                w0 = w_of[s0]
                dve.wait_ge(hi_ready, w0 + 1 + i * nw)
                V.tensor_tensor(w_lo[:, w0 % SPLIT, :], raw[:, s0 % RAW, :],
                                w_hi[:, w0 % SPLIT, :].bitcast(F32), ALU.subtract).then_inc(slot_done, 1)

            def modulate(s0, i=0, kt=None):
                layer, kt0, col = m_of[s0]
                dve.wait_ge(loaded[s0 % RAW], 16 * (s0 // RAW + 1) + i * 16)
                if kt is not None:
                    dve.wait_ge(slot_done, s0 + i * 4)
                elif kt0 > 0:
                    dve.wait_ge(slot_done, m_slots[m_of_slot(layer, kt0 - 1, col)] + 1)
                elif col in (0, 2 * D):
                    dve.wait_ge(ev(("acc" if col == 0 else "row") + f"{layer}_start"), 16)
                target = mod_acc[:, col:col + SLOT] if col < 2 * D else mod_row[:, col - 2 * D:col - 2 * D + SLOT]
                V.scalar_tensor_tensor(out=target, in0=raw[:, s0 % RAW, :],
                                       scalar=cond[:, bass.ds(kt0 if kt is None else kt, 1)],
                                       in1=target, op0=ALU.mult, op1=ALU.add).then_inc(slot_done, 1)

            def m_of_slot(layer, kt, col):
                return m_holds.index((layer, kt, col // SLOT))

            def advance(w_to):
                while pos_s[0] < len(kinds) and pos_s[0] <= w_slots[min(w_to, len(w_slots)) - 1]:
                    if kinds[pos_s[0]] == "M":
                        modulate(pos_s[0])
                    else:
                        split(pos_s[0])
                    pos_s[0] += 1

            def chunks(name, bodies, per, read=None, c0=0, hook=None):
                p = ph[name]
                assert pos_s[0] == w_slots[p.w0 + c0 * p.ws + 3] + 1, name

                def body(i):
                    for q in range(per):
                        for j in range(p.ws):
                            if bodies == 1:
                                advance(p.w0 + (c0 + q) * p.ws + j + 5)
                            else:
                                split(p.slot0 + (c0 + q) * p.per + 4 + j, i, per * p.per, per * p.ws)
                            if hook:
                                hook(i, c0 + q, j)
                        if read:
                            read(i, c0 + q)
                repeat(dve, bodies, body)
                if bodies > 1:
                    pos_s[0] += bodies * per * p.per

            def add_chunk(p, gated, gain=False):
                def read(i, q):
                    c = p.chunk0 + q
                    dve.wait_ge(w_used, p.w0 + (q + 1) * p.ws + i * (2 * p.ws))
                    col = bass.ds((i * 2 + q) * N, N)
                    for tb in range(TB):
                        if gated:
                            V.tensor_tensor(resid[:, tb, :], acc[c % 2][tb], mod_row[:, col], ALU.mult).then_inc(
                                ev(p.name + "_gated"), 1)
                            dve.wait_ge(ev(p.name + "_gated"), 2 * q + tb + 1 + i * 4)
                            if gain:
                                wait(dve, ev("sq2"), 2 * q)
                                V.tensor_tensor(before_gain[:, tb, :], x[:, tb, col], resid[:, tb, :],
                                                ALU.add).then_inc(ev("x2_summed"), 1)
                                dve.wait_ge(ev("x2_summed"), 2 * q + tb + 1)
                                ins = V.tensor_tensor(x[:, tb, col], before_gain[:, tb, :], row[:, col], ALU.mult)
                            else:
                                ins = V.tensor_tensor(x[:, tb, col], x[:, tb, col], resid[:, tb, :], ALU.add)
                        else:
                            ins = V.tensor_tensor(x[:, tb, col], acc[c % 2][tb], x[:, tb, col], ALU.add)
                        if tb == TB - 1:
                            ins.then_inc(pair_read[c % 2], 1)
                return read

            def rsqrt(sums, y, scale):
                n = y.shape[1]
                half, sq = newton[:, 0, 0:n], newton[:, 1, 0:n]
                link(V.tensor_scalar(half, sums, scale, EPS, ALU.mult, ALU.add))
                link(V.tensor_scalar(sq.bitcast(I32), half.bitcast(I32), 1, None, ALU.logical_shift_right))
                link(V.tensor_scalar(y.bitcast(I32), sq.bitcast(I32), -1.0, float(0x5F3759DF), ALU.mult, ALU.add))
                link(V.tensor_scalar(half, half, -0.5, None, ALU.mult))
                for _ in range(3):
                    link(V.tensor_tensor(sq, y, y, ALU.mult))
                    link(V.tensor_tensor(sq, sq, half, ALU.mult))
                    link(V.scalar_tensor_tensor(out=y, in0=sq, scalar=1.5, in1=y, op0=ALU.add, op1=ALU.mult))

            def token_sums(k, dst):
                link(V.tensor_reduce(dst, colsum[:, 8 * k:8 * k + 8].rearrange("p (t c) -> p t c", t=TB), AX_X, ALU.add))

            def turn_lo_of(name, banks, hi, lo, scale=None, at_bank=0):
                for b in range(at_bank, at_bank + banks):
                    g = turns[name] + b
                    dve.wait_ge(turn_hi, g + 1)
                    if scale is None:
                        V.tensor_tensor(lo[:, 2 * b:2 * b + 2, :].rearrange("p k t -> p (k t)"), turn[g % 2],
                                        hi[:, 2 * b:2 * b + 2, :].rearrange("p k t -> p (k t)").bitcast(F32),
                                        ALU.subtract).then_inc(turn_done, 1)
                    else:
                        for k in range(2):
                            ins = V.scalar_tensor_tensor(
                                out=lo[:, 2 * b + k, :], in0=turn[g % 2][:, k * T:(k + 1) * T],
                                scalar=scale[:, 2 * b + k:2 * b + k + 1], in1=hi[:, 2 * b + k, :].bitcast(F32),
                                op0=ALU.mult, op1=ALU.subtract)
                        ins.then_inc(turn_done, 1)

            plain = lambda name, hi=act_hi, lo=act_lo, scale=None: (
                lambda b: turn_lo_of(name, 1, hi, lo, scale, b))

            def affine(name):
                def step(b):
                    g = turns[name] + b
                    dve.wait_ge(turn_hi, g + 1)
                    for k in range(2):
                        ct = 2 * b + k
                        ins = V.scalar_tensor_tensor(
                            out=turned[:, b % 2, k * T:(k + 1) * T], in0=turn[g % 2][:, k * T:(k + 1) * T],
                            scalar=scale1[:, ct:ct + 1], in1=act_hi[:, ct, :].bitcast(F32), op0=ALU.mult, op1=ALU.subtract)
                    ins.then_inc(turn_affine, 1)
                    dve.wait_ge(turn_affine, b + 1 + (8 if name == "h1" else 0))
                    for k in range(2):
                        ct = 2 * b + k
                        ins = V.tensor_scalar(act_lo[:, ct, :], turned[:, b % 2, k * T:(k + 1) * T], shift[:, ct:ct + 1],
                                              None, ALU.add)
                    ins.then_inc(turn_done, 1)
                return step

            def mod_columns(layer, gain):
                dve.wait_ge(ev(f"cols{layer}_read"), 1)
                link(V.tensor_copy(shift, rest[0][:, 0:16]))
                link(V.scalar_tensor_tensor(out=scale1, in0=rest[0][:, 16:32], scalar=1.0, in1=gain,
                                            op0=ALU.add, op1=ALU.mult))
                V.engine_nop().then_inc(ev(f"shift{layer}"), 1)

            dve.wait_ge(ev("vecT"), 1)
            V.tensor_copy(vec[:, 0:122], rest[0][:, 0:122]).then_inc(ev("vec"), 1)
            dve.wait_ge(ev("vec"), 1)
            link(V.tensor_scalar(qgs, qg, HD ** -0.5, None, ALU.mult))
            link(V.tensor_copy(pos, pos_i[:, :]))
            ang, red, turns_n, tmp = (rope_a[:, i, :, :] for i in range(4))
            for tb in range(TB):
                link(V.tensor_scalar(ang[:, tb, :], freq, pos[:, tb:tb + 1], None, ALU.mult))
            link(V.tensor_scalar(turns_n, ang, 1.0 / TWO_PI, ROUND, ALU.mult, ALU.add))
            link(V.tensor_scalar(turns_n, turns_n, ROUND, None, ALU.subtract))
            for part in TWO_PI_PARTS:
                link(V.scalar_tensor_tensor(out=ang, in0=turns_n, scalar=-part, in1=ang, op0=ALU.mult, op1=ALU.add))
            link(V.tensor_scalar(ang, ang, PI_IN, -PI_IN, ALU.min, ALU.max))
            link(V.tensor_scalar(red, ang, np.pi / 2, None, ALU.add))
            link(V.tensor_scalar(tmp, red, np.pi, -TWO_PI, ALU.is_gt, ALU.mult))
            link(V.tensor_tensor(red, red, tmp, ALU.add))
            V.tensor_scalar(red, red, PI_IN, -PI_IN, ALU.min, ALU.max).then_inc(ev("angles"), 1)

            dve.wait_ge(ev("cond"), 1)
            for j in range(4):
                modulate(j)
            dve.wait_ge(ev("sq0"), 1)
            rsqrt(sumsq, rstd, 1.0 / D)
            V.engine_nop().then_inc(ev("rstd0"), 1)
            for col in range(4):
                with dve.Fori(1 if col == 0 else 0, KT // 4) as i:
                    for j in range(4):
                        modulate(KT * col + j, i, i * 4 + j)
            pos_s[0] = 64
            advance(4)
            mod_columns(0, norm0)
            for b in range(2):
                affine("h0")(b)
            chunks("pool_v", 1, 4, hook=behind(2, affine("h0")))
            chunks("pool_g", 1, 4, hook=placed(plain("pooled"), 0, *((3, j) for j in range(2, 8))))
            p = ph["grp"]
            mixed = plain("mixed", scale=pscale)

            def gate_group(i, g):
                c = p.chunk0 + g
                dve.wait_ge(w_used, p.w0 + 2 * g + 2)
                for tb in range(TB):
                    ins = V.tensor_tensor(u_nat[:, tb, g * N:(g + 1) * N], acc[c % 2][tb],
                                          gate_nat[:, tb, g * N:(g + 1) * N], ALU.mult)
                ins.then_inc(pair_read[c % 2], 1)
            chunks("grp", 1, 4, gate_group, hook=hooks(placed(plain("pooled"), 6, (0, 1), (1, 0)),
                                                       placed(mixed, 0, (2, 0), (2, 1), (3, 0), (3, 1))))
            mixed(4)
            mixed(5)
            dve.wait_ge(ev("gate0_row"), 4)
            chunks("pool_out", 1, 4, add_chunk(ph["pool_out"], True),
                   hook=placed(mixed, 6, (0, 1), (0, 2)))
            V.engine_nop().then_inc(ev("x1_done"), 1)
            mod_columns(1, norm1)
            dve.wait_ge(ev("sq1"), 4)
            token_sums(0, sumsq)
            rsqrt(sumsq, rstd, 1.0 / D)
            V.engine_nop().then_inc(ev("rstd1"), 1)
            for c in range(4):
                V.tensor_scalar(normed[:, 0, c * N:(c + 1) * N], x[:, 0, c * N:(c + 1) * N], rstd[:, 0:1], None,
                                ALU.mult).then_inc(ev("normed1"), 1)
            for b in range(2):
                affine("h1")(b)
            chunks("attn_idx", 1, 2, hook=behind(2, affine("h1")))
            advance(ph["attn_v"].w0 + 4)

            def rotate(tb, col, heads, width, half, f0, k, i=0):
                y = proj1[:, tb, bass.ds(col, heads * width)].rearrange("p (h w) -> p h w", h=heads)
                x1, x2 = y[:, :, 0:half], y[:, :, half:2 * half]
                cos = rope_c[:, tb, f0:f0 + half].unsqueeze(1).to_broadcast([P, heads, half])
                sin = rope_s[:, tb, f0:f0 + half].unsqueeze(1).to_broadcast([P, heads, half])
                t = [rope_t[:, n, 0:heads * half].rearrange("p (h w) -> p h w", h=heads) for n in range(4)]
                wait(dve, rope_add, k + i * 4)
                V.tensor_tensor(t[0], x1, cos, ALU.mult)
                V.tensor_tensor(t[1], x2, sin, ALU.mult)
                V.tensor_tensor(t[2], x2, cos, ALU.mult)
                V.tensor_tensor(t[3], x1, sin, ALU.mult).then_inc(rope_mul, 1)
                dve.wait_ge(rope_mul, k + 1 + i * 4)
                V.tensor_tensor(x1, t[0], t[1], ALU.subtract)
                V.tensor_tensor(x2, t[2], t[3], ALU.add).then_inc(rope_add, 1)

            def rotate_heads(i, q):
                if q % 2 == 1:
                    n = q // 2
                    for k in range(2):
                        dve.wait_ge(pair_read[k], ph["attn_qk"].chunk0 // 2 + n + 1 + i)
                    for k in range(2):
                        for tb in range(TB):
                            rotate(tb, i * N + (n * N + k * K1), 4, HD, ROT // 2, 0, 2 + 4 * n + 2 * k + tb, i)

            def index_inputs(i, c, j):
                if j == 0:
                    dve.wait_ge(ev("rope"), 1)
                    dve.wait_ge(ev("rest_read"), 1)
                    for q in range(2):
                        dve.wait_ge(pair_read[q], (ph["attn_idx"].chunk0 + 2) // 2)
                    for tb in range(TB):
                        rotate(tb, QI, IH + 1, ID, IROT // 2, ROT // 2, tb)
                    dve.wait_ge(rope_add, 2)
                    for k in range(2):
                        V.tensor_copy(ki_twice[:, :, k * ID:(k + 1) * ID], proj1[:, :, KI:KI + ID])
                    V.tensor_scalar(proj1[:, :, WI:WI + IH], proj1[:, :, WI:WI + IH], (IH * ID) ** -0.5, None, ALU.mult)
                    V.tensor_copy(work[:, :], hidden).then_inc(ev("index_in"), 1)
                elif 3 <= j < 7:
                    dve.wait_ge(turn_hi, turns["qi"] + j - 2)
                    V.tensor_copy(qiT[:, 2 * (j - 3) + 1, :], turn[(turns["qi"] + j - 3) % 2][:, T:2 * T]).then_inc(
                        turn_done, 1)
                elif j == 7:
                    dve.wait_ge(turn_hi, turns["ki"] + 1)
                    V.engine_nop().then_inc(turn_done, 1)

            def index_heads(i, c, j):
                k = (c - 1) * 8 + j
                if k == 0:
                    dve.wait_ge(ev("index_in"), 1)
                if k % 3 == 1:
                    for h in (k // 3 * 2, k // 3 * 2 + 1):
                        dve.wait_ge(i_relu, h + 1)
                        wait(dve, i_done, h)
                        for tb, (c0, c1) in enumerate(((0, P), (P, 384))):
                            ins = V.scalar_tensor_tensor(out=work[:, c0:c1], in0=relu[:, h % 2, c0:c1],
                                                         scalar=proj1[:, tb, WI + h:WI + h + 1], in1=work[:, c0:c1],
                                                         op0=ALU.mult, op1=ALU.add)
                        ins.then_inc(i_done, 1)

            assert TOPK == 8 * ph["attn_qk"].ws

            def top_keys(i, c, j):
                c0, c1 = ((0, P), (P, 384))[c]
                if c == 0 and j == 0:
                    dve.wait_ge(i_done, IH)
                link(V.max(out=best, in_=work[:, c0:c1]))
                link(V.match_replace(out=work[:, c0:c1], in_to_replace=best, in_values=work[:, c0:c1],
                                     imm_value=TAKEN))
                if c == 1 and j == 7:
                    link(V.tensor_scalar(amask[:, :], work[:, :], TAKEN, -LOW, ALU.is_equal, ALU.mult))
                    V.scalar_tensor_tensor(out=amask[:, :], in0=amask[:, :], scalar=LOW, in1=hidden,
                                           op0=ALU.add, op1=ALU.min).then_inc(ev("masked"), 1)
                    dve.wait_ge(ev("masked"), 1)

            chunks("attn_v", 1, 1, hook=index_inputs)
            chunks("attn_v", 1, 3, c0=1, hook=index_heads)
            chunks("attn_qk", 1, 2, rotate_heads, hook=top_keys)

            def attend(t, r):
                if runs(t - 1):
                    wait(dve, s_full, t)
                    wait(dve, p_ready, t - 1)
                    V.scalar_tensor_tensor(out=logit[:, :], in0=rest[0][:, 0:384], scalar=HD ** -0.5,
                                           in1=amask[:, :], op0=ALU.mult, op1=ALU.add).then_inc(s_read, 1)
                    dve.wait_ge(s_read, t)
                    for tb, (c0, c1) in enumerate(((0, P), (P, 384))):
                        V.tensor_reduce(top[:, tb:tb + 1], logit[:, c0:c1], AX_X, ALU.max).then_inc(l_max, 1)
                    dve.wait_ge(l_max, t * 2)
                    V.tensor_scalar(ntop, top, -1.0, None, ALU.mult).then_inc(l_ready, 1)
                if runs(t - 3):
                    dve.wait_ge(o_full, t - 2)
                    wait(dve, o_done, t - 3)
                    d = 2 * ((r - 3) % 4)
                    V.reciprocal(rden, den[:, d:d + 2]).then_inc(r_ready, 1)
                    dve.wait_ge(r_ready, t - 2)
                    for tb in range(TB):
                        ins = V.tensor_scalar(proj1[:, tb, bass.ds(t * P - 3 * P, P)], rest[1][:, tb * P:(tb + 1) * P],
                                              rden[:, tb:tb + 1], None, ALU.mult)
                    ins.then_inc(o_done, 1)
            chunks("attn_qk", 1, 6, rotate_heads, c0=2, hook=at_heads(-5, (2, attend)))
            o1 = plain("o1", o1_hi, o1_lo)
            chunks("attn_gate", 1, 4, hook=hooks(at_heads(11, (2, attend)), placed(o1, 0, (3, 5), (3, 6), (3, 7))))
            dve.wait_ge(pair_read[1], (ph["attn_gate"].chunk0 + 3) // 2 + 1)
            dve.wait_ge(o_done, HEADS)
            V.tensor_tensor(proj1[:, :, 3 * N:D], proj1[:, :, 3 * N:D], proj1[:, :, G1 + 3 * N:QI], ALU.mult).then_inc(
                ev("o_last"), 1)
            o1(3)
            dve.wait_ge(ev("gate1_row"), 4)
            dve.wait_ge(ev("final_row"), 16)
            h2 = plain("h2", scale=anorm)
            chunks("attn_out", 1, 4, add_chunk(ph["attn_out"], True, True),
                   hook=hooks(behind(4, o1), streamed(1, h2)))
            V.engine_nop().then_inc(ev("x2_done"), 1)

            def norm_twice(i, c, j):
                if c == 0 and j == 6:
                    dve.wait_ge(ev("sq2"), 8)
                    token_sums(0, sumsq)
                    rsqrt(sumsq, rfinal, 1.0 / D)
                    token_sums(1, sumnext)
                    for _ in range(2):
                        link(V.tensor_tensor(sumnext, sumnext, rfinal, ALU.mult))
                    rsqrt(sumnext, rnext, 1.0 / D)
                    V.tensor_tensor(rstd, rfinal, rnext, ALU.mult).then_inc(ev("rstd2"), 1)
                if c == 1 and j in (2, 4):
                    tb = j // 2 - 1
                    V.tensor_scalar(x[:, tb, :], x[:, tb, :], rfinal[:, tb:tb + 1], None, ALU.mult).then_inc(
                        ev("x3_done"), 1)
            chunks("in_uv", 1, 4, hook=hooks(last_two(1, h2), norm_twice))
            chunks("in_qkv", 3, 2)

            def norm_groups(i, c, j):
                y = proj2[:, c, S2:V2].rearrange("p (g c) -> p g c", c=P)
                s, r = ssq2[:, 24 * c:24 * c + 24], rs2[:, 24 * c:24 * c + 24]
                if j == 2:
                    dve.wait_ge(ev("squares"), c + 1)
                    V.tensor_reduce(s, squares[:, :].rearrange("p (g c) -> p g c", c=P), AX_X, ALU.add).then_inc(
                        ev("squares_sum"), 1)
                    dve.wait_ge(ev("squares_sum"), c + 1)
                    rsqrt(s, r, 1.0 / P)
                if j == 3:
                    V.tensor_tensor(y, y, r.unsqueeze(2).to_broadcast([P, 24, P]), ALU.mult).then_inc(
                        ev("qk_normed"), 1)
                if c == 1 and j == 4:
                    dve.wait_ge(ev("sgu_row"), 16)
                    dve.wait_ge(ev("qk_normed"), 2)
                    for tb in range(TB):
                        V.tensor_tensor(proj2[:, tb, S2:Q2], proj2[:, tb, S2:Q2], sgu_row[:, :], ALU.mult).then_inc(
                            ev("sgu_in"), 1)

            def gate_spatial(i, c, j):
                if c == 2 and j in (1, 3):
                    for n in (j - 1, j):
                        dve.wait_ge(ev("sgu_full"), n + 1)
                        tb, g0 = n // 2, n % 2 * 4
                        for g in range(g0, g0 + 4):
                            u = proj2[:, tb, g * P:(g + 1) * P]
                            ins = V.scalar_tensor_tensor(out=u, in0=mixes[n % 2][:, (g - g0) * P:(g - g0 + 1) * P],
                                                         scalar=bs[:, g:g + 1], in1=u, op0=ALU.add, op1=ALU.mult)
                        ins.then_inc(ev("sgu_read"), 1)

            def sticks(t, r):
                if runs(t - 2, SBH):
                    dve.wait_ge(b_tail, t - 1)
                    V.tensor_tensor(sb_hit[:, t % 2, :], turn[1][:, 0:384], sb_hit[:, t % 2, :],
                                    ALU.add).then_inc(b_arg, 1)
                if runs(t - 1, SBH):
                    dve.wait_ge(b_log, t)
                    wait(dve, b_tail, t - 1)
                    wait(dve, b_w, t - 2)
                    V.scalar_tensor_tensor(out=sb_miss[:, :], in0=rest[0][:, 0:384], scalar=0.0,
                                           in1=sb_log[:, :], op0=ALU.max, op1=ALU.add).then_inc(b_sum, 1)
                    V.scalar_tensor_tensor(out=sb_hit[:, (t - 1) % 2, :], in0=rest[0][:, 0:384], scalar=0.0,
                                           in1=sb_log[:, :], op0=ALU.min, op1=ALU.subtract).then_inc(z_read, 1)
                    dve.wait_ge(b_sum, t)
                    V.tensor_tensor(sb_miss[:, :], sb_miss[:, :], nstrict, ALU.mult).then_inc(b_miss, 1)

            def mask(t, r):
                if runs(t - 2, SBH):
                    dve.wait_ge(b_w, t - 1)
                    V.tensor_tensor(sb_w[:, :], sb_w[:, :], strict, ALU.mult).then_inc(b_mask, 1)
            heads2 = at_heads(-5, (2, sticks), (3, mask))

            def spatial_and_heads(i, c, j):
                gate_spatial(i, c, j)
                heads2(i, c, j)
            chunks("in_gates", 1, 2, hook=norm_groups)
            chunks("in_gates", 1, 6, c0=2, hook=hooks(spatial_and_heads, placed(plain("y2"), 0, (7, 5), (7, 6), (7, 7))))
            turn_lo_of("y2", 1, act_hi, act_lo, at_bank=3)
            p = ph["up"]

            def merged_behind(i, c, j):
                if c == 3 and j in (0, 2):
                    b, g = j // 2, turns["merged"] + j // 2
                    dve.wait_ge(turn_hi, g + 1 + i * 2)
                    kts = bass.ds(i * 4 + 2 * b, 2)
                    V.tensor_tensor(merged_lo[:, kts, :].rearrange("p k t -> p (k t)"), turn[g % 2],
                                    merged_hi[:, kts, :].rearrange("p k t -> p (k t)").bitcast(F32),
                                    ALU.subtract).then_inc(turn_done, 1)

            def merge(i, q):
                n = q // 2
                dve.wait_ge(w_used, p.w0 + 4 * q + 4 + i * 8)
                for tb in range(TB):
                    g = proj2[:, tb, bass.ds(i * N + (n * N + (GA, GB)[q % 2]), N)]
                    ins = V.tensor_tensor(g, acc[q % 2][tb], g, ALU.mult)
                    if q % 2 == 1:
                        ins.then_inc(ev("up_gated"), 1)
                        dve.wait_ge(ev("up_gated"), tb + 1 + 2 * n + i * 2)
                        dve.wait_ge(pair_read[0], p.chunk0 // 2 + 1 + n + i)
                        ga = proj2[:, tb, bass.ds(i * N + (n * N + GA), N)]
                        ins = V.tensor_tensor(ga, ga, g, ALU.add)
                ins.then_inc(pair_read[q % 2], 1)
            chunks("up", 1, 2, merge, hook=behind(4, plain("y2")))
            chunks("up", 3, 2, merge, c0=2, hook=merged_behind)
            h3 = plain("h3", scale=fnorm)
            dve.wait_ge(ev("x3_done"), 2)
            chunks("w_o", 1, 4, add_chunk(ph["w_o"], False),
                   hook=hooks(last_two(1, plain("merged", merged_hi, merged_lo)), streamed(1, h3)))

            def norm4(i, c, j):
                if c == 0 and j == 6:
                    dve.wait_ge(ev("sq4"), 4)
                    token_sums(0, sumsq)
                    rsqrt(sumsq, rstd, 1.0 / D)
                    V.engine_nop().then_inc(ev("rstd4"), 1)
            p = ph["ffn_in"]

            def hid_lo_of(j):
                for b in range(2):
                    g = turns["hid"] + b
                    dve.wait_ge(turn_hi, g + 1 + j * 2)
                    kts = bass.ds(j * 4 + 2 * b, 2)
                    V.tensor_tensor(hid_lo[:, kts, :].rearrange("p k t -> p (k t)"), turn[g % 2],
                                    hid_hi[:, kts, :].rearrange("p k t -> p (k t)").bitcast(F32),
                                    ALU.subtract).then_inc(turn_done, 1)

            def ffn_in(j, first):
                for q in range(2):
                    for k in range(8):
                        split(p.slot0 + 4 + q * 8 + k, j, 16, 16)
                        if first:
                            hooks(last_two(1, h3), norm4)(0, q, k)
                    if q == 0 and not first:
                        hid_lo_of(j - 1)
                    if q == 1:
                        dve.wait_ge(w_used, p.w0 + 16 + j * 16)
                        dve.wait_ge(gate_ready, j + 1)
                        for tb in range(TB):
                            ins = V.scalar_tensor_tensor(out=hid[:, tb, :], in0=acc[1][tb], scalar=rstd[:, tb:tb + 1],
                                                         in1=hid[:, tb, :], op0=ALU.mult, op1=ALU.mult)
                        ins.then_inc(hid_ready, 1)
            ffn_in(0, True)
            with dve.Fori(1, 11) as j:
                ffn_in(j, False)
            hid_lo_of(10)
            pos_s[0] += 22 * 8
            p = ph["ffn_out"]

            def ffn_out(i):
                for j in range(4):
                    split(p.slot0 + 4 + j, i, 4, 4)
            repeat(dve, 22, ffn_out)
            pos_s[0] += 88
            dve.wait_ge(w_used, p.w0 + 88)
            for tb, n in X5_ORDER:
                cols = slice(n * N, (n + 1) * N)
                V.tensor_tensor(x[:, tb, cols], ps[:, X5_BANK[tb][n]], x[:, tb, cols], ALU.add).then_inc(ev("x5_cols"), 1)
            turn_lo_of("h4", 2, act_hi, act_lo, pnorm)
            p = ph["ple_in"]
            h4 = behind(2, plain("h4", scale=pnorm))
            for c in range(4):
                for j in range(9):
                    advance(p.w0 + 9 * c + 4 + j + 1)
                    if j < 8:
                        h4(0, c, j)
                    if c == 0 and j == 7:
                        turn_lo_of("p", 1, pT_hi, pT_lo)
                        dve.wait_ge(ev("sq5"), 2)
                        rsqrt(sumsq, rstd, 1.0 / D)
                        V.engine_nop().then_inc(ev("rstd5"), 1)
                dve.wait_ge(w_used, p.w0 + 9 * c + 9)
                dve.wait_ge(pair_read[0], pairs_before + c + 1)
                cols = slice(c * N, (c + 1) * N)
                for tb in range(TB):
                    ins = V.tensor_tensor(ple[:, tb, :], ps[:, 4 * (c % 2) + 2 + tb], ple[:, tb, :], ALU.mult)
                ins.then_inc(pair_read[1], 1)
                dve.wait_ge(pair_read[1], pairs_before + c + 1)
                for tb in range(TB):
                    ins = V.tensor_tensor(x[:, tb, cols], x[:, tb, cols], ple[:, tb, :], ALU.add)
                ins.then_inc(ev("x_final"), 1)

        @block.tensor
        def _(pe):
            M = nc.tensor.matmul

            def three(dst, hi_t, lo_t, w, cols, first, last):
                wh, wl = w_hi[:, w, cols], w_lo[:, w, cols]
                M(dst, hi_t, wh, start=first, stop=False)
                M(dst, hi_t, wl, start=False, stop=False)
                return M(dst, lo_t, wh, start=False, stop=last)

            def chunk(p, q, i, per, kts, turned_at, hook=None, split_acts=(act_hi, act_lo)):
                c = p.chunk0 + q
                hi_t, lo_t = split_acts
                wait(pe, pair_read[c % 2], c // 2 + i * (per // 2))
                for n in range(len(kts) // 2):
                    pe.wait_ge(slot_done, w_slots[p.w0 + q * p.ws + n] + 1 + i * (per * p.per))
                    w0 = p.w0 + q * p.ws + n
                    for k in range(2):
                        kt = kts[2 * n + k]
                        if kt % 2 == 0:
                            pe.wait_ge(turn_done, turned_at + kt // 2 + 1)
                        for tb in range(TB):
                            t = slice(tb * P, (tb + 1) * P)
                            ins = three(acc[c % 2][tb], hi_t[:, kt, t], lo_t[:, kt, t], w0 % SPLIT,
                                        slice(k * N, (k + 1) * N), n == 0 and k == 0,
                                        n == len(kts) // 2 - 1 and k == 1)
                            if k == 1 and tb == 1:
                                ins.then_inc(w_used, 1)
                    if hook:
                        hook(i, q, n)

            def chunks(name, bodies, per, turned, kts=range(KT), c0=0, hook=None, split_acts=(act_hi, act_lo)):
                p = ph[name]

                def body(i):
                    for q in range(per):
                        chunk(p, c0 + q, i, per, kts, turns[turned], hook, split_acts)
                repeat(pe, bodies, body)

            def turn_bank(g, tiles, i=0, ni=0):
                wait(pe, turn_done, g - 1 + i * ni)
                for n, tile in enumerate(tiles):
                    ins = nc.tensor.transpose(turn[g % 2][:, n * P:(n + 1) * P], tile, ident)
                ins.then_inc(turn_full, 1)

            def turner(name, src, waits=None):
                def step(b):
                    if waits:
                        waits(b)
                    turn_bank(turns[name] + b, [src(tb, 2 * b + k) for k in range(2) for tb in range(TB)])
                return step

            def turn_first(n, step):
                for b in range(n):
                    step(b)

            def added(name):
                return lambda b: columns_read(pe, ph[name], b // 2)

            def summed_columns(layer, col):
                pe.wait_ge(slot_done, m_slots[96 * layer + KT * (col + 1) - 1] + 1)
                for j in range(8 * col, 8 * col + 8):
                    ins = M(rest[0][:, j:j + 1], mod_acc[:, j * P:(j + 1) * P], ones[:, 0:1], start=True, stop=True)
                if col == 3:
                    ins.then_inc(ev(f"cols{layer}_read"), 1)

            def sum_row(name, after, at_chunk=0):
                def hook(i, c, n):
                    if c == at_chunk and n % 2 == 0:
                        row_chunk(name, n // 2, after)
                return hook

            def row_chunk(name, c, after):
                if c == 0:
                    pe.wait_ge(slot_done, after)
                wait(pe, ev(name + "_row"), c - 1)
                M(rest[c % 2], ones, mod_row[:, c * N:(c + 1) * N], start=True, stop=True).then_inc(
                    ev(name + "_full"), 1)

            tile = lambda buf: (lambda tb, kt: buf[:, tb, kt * P:(kt + 1) * P])

            pe.wait_ge(ev("const_in"), 16)
            pe.wait_ge(ev("vec_in"), 16 * (len(vec_sources) + 1))
            nc.tensor.transpose(rest[0][:, 0:122], vec_rows[0:122, :], ident[0:122, 0:122]).then_inc(ev("vecT"), 1)
            pe.wait_ge(ev("vec"), 1)
            for col in range(3):
                summed_columns(0, col)
            pe.wait_ge(ev("normed0"), 2)
            h0 = turner("h0", tile(normed))
            turn_first(2, h0)
            summed_columns(0, 3)
            chunks("pool_v", 1, 4, "h0", hook=behind(2, h0))
            pe.wait_ge(ev("mix_in"), 16)

            def pool_bank(b):
                g = turns["pooled"] + b
                wait(pe, turn_done, g - 1)
                columns_read(pe, ph["pool_v"], b // 2)
                for k in range(2):
                    ct = 2 * b + k
                    c = slice(ct * P, (ct + 1) * P)
                    M(turn[g % 2][:, k * T:(k + 1) * T], v_nat[:, 0, c], pool_mix[:, 0, ct // 4, :], start=True, stop=False)
                    ins = M(turn[g % 2][:, k * T + P:(k + 1) * T], v_nat[:, 1, c], pool_mix[:, 1, ct // 4, P:T],
                            start=False, stop=True)
                ins.then_inc(turn_full, 1)

            chunks("pool_g", 1, 4, "h0", hook=hooks(sum_row("gate0", ends[0, 1], 2),
                                                    placed(pool_bank, 0, *((3, n) for n in range(1, 7)))))
            mixed = turner("mixed", tile(u_nat), added("grp"))
            in_grp = hooks(placed(pool_bank, 6, (0, 0), (0, 1)),
                           placed(mixed, 0, (1, 1), (2, 0), (2, 1), (3, 0), (3, 1)))
            for g in range(4):
                chunk(ph["grp"], g, 0, 4, range(4 * g, 4 * g + 4), turns["pooled"], in_grp)
            mixed(5)

            def columns_behind(i, c, n):
                if n == 6:
                    summed_columns(1, c)
            chunks("pool_out", 1, 4, "mixed", hook=hooks(placed(mixed, 6, (0, 0), (0, 1)), columns_behind))

            def normed1(b):
                pe.wait_ge(ev("normed1"), b // 2 + 1)
                pe.wait_ge(ev("normed1_b"), b // 2 + 1)
            h1 = turner("h1", tile(normed), normed1)
            turn_first(2, h1)
            chunks("attn_idx", 1, 2, "h1", hook=behind(2, h1))
            p = ph["attn_rest"]
            w80 = PROJ1 - KI
            for j in range(2):
                pe.wait_ge(slot_done, p.slot0 + j + 1)
                for tb in range(TB):
                    for k in range(8):
                        kt, t = 8 * j + k, slice(tb * P, (tb + 1) * P)
                        ins = three(rest[tb][:, 0:w80], act_hi[:, kt, t], act_lo[:, kt, t], (p.w0 + j) % SPLIT,
                                    slice(k * w80, (k + 1) * w80), kt == 0, kt == KT - 1)
                ins.then_inc(w_used, 1)

            def turn_index(i, c, n):
                if n == 2:
                    pe.wait_ge(ev("index_in"), 1)
                if 2 <= n < 6:
                    b = n - 2
                    turn_bank(turns["qi"] + b, [proj1[:, tb, QI + (2 * b + k) * P:QI + (2 * b + k + 1) * P]
                                                for k in range(2) for tb in range(TB)])
                elif n == 6:
                    turn_bank(turns["ki"], [ki_twice[:, tb, :] for tb in range(TB)])

            def index_heads(i, c, n):
                k = (c - 1) * 8 + n
                if k == 0:
                    pe.wait_ge(turn_done, turns["ki"] + 1)
                    pe.wait_ge(ev("rest_read"), 1)
                if k % 3 == 0:
                    for h in (k // 3 * 2, k // 3 * 2 + 1):
                        wait(pe, i_relu, h - 1)
                        r = slice(h % 2 * ID, (h % 2 + 1) * ID)
                        M(rest[h % 2][:, 0:P], qiT[r, h // 2, 0:P], kiT[r, 0:P], start=True, stop=True)
                        M(rest[h % 2][:, P:384], qiT[r, h // 2, P:T], kiT[r, :], start=True, stop=True).then_inc(
                            i_full, 1)

            def index_read(i, c, n):
                if c == 0 and n == 0:
                    pe.wait_ge(i_relu, IH)
            chunks("attn_v", 1, 1, "h1", hook=turn_index)
            chunks("attn_v", 1, 3, "h1", c0=1, hook=index_heads)
            chunks("attn_qk", 1, 2, "h1", hook=hooks(index_read, sum_row("gate1", ends[1, 1])))

            def attend(t, r):
                if runs(t - 1):
                    wait(pe, qk_ready, t)
                    wait(pe, s_read, t - 1)
                    if isinstance(t, int) and t == 1:
                        pe.wait_ge(ev("gate1_row"), 4)
                    q, k = headT[:, 0, :], headT[:, 1, :]
                    M(rest[0][:, 0:P], q[:, 0:P], k[:, 0:P], start=True, stop=True)
                    M(rest[0][:, P:384], q[:, P:T], k, start=True, stop=True).then_inc(s_full, 1)
                if runs(t - 2):
                    wait(pe, p_ready, t - 1)
                    wait(pe, pt_ready, t - 2)
                    for n in range(3):
                        ins = nc.tensor.transpose(turn[1][:, n * P:(n + 1) * P], prob[:, n * P:(n + 1) * P], ident)
                    ins.then_inc(pt_full, 1)
                if runs(t - 3):
                    wait(pe, pt_ready, t - 2)
                    wait(pe, o_done, t - 3)
                    v = [proj1[:, tb, bass.ds(t * P + (V1 - 3 * P), P)] for tb in range(TB)]
                    o = rest[1]
                    M(o[:, 0:P], probT[:, 0:P], v[0], start=True, stop=True)
                    M(o[:, P:T], probT[:, P:2 * P], v[0], start=True, stop=False)
                    M(o[:, P:T], probT[:, 2 * P:384], v[1], start=False, stop=True).then_inc(o_full, 1)
                if runs(t):
                    pe.wait_ge(in_ready, t + 1)
                    wait(pe, qk_ready, t)
                    for n in range(4):
                        ins = nc.tensor.transpose(turn[0][:, n * P:(n + 1) * P], head_in[:, n // 2, n % 2, :], ident)
                    ins.then_inc(qk_full, 1)
            chunks("attn_qk", 1, 6, "h1", c0=2, hook=at_heads(-5, (0, attend)))

            def gated(b):
                pe.wait_ge(ev("o_gated"), min(b // 2 + 1, 3))
                if b == 4:
                    pe.wait_ge(o_done, HEADS)
                if b == 6:
                    pe.wait_ge(ev("o_last"), 1)
            o1 = turner("o1", tile(proj1), gated)
            chunks("attn_gate", 1, 4, "h1", hook=hooks(at_heads(11, (0, attend)), placed(o1, 0, (3, 4), (3, 5), (3, 6))))
            o1(3)
            h2 = turner("h2", tile(x), added("attn_out"))
            chunks("attn_out", 1, 4, "o1", hook=hooks(behind(4, o1), streamed(0, h2)), split_acts=(o1_hi, o1_lo))
            chunks("in_uv", 1, 4, "h2", hook=last_two(0, h2))
            chunks("in_qkv", 3, 2, "h2")

            def turn_ws(i, c, n):
                if c == 0 and n == 1:
                    pe.wait_ge(ev("w_s_low"), 1)
                    for b in range(2):
                        for g in range(4):
                            ins = nc.tensor.transpose(rest[b][:, g * P:(g + 1) * P], w_s[:, 4 * b + g, :], ident)
                        ins.then_inc(ev("ws_turned"), 1)

            def mix_spatial(i, c, n):
                if c == 2 and n == 0:
                    pe.wait_ge(ev("w_sT"), 2)
                    pe.wait_ge(ev("sgu_in"), 2)
                    pe.wait_ge(turn_done, turns["y2"])
                if c == 2 and n in (0, 2):
                    for m in (n, n + 1):
                        wait(pe, ev("sgu_read"), m - 1)
                        tb, g0 = m // 2, m % 2 * 4
                        for g in range(g0, g0 + 4):
                            ins = M(mixes[m % 2][:, (g - g0) * P:(g - g0 + 1) * P], w_sT[:, g, :],
                                    proj2[:, tb, S2 + g * P:S2 + (g + 1) * P], start=True, stop=True)
                        ins.then_inc(ev("sgu_full"), 1)

            def stick(t, r):
                if runs(t - 1, SBH):
                    wait(pe, qk2_ready, t)
                    wait(pe, z_read, t - 1)
                    q, k = headT2[:, 0, :], headT2[:, 1, :]
                    M(rest[0][:, 0:T], k[:, 0:P], q, start=True, stop=True)
                    M(rest[0][:, T:384], k[:, P:T], q[:, P:T], start=True, stop=True).then_inc(z_full, 1)
                if runs(t - 2, SBH):
                    pe.wait_ge(b_miss, t - 1)
                    wait(pe, b_arg, t - 2)
                    if t == 2:
                        pe.wait_ge(ev("sgu_read"), 4)
                    tail = turn[1]
                    M(tail[:, 0:T], later, sb_miss[:, 0:T], start=True, stop=False)
                    M(tail[:, P:T], ones, sb_miss[:, T:384], start=False, stop=True)
                    M(tail[:, T:384], later, sb_miss[:, T:384], start=True, stop=True).then_inc(b_tail, 1)
                if runs(t - 3, SBH):
                    pe.wait_ge(b_mask, t - 2)
                    wait(pe, y_done, t - 3)
                    v = [proj2[:, tb, bass.ds(t * P + (V2 - 3 * P), P)] for tb in range(TB)]
                    y = rest[1]
                    M(y[:, 0:P], sb_w[:, 0:P], v[0], start=True, stop=True)
                    M(y[:, P:T], sb_w[:, P:T], v[0], start=True, stop=False)
                    M(y[:, P:T], sb_w[:, T:384], v[1], start=False, stop=True).then_inc(y_full, 1)
                if runs(t, SBH):
                    pe.wait_ge(in2_ready, t + 1)
                    wait(pe, qk2_ready, t)
                    for n in range(4):
                        ins = nc.tensor.transpose(turn[0][:, n * P:(n + 1) * P], head_in2[:, n // 2, n % 2, :], ident)
                    ins.then_inc(qk2_full, 1)
            heads2 = at_heads(-5, (0, stick))

            def spatial_and_heads(i, c, n):
                mix_spatial(i, c, n)
                heads2(i, c, n)
            chunks("in_gates", 1, 2, "h2", hook=turn_ws)

            def y_b_done(b):
                if b == 4:
                    pe.wait_ge(y_done, SBH)
            y2 = turner("y2", lambda tb, kt: proj2[:, tb, (kt * P if kt < 8 else Q2 + kt * P - 1024):][:, 0:P], y_b_done)
            chunks("in_gates", 1, 6, "h2", c0=2, hook=hooks(spatial_and_heads, placed(y2, 0, (7, 4), (7, 5), (7, 6))))
            y2(3)

            def merged_behind(i, c, n):
                if (c, n) in ((2, 3), (3, 1)):
                    b = c - 2
                    pe.wait_ge(pair_read[1], ph["up"].chunk0 // 2 + 1 + i)
                    turn_bank(turns["merged"] + b,
                              [proj2[:, tb, GA + i * N + (2 * b + k) * P:][:, 0:P]
                               for k in range(2) for tb in range(TB)], i, 2)
            p = ph["up"]

            def up(i, c0, hook):
                chunk(p, c0, i, 2, range(8), turns["y2"], hook)
                chunk(p, c0 + 1, i, 2, range(8, 16), turns["y2"], hook)
            up(0, 0, behind(4, y2))
            for i in range(3):
                up(i, 2, merged_behind)

            def merged_read(b):
                pe.wait_ge(pair_read[1], p.chunk0 // 2 + 4)
            merged = turner("merged", lambda tb, kt: proj2[:, tb, GA + kt * P:GA + (kt + 1) * P], merged_read)
            h3 = turner("h3", tile(x), added("w_o"))
            chunks("w_o", 1, 4, "merged", hook=hooks(last_two(0, merged), streamed(0, h3)),
                   split_acts=(merged_hi, merged_lo))
            p = ph["ffn_in"]

            def turn_hid(j):
                pe.wait_ge(hid_ready, j + 1)
                for b in range(2):
                    turn_bank(turns["hid"] + b, [hid[:, tb, (2 * b + k) * P:(2 * b + k + 1) * P]
                                                 for k in range(2) for tb in range(TB)], j, 2)

            def ffn_in(j, first):
                for q in range(2):
                    if first:
                        pe.wait_ge(pair_read[q], p.chunk0 // 2)
                    else:
                        pe.wait_ge((gate_ready, hid_ready)[q], j)
                    ffn_chunk(j, q)
                    if q == 0 and not first:
                        turn_hid(j - 1)

            def ffn_chunk(j, q):
                for n in range(8):
                    pe.wait_ge(slot_done, p.slot0 + q * 8 + n + 1 + j * 16)
                    for k in range(2):
                        kt = 2 * n + k
                        if k == 0:
                            pe.wait_ge(turn_done, turns["h3"] + n + 1)
                        for tb in range(TB):
                            t = slice(tb * P, (tb + 1) * P)
                            ins = three(acc[q][tb], act_hi[:, kt, t], act_lo[:, kt, t], (p.w0 + n) % SPLIT,
                                        slice(k * N, (k + 1) * N), kt == 0, kt == KT - 1)
                    ins.then_inc(w_used, 1)
                    if isinstance(j, int):
                        last_two(0, h3)(0, q, n)

            ffn_in(0, True)
            with pe.Fori(1, 11) as j:
                ffn_in(j, False)
            p = ph["ffn_out"]

            def ffn_out(i, first, last):
                for q in range(2):
                    pe.wait_ge(hid_copied, i * 2 + (q + 1))
                    for j in range(2):
                        pe.wait_ge(slot_done, p.slot0 + 2 * q + j + 1 + i * 4)
                        w0 = p.w0 + 2 * q + j
                        if first and q == 0:
                            if j == 0:
                                pe.wait_ge(gate_ready, 11)
                            else:
                                turn_hid(10)
                        for tb in range(TB):
                            if first and (q, j, tb) == (0, 1, 1):
                                pe.wait_ge(turn_done, turns["h4"])
                            hi, lo = (hid_at[:, q, k, tb * P:(tb + 1) * P] for k in range(2))
                            for n in range(2):
                                ins = three(ps[:, X5_BANK[tb][2 * j + n]], hi, lo, w0 % SPLIT,
                                            slice(n * N, (n + 1) * N), first and q == 0, last and q == 1)
                        ins.then_inc(w_used, 1)
            ffn_out(0, True, False)
            with pe.Fori(1, HKT // 2 - 1) as i:
                ffn_out(i, False, False)
            ffn_out(HKT // 2 - 1, False, True)

            def x5_columns(b):
                pe.wait_ge(ev("x5_cols"), (4, 6, 7, 8)[b // 2])
            h4 = turner("h4", tile(x), x5_columns)
            turn_first(2, h4)
            pe.wait_ge(ev("x5_cols"), 5)
            h4_behind = behind(2, h4)
            p = ph["ple_in"]
            for c in range(4):
                for q in range(2):
                    if c > 1:
                        pe.wait_ge(pair_read[q], pairs_before + c - 1)
                    for n in range(8 if q == 0 else 1):
                        s = 9 * c + (n if q == 0 else 8)
                        pe.wait_ge(slot_done, p.slot0 + s + 1)
                        for k in range(2):
                            kt = 2 * n + k
                            if k == 0:
                                pe.wait_ge(turn_done, (turns["h4"] + n + 1) if q == 0 else turns["p"] + 1)
                            hi, lo = (act_hi, act_lo) if q == 0 else (pT_hi, pT_lo)
                            for tb in range(TB):
                                t = slice(tb * P, (tb + 1) * P)
                                ins = three(ps[:, 4 * (c % 2) + 2 * q + tb], hi[:, kt, t], lo[:, kt, t], (p.w0 + s) % SPLIT,
                                            slice(k * N, (k + 1) * N), kt == 0, kt == (KT - 1 if q == 0 else 1))
                        ins.then_inc(w_used, 1)
                        if c == 0 and q == 0:
                            h4_behind(0, 0, n)
                            if n == 6:
                                pe.wait_ge(ev("p_in"), 16)
                                turn_bank(turns["p"], [p_nat[:, tb, k * P:(k + 1) * P]
                                                       for k in range(2) for tb in range(TB)])



_INS = ["x", "c", "positions", "norm_g", "mod_w", "mod_b", "pool_w_in", "pool_w_grp", "pool_scale", "pool_w_out",
        "attn_w_in", "attn_w_out", "final_g", "p_2", "attn_norm_g_2", "w_in_2", "sgu_norm_g_2", "w_s_2", "b_s_2",
        "q_norm_g_2", "k_norm_g_2", "w_up_a_2", "w_up_b_2", "w_o_2", "ffn_norm_g_2", "w_ffn_in_2",
        "w_ffn_out_2", "ple_norm_g_2", "w_ple_gate_2", "w_ple_2"]


def tables():
    r, c = np.arange(P)[:, None], np.arange(P)[None, :]
    zero, one = np.zeros((P, P)), np.ones((P, P))
    low = np.where(c <= r, 0.0, LOW)
    before = (r < c) * 1.0
    hidden = np.concatenate([low, zero, low], 1)
    strict = np.concatenate([before, one, before], 1)
    theta = 500000.0
    freq = np.concatenate([np.float32(theta) ** (-np.arange(rot // 2, dtype=np.float32) * 2.0 / rot)
                           for rot in (ROT, IROT)])
    const = np.concatenate([np.eye(P), one, (r > c) * 1.0, hidden, strict, -strict,
                            np.broadcast_to(freq, (P, HALVES))], 1).astype(np.float32)
    s, t = np.arange(T)[:, None], np.arange(T)[None, :]
    mix = [((s <= t) & (s > t - w)) / np.minimum(t + 1, w) - (s == t) for w in (2, 4, 8, 16)]
    mix = np.stack(mix).astype(np.float32).reshape(4, TB, P, T).transpose(2, 1, 0, 3)
    return np.ascontiguousarray(const), np.ascontiguousarray(mix)


def kernel(**inputs):
    import concourse.bacc as _bacc
    from concourse.bass_utils import run_bass_kernel_spmd as _run

    nc = _bacc.Bacc("TRN2", target_bir_lowering=False, num_devices=1)
    arrays, args = {}, []
    const, mix = tables()
    for name, a in [(n, inputs[n]) for n in _INS] + [("const", const), ("pool_mix", mix)]:
        a = np.ascontiguousarray(a)
        arrays[f"in_{name}"] = a
        args.append(nc.dram_tensor(f"in_{name}", a.shape, mybir.dt.from_np(a.dtype), kind="ExternalInput").ap())
    out = nc.dram_tensor("out_0", (1, T, D), F32, kind="ExternalOutput").ap()
    build(nc, *args, out)
    r = _run(nc, [arrays], core_ids=[0])
    return r.results[0]["out_0"]
```
